# Optimizing a Trainium2 kernel written in Bass

```python
import math
import jax, jax.numpy as jnp
from jax import lax
import numpy as np

D_MODEL = 2048
BATCH = 1
SEQ = 256
DEPTH = 1

MEM_LEN = 256
NORM_EPS = 1e-6

DA_HEADS = 8
DA_QK_DIM = 64
DA_V_DIM = 2 * DA_QK_DIM
DA_WIDTH = DA_HEADS * DA_V_DIM
Q_BLOCK = 128

HG_HEADS = 8
HG_DK = 128
HG_DV = 128
HG_WIDTH = HG_HEADS * HG_DV
HG_CHUNK = 64

MIX_WIDTH = DA_WIDTH + HG_WIDTH

DA_Q_COLS = DA_HEADS * 2 * DA_QK_DIM
DA_K_COLS = DA_HEADS * 2 * DA_QK_DIM
DA_V_COLS = DA_WIDTH
HG_KEY_COLS = HG_HEADS * HG_DK
HG_VAL_COLS = HG_HEADS * HG_DV
IN_SIZES = (DA_Q_COLS, DA_K_COLS, DA_V_COLS, HG_KEY_COLS, HG_KEY_COLS, HG_VAL_COLS, HG_VAL_COLS)
IN_COLS = sum(IN_SIZES)
IN_SPLITS = tuple(int(v) for v in np.cumsum(IN_SIZES)[:-1])

REL_BUCKETS = 32
REL_MAX_DIST = 128

CX_HEADS = 4
CX_HEAD_DIM = 128
CX_WIDTH = CX_HEADS * CX_HEAD_DIM

FFN_HIDDEN = ((8 * D_MODEL // 3 + 255) // 256) * 256


def rms_norm(x, g):
    xf = x.astype(jnp.float32)
    y = xf * lax.rsqrt(jnp.mean(xf * xf, axis=-1, keepdims=True) + NORM_EPS)
    return (y * g.astype(jnp.float32)).astype(x.dtype)

def t5_causal_bucket(dist):
    n = jnp.maximum(dist, 0)
    max_exact = REL_BUCKETS // 2
    nf = jnp.maximum(n, 1).astype(jnp.float32)
    large = max_exact + (jnp.log(nf / max_exact) / math.log(REL_MAX_DIST / max_exact)
                         * (REL_BUCKETS - max_exact)).astype(jnp.int32)
    large = jnp.minimum(large, REL_BUCKETS - 1)
    return jnp.where(n < max_exact, n, large)

def differential_attention(q, k, v, lam, lam_init, subln_g, rel_bias):
    B, S = q.shape[0], q.shape[1]
    n_blk = S // Q_BLOCK
    scale = DA_QK_DIM ** -0.5
    kt = jnp.transpose(k, (0, 2, 3, 1, 4))
    vt = jnp.transpose(v, (0, 2, 1, 3))
    qb = q.reshape(B, n_blk, Q_BLOCK, DA_HEADS, 2, DA_QK_DIM).transpose(1, 0, 3, 4, 2, 5)
    k_pos = jnp.arange(S)

    def block(args):
        q_blk, blk = args
        q_pos = blk * Q_BLOCK + jnp.arange(Q_BLOCK)
        dist = q_pos[:, None] - k_pos[None, :]
        bias = jnp.transpose(rel_bias[t5_causal_bucket(dist)], (2, 0, 1)).astype(jnp.float32)
        s = jnp.einsum('bhmqd,bhmkd->bhmqk', q_blk, kt).astype(jnp.float32) * scale + bias[None, :, None]
        s = jnp.where(dist >= 0, s, -jnp.inf)
        p = jax.nn.softmax(s, axis=-1)
        a = p[:, :, 0] - lam * p[:, :, 1]
        return jnp.einsum('bhqk,bhkd->bhqd', a.astype(vt.dtype), vt)

    o = lax.map(block, (qb, jnp.arange(n_blk)))
    o = rms_norm(o, subln_g) * (1.0 - lam_init)
    return o.transpose(1, 0, 3, 2, 4).reshape(B, S, DA_WIDTH)

def hgrn2(f_logit, q, i, g, lb, onorm_g):
    B, S = q.shape[0], q.shape[1]
    n_chunk = S // HG_CHUNK
    f = lb.astype(jnp.float32) + (1.0 - lb.astype(jnp.float32)) * jax.nn.sigmoid(f_logit.astype(jnp.float32))
    log_f = jnp.log(f)
    k = 1.0 - f

    def to_chunks(t, d):
        return t.astype(jnp.float32).reshape(B, n_chunk, HG_CHUNK, HG_HEADS, d).transpose(1, 0, 3, 2, 4)

    qc, kc, vc, gc = to_chunks(q, HG_DK), to_chunks(k, HG_DK), to_chunks(i, HG_DV), to_chunks(log_f, HG_DK)
    causal = jnp.tril(jnp.ones((HG_CHUNK, HG_CHUNK), dtype=bool))

    def step(state, inp):
        qt, kt, vt, gt = inp
        b = jnp.cumsum(gt, axis=2)
        diff = b[:, :, :, None, :] - b[:, :, None, :, :]
        decay = jnp.exp(jnp.where(causal[:, :, None], diff, -jnp.inf))
        attn = jnp.einsum('bhtc,bhsc,bhtsc->bhts', qt, kt, decay)
        o = (jnp.einsum('bhts,bhsv->bhtv', attn, vt)
             + jnp.einsum('bhtc,bhcv->bhtv', qt * jnp.exp(b), state))
        b_last = b[:, :, -1:, :]
        state = (jnp.exp(b_last[:, :, 0, :])[..., None] * state
                 + jnp.einsum('bhsc,bhsv->bhcv', kt * jnp.exp(b_last - b), vt))
        return state, o

    state0 = jnp.zeros((B, HG_HEADS, HG_DK, HG_DV), jnp.float32)
    _, outs = lax.scan(step, state0, (qc, kc, vc, gc))
    o = outs.transpose(1, 0, 3, 2, 4).reshape(B, S, HG_HEADS, HG_DV).astype(q.dtype)
    o = rms_norm(o, onorm_g) * jax.nn.silu(g.reshape(B, S, HG_HEADS, HG_DV))
    return o.reshape(B, S, HG_WIDTH)

def first_inputs(seed: int = 0) -> dict:
    key = jax.random.key(seed)
    ks = jax.random.split(key, 24)

    def w(k, shape, fan_in):
        return jax.random.normal(k, shape, jnp.float32) * fan_in ** -0.5

    def gain(k, shape):
        return 1.0 + 0.02 * jax.random.normal(k, shape, jnp.float32)

    return {
        "x": jax.random.normal(ks[0], (BATCH, SEQ, D_MODEL), jnp.float32),
        "mem": jax.random.normal(ks[1], (BATCH, MEM_LEN, D_MODEL), jnp.float32),
        "w_in": w(ks[2], (DEPTH, D_MODEL, IN_COLS), D_MODEL),
        "w_out": w(ks[3], (DEPTH, MIX_WIDTH, D_MODEL), MIX_WIDTH),
        "w_cq": w(ks[4], (DEPTH, D_MODEL, CX_WIDTH), D_MODEL),
        "w_ckv": w(ks[5], (DEPTH, D_MODEL, 2 * CX_WIDTH), D_MODEL),
        "w_co": w(ks[6], (DEPTH, CX_WIDTH, D_MODEL), CX_WIDTH),
        "w_ffn_in": w(ks[7], (DEPTH, D_MODEL, 2 * FFN_HIDDEN), D_MODEL),
        "w_ffn_out": w(ks[8], (DEPTH, FFN_HIDDEN, D_MODEL), FFN_HIDDEN),
        "mix_pre_g": gain(ks[9], (DEPTH, D_MODEL)),
        "mix_post_g": gain(ks[10], (DEPTH, D_MODEL)),
        "cross_pre_g": gain(ks[11], (DEPTH, D_MODEL)),
        "cross_post_g": gain(ks[12], (DEPTH, D_MODEL)),
        "mem_norm_g": gain(ks[13], (DEPTH, D_MODEL)),
        "ffn_pre_g": gain(ks[14], (DEPTH, D_MODEL)),
        "ffn_post_g": gain(ks[15], (DEPTH, D_MODEL)),
        "da_subln_g": gain(ks[16], (DEPTH, DA_V_DIM)),
        "hg_onorm_g": gain(ks[17], (DEPTH, HG_DV)),
        "lambda_q1": 0.1 * jax.random.normal(ks[18], (DEPTH, DA_QK_DIM), jnp.float32),
        "lambda_k1": 0.1 * jax.random.normal(ks[19], (DEPTH, DA_QK_DIM), jnp.float32),
        "lambda_q2": 0.1 * jax.random.normal(ks[20], (DEPTH, DA_QK_DIM), jnp.float32),
        "lambda_k2": 0.1 * jax.random.normal(ks[21], (DEPTH, DA_QK_DIM), jnp.float32),
        "hg_lb_logits": 0.5 * jax.random.normal(ks[22], (DEPTH, HG_KEY_COLS), jnp.float32),
        "rel_bias": 0.1 * jax.random.normal(ks[23], (REL_BUCKETS, DA_HEADS), jnp.float32),
    }

def first_block(x, mem, w_in, w_out, w_cq, w_ckv, w_co, w_ffn_in, w_ffn_out,
              mix_pre_g, mix_post_g, cross_pre_g, cross_post_g, mem_norm_g,
              ffn_pre_g, ffn_post_g, da_subln_g, hg_onorm_g,
              lambda_q1, lambda_k1, lambda_q2, lambda_k2, hg_lb_logits, rel_bias):
    B, S = x.shape[0], x.shape[1]
    M = mem.shape[1]
    lb_p = jax.nn.softmax(hg_lb_logits.astype(jnp.float32), axis=0)
    lower_bounds = jnp.cumsum(lb_p, axis=0) - lb_p[0:1]

    for l in range(DEPTH):
        h = rms_norm(x, mix_pre_g[l])
        proj = h @ w_in[l]
        q_da, k_da, v_da, f_hg, q_hg, i_hg, g_hg = jnp.split(proj, IN_SPLITS, axis=-1)

        lam_init = 0.8 - 0.6 * math.exp(-0.3 * l)
        lam = (jnp.exp(jnp.sum(lambda_q1[l].astype(jnp.float32) * lambda_k1[l].astype(jnp.float32)))
               - jnp.exp(jnp.sum(lambda_q2[l].astype(jnp.float32) * lambda_k2[l].astype(jnp.float32)))
               + lam_init)
        o_da = differential_attention(
            q_da.reshape(B, S, DA_HEADS, 2, DA_QK_DIM),
            k_da.reshape(B, S, DA_HEADS, 2, DA_QK_DIM),
            v_da.reshape(B, S, DA_HEADS, DA_V_DIM),
            lam, lam_init, da_subln_g[l], rel_bias)
        o_hg = hgrn2(f_hg, q_hg, i_hg, g_hg, lower_bounds[l], hg_onorm_g[l])
        mixed = jnp.concatenate([o_da, o_hg], axis=-1) @ w_out[l]
        x = x + rms_norm(mixed, mix_post_g[l])

        h = rms_norm(x, cross_pre_g[l])
        m = rms_norm(mem, mem_norm_g[l])
        qx = (h @ w_cq[l]).reshape(B, S, CX_HEADS, CX_HEAD_DIM)
        kv = (m @ w_ckv[l]).reshape(B, M, 2, CX_HEADS, CX_HEAD_DIM)
        s = jnp.einsum('bqhd,bkhd->bhqk', qx, kv[:, :, 0]).astype(jnp.float32) * CX_HEAD_DIM ** -0.5
        p = jax.nn.softmax(s, axis=-1)
        o = jnp.einsum('bhqk,bkhd->bqhd', p.astype(x.dtype), kv[:, :, 1]).reshape(B, S, CX_WIDTH)
        x = x + rms_norm(o @ w_co[l], cross_post_g[l])

        h = rms_norm(x, ffn_pre_g[l])
        gate, up = jnp.split(h @ w_ffn_in[l], 2, axis=-1)
        x = x + rms_norm((jax.nn.silu(gate) * up) @ w_ffn_out[l], ffn_post_g[l])

    return x


N_MIXERS = 2
N_HEADS = 16
HEAD_DIM = 128
N_KV_GROUPS = 4
HEADS_PER_GROUP = N_HEADS // N_KV_GROUPS
CMP_BLOCK = 32
CMP_STRIDE = 16
CMP_HIDDEN = 2 * HEAD_DIM
SEL_BLOCK = 64
SEL_TOPK = 16
WINDOW = 512
N_GATES = 3
KV_WIDTH = N_KV_GROUPS * HEAD_DIM
NSA_IN_COLS = N_HEADS * HEAD_DIM + 6 * KV_WIDTH + N_GATES * N_HEADS
SSM_GROUP = 16
SSM_GROUPS = D_MODEL // SSM_GROUP
SSM_STATE = 64
D_FF = ((8 * D_MODEL + 2) // 3 + 255) // 256 * 256
N_NSA_LAYERS = (DEPTH + N_MIXERS - 1) // N_MIXERS
N_S5_LAYERS = DEPTH // N_MIXERS
RMS_EPS = 1e-6
NEG_INF = -1e30
FORCE_SCORE = 1e9


def rmsnorm(x, g):
    x32 = x.astype(jnp.float32)
    y = x32 * lax.rsqrt(jnp.mean(x32 * x32, axis=-1, keepdims=True) + RMS_EPS)
    return (y * g.astype(jnp.float32)).astype(x.dtype)

def rel_bucket(dist):
    n = jnp.maximum(dist, 0)
    max_exact = REL_BUCKETS // 2
    large = max_exact + (jnp.log(jnp.maximum(n, 1).astype(jnp.float32) / max_exact)
                         / math.log(REL_MAX_DIST / max_exact)
                         * (REL_BUCKETS - max_exact)).astype(jnp.int32)
    large = jnp.minimum(large, REL_BUCKETS - 1)
    return jnp.where(n < max_exact, n, large)

def masked_softmax(s, mask):
    s = jnp.where(mask, s.astype(jnp.float32), NEG_INF)
    p = jax.nn.softmax(s, axis=-1)
    return jnp.where(mask, p, 0.0)

def nsa_mixer(h, rel_bias, w_in, w_out, pos_k, w1_k, w2_k, pos_v, w1_v, w2_v):
    Bsz, S, _ = h.shape
    G, HPG, DH = N_KV_GROUPS, HEADS_PER_GROUP, HEAD_DIM
    proj = h @ w_in
    qe = N_HEADS * DH
    bounds = [qe + i * KV_WIDTH for i in range(7)]
    q, kc, vc, ks, vs, kw, vw, gl = jnp.split(proj, bounds, axis=-1)
    q = q.reshape(Bsz, S, G, HPG, DH) * (DH ** -0.5)
    kc, vc, ks, vs, kw, vw = [a.reshape(Bsz, S, G, DH) for a in (kc, vc, ks, vs, kw, vw)]
    gates = jax.nn.sigmoid(gl.astype(jnp.float32)).astype(h.dtype).reshape(Bsz, S, N_GATES, G, HPG)
    t = jnp.arange(S, dtype=jnp.int32)

    n_cmp = (S - CMP_BLOCK) // CMP_STRIDE + 1
    starts = jnp.arange(n_cmp, dtype=jnp.int32) * CMP_STRIDE
    gidx = starts[:, None] + jnp.arange(CMP_BLOCK, dtype=jnp.int32)[None, :]

    def compress(kv, pos, w1, w2):
        blk = kv[:, gidx] + pos[None, None, :, None, :]
        blk = jnp.moveaxis(blk, 3, 2).reshape(Bsz, n_cmp, G, CMP_BLOCK * DH)
        return jax.nn.gelu(blk @ w1) @ w2

    kcc = compress(kc, pos_k, w1_k, w2_k)
    vcc = compress(vc, pos_v, w1_v, w2_v)
    dist_c = t[:, None] - (starts + CMP_BLOCK - 1)[None, :]
    mask_c = dist_c >= 0
    bias_c = rel_bias[rel_bucket(dist_c)].transpose(2, 0, 1).reshape(G, HPG, S, n_cmp)
    s_c = jnp.einsum('btghd,bcgd->bghtc', q, kcc).astype(jnp.float32) + bias_c
    p_c = masked_softmax(s_c, mask_c)
    o_c = jnp.einsum('bghtc,bcgd->btghd', p_c.astype(vcc.dtype), vcc)

    imp = p_c.sum(axis=2)
    n_sel = S // SEL_BLOCK
    ratio = SEL_BLOCK // CMP_STRIDE
    lo = CMP_BLOCK // CMP_STRIDE - 1
    count = ratio + lo
    right = max(0, (count - 1) + ratio * n_sel - lo - n_cmp)
    imp_pad = jnp.pad(imp, ((0, 0), (0, 0), (0, 0), (lo, right)))
    imp_slc = sum(imp_pad[..., k:k + ratio * n_sel:ratio] for k in range(count))
    j = jnp.arange(n_sel, dtype=jnp.int32)
    t_blk = t // SEL_BLOCK
    forced = (j[None, :] == 0) | (j[None, :] == t_blk[:, None]) | (j[None, :] == t_blk[:, None] - 1)
    causal_blk = (j * SEL_BLOCK)[None, :] <= t[:, None]
    score = jnp.where(forced, FORCE_SCORE, imp_slc)
    score = jnp.where(causal_blk, score, NEG_INF)
    k_top = min(SEL_TOPK, n_sel)
    _, sel_idx = lax.top_k(score, k_top)

    ks_blocks = ks.reshape(Bsz, n_sel, SEL_BLOCK, G, DH).transpose(0, 3, 1, 2, 4)
    vs_blocks = vs.reshape(Bsz, n_sel, SEL_BLOCK, G, DH).transpose(0, 3, 1, 2, 4)
    nq = S // Q_BLOCK
    q_chunks = q.reshape(Bsz, nq, Q_BLOCK, G, HPG, DH).transpose(1, 0, 2, 3, 4, 5)
    idx_chunks = sel_idx.reshape(Bsz, G, nq, Q_BLOCK, k_top).transpose(2, 0, 1, 3, 4)
    t0s = jnp.arange(nq, dtype=jnp.int32) * Q_BLOCK
    table_g = rel_bias.T.reshape(G, HPG, REL_BUCKETS)
    bi = jnp.arange(Bsz)[:, None, None, None]
    gi = jnp.arange(G)[None, :, None, None]
    gi5 = jnp.arange(G)[None, :, None, None, None]
    hi5 = jnp.arange(HPG)[None, None, :, None, None]
    in_blk = jnp.arange(SEL_BLOCK, dtype=jnp.int32)

    def sel_chunk(args):
        qc, ic, t0 = args
        kg = ks_blocks[bi, gi, ic].reshape(Bsz, G, Q_BLOCK, k_top * SEL_BLOCK, DH)
        vg = vs_blocks[bi, gi, ic].reshape(Bsz, G, Q_BLOCK, k_top * SEL_BLOCK, DH)
        kpos = (ic[..., None] * SEL_BLOCK + in_blk).reshape(Bsz, G, Q_BLOCK, k_top * SEL_BLOCK)
        tq = t0 + jnp.arange(Q_BLOCK, dtype=jnp.int32)
        dist = tq[None, None, :, None] - kpos
        bias = table_g[gi5, hi5, rel_bucket(dist)[:, :, None]]
        s = jnp.einsum('bqghd,bgqkd->bghqk', qc, kg).astype(jnp.float32) + bias
        p = masked_softmax(s, (dist >= 0)[:, :, None])
        return jnp.einsum('bghqk,bgqkd->bqghd', p.astype(vg.dtype), vg)

    o_s = lax.map(sel_chunk, (q_chunks, idx_chunks, t0s))
    o_s = o_s.transpose(1, 0, 2, 3, 4, 5).reshape(Bsz, S, G, HPG, DH)

    nb = S // Q_BLOCK
    n_band = WINDOW // Q_BLOCK

    def band(kv):
        padded = jnp.pad(kv, ((0, 0), (WINDOW, 0), (0, 0), (0, 0))).reshape(Bsz, nb + n_band, Q_BLOCK, G, DH)
        return jnp.concatenate([padded[:, i:i + nb] for i in range(n_band + 1)], axis=2)

    kwb, vwb = band(kw), band(vw)
    qi = jnp.arange(Q_BLOCK, dtype=jnp.int32)
    ki = jnp.arange((n_band + 1) * Q_BLOCK, dtype=jnp.int32)
    dist_w = qi[:, None] + WINDOW - ki[None, :]
    key_abs = jnp.arange(nb, dtype=jnp.int32)[:, None] * Q_BLOCK - WINDOW + ki[None, :]
    mask_w = ((dist_w >= 0) & (dist_w < WINDOW))[None] & (key_abs >= 0)[:, None, :]
    bias_w = rel_bias[rel_bucket(dist_w)].transpose(2, 0, 1).reshape(G, HPG, Q_BLOCK, -1)
    qw = q.reshape(Bsz, nb, Q_BLOCK, G, HPG, DH)
    s_w = jnp.einsum('bjqghd,bjkgd->bjghqk', qw, kwb).astype(jnp.float32) + bias_w
    p_w = masked_softmax(s_w, mask_w[:, None, None])
    o_w = jnp.einsum('bjghqk,bjkgd->bjqghd', p_w.astype(vwb.dtype), vwb).reshape(Bsz, S, G, HPG, DH)

    o = (gates[:, :, 0, :, :, None] * o_c + gates[:, :, 1, :, :, None] * o_s
         + gates[:, :, 2, :, :, None] * o_w)
    return o.reshape(Bsz, S, N_HEADS * DH) @ w_out

def s5_mixer(h, A_re, A_im, log_dt, B_re, B_im, C_re, C_im, D_skip, w_glu):
    Bsz, S, D = h.shape
    f32 = jnp.float32
    A_re, A_im, log_dt = A_re.astype(f32), A_im.astype(f32), log_dt.astype(f32)
    B_re, B_im, C_re, C_im = B_re.astype(f32), B_im.astype(f32), C_re.astype(f32), C_im.astype(f32)
    u = h.astype(f32).reshape(Bsz, S, SSM_GROUPS, SSM_GROUP)
    dt = jnp.exp(log_dt)[:, None]
    decay = jnp.exp(A_re * dt)
    ab_re = decay * jnp.cos(A_im * dt)
    ab_im = decay * jnp.sin(A_im * dt)
    pr, pi_ = ab_re - 1.0, ab_im
    den = A_re * A_re + A_im * A_im
    cf_re = (pr * A_re + pi_ * A_im) / den
    cf_im = (pi_ * A_re - pr * A_im) / den
    bb_re = cf_re[..., None] * B_re - cf_im[..., None] * B_im
    bb_im = cf_re[..., None] * B_im + cf_im[..., None] * B_re
    bu_re = jnp.einsum('bsgc,gnc->bsgn', u, bb_re)
    bu_im = jnp.einsum('bsgc,gnc->bsgn', u, bb_im)
    a_re = jnp.broadcast_to(ab_re, bu_re.shape)
    a_im = jnp.broadcast_to(ab_im, bu_im.shape)

    def combine(e1, e2):
        a1r, a1i, b1r, b1i = e1
        a2r, a2i, b2r, b2i = e2
        return (a1r * a2r - a1i * a2i, a1r * a2i + a1i * a2r,
                a2r * b1r - a2i * b1i + b2r, a2r * b1i + a2i * b1r + b2i)

    _, _, x_re, x_im = lax.associative_scan(combine, (a_re, a_im, bu_re, bu_im), axis=1)
    y = (jnp.einsum('bsgn,gcn->bsgc', x_re, C_re) - jnp.einsum('bsgn,gcn->bsgc', x_im, C_im)
         + D_skip.astype(f32).reshape(SSM_GROUPS, SSM_GROUP) * u)
    y = jax.nn.gelu(y).reshape(Bsz, S, D).astype(h.dtype)
    z = y @ w_glu
    return z[..., :D] * jax.nn.sigmoid(z[..., D:])

def swiglu(h, w_in, w_out):
    z = h @ w_in
    a, b = z[..., :D_FF], z[..., D_FF:]
    return (jax.nn.silu(a) * b) @ w_out

def second_inputs(seed: int = 0) -> dict:
    key = jax.random.key(seed)
    ks = jax.random.split(key, 32)

    def nrm(k, shape, scale):
        return jax.random.normal(k, shape, jnp.float32) * scale

    D, H, DH, G, N, C = D_MODEL, N_HEADS, HEAD_DIM, SSM_GROUPS, SSM_STATE, SSM_GROUP
    n_idx = jnp.arange(N, dtype=jnp.float32)
    return {
        "x": nrm(ks[0], (BATCH, SEQ, D), 1.0),
        "rel_bias": nrm(ks[1], (REL_BUCKETS, H), 0.2),
        "mix_norm_g": 1.0 + nrm(ks[2], (DEPTH, D), 0.02),
        "ffn_norm_g": 1.0 + nrm(ks[3], (DEPTH, D), 0.02),
        "final_norm_g": 1.0 + nrm(ks[4], (D,), 0.02),
        "nsa_w_in": nrm(ks[5], (N_NSA_LAYERS, D, NSA_IN_COLS), D ** -0.5),
        "nsa_w_out": nrm(ks[6], (N_NSA_LAYERS, H * DH, D), (H * DH) ** -0.5),
        "cmp_pos_k": nrm(ks[7], (N_NSA_LAYERS, CMP_BLOCK, DH), 0.1),
        "cmp_w1_k": nrm(ks[8], (N_NSA_LAYERS, CMP_BLOCK * DH, CMP_HIDDEN), (CMP_BLOCK * DH) ** -0.5),
        "cmp_w2_k": nrm(ks[9], (N_NSA_LAYERS, CMP_HIDDEN, DH), CMP_HIDDEN ** -0.5),
        "cmp_pos_v": nrm(ks[10], (N_NSA_LAYERS, CMP_BLOCK, DH), 0.1),
        "cmp_w1_v": nrm(ks[11], (N_NSA_LAYERS, CMP_BLOCK * DH, CMP_HIDDEN), (CMP_BLOCK * DH) ** -0.5),
        "cmp_w2_v": nrm(ks[12], (N_NSA_LAYERS, CMP_HIDDEN, DH), CMP_HIDDEN ** -0.5),
        "s5_A_re": -0.5 + nrm(ks[13], (N_S5_LAYERS, G, N), 0.01),
        "s5_A_im": math.pi * n_idx + nrm(ks[14], (N_S5_LAYERS, G, N), 0.01),
        "s5_log_dt": jax.random.uniform(ks[15], (N_S5_LAYERS, G), jnp.float32,
                                        math.log(1e-3), math.log(1e-1)),
        "s5_B_re": nrm(ks[16], (N_S5_LAYERS, G, N, C), (2 * C) ** -0.5),
        "s5_B_im": nrm(ks[17], (N_S5_LAYERS, G, N, C), (2 * C) ** -0.5),
        "s5_C_re": nrm(ks[18], (N_S5_LAYERS, G, C, N), (2 * N) ** -0.5),
        "s5_C_im": nrm(ks[19], (N_S5_LAYERS, G, C, N), (2 * N) ** -0.5),
        "s5_D": nrm(ks[20], (N_S5_LAYERS, D), 1.0),
        "s5_w_glu": nrm(ks[21], (N_S5_LAYERS, D, 2 * D), D ** -0.5),
        "ffn_w_in": nrm(ks[22], (DEPTH, D, 2 * D_FF), D ** -0.5),
        "ffn_w_out": nrm(ks[23], (DEPTH, D_FF, D), D_FF ** -0.5),
    }

def second_block(x, rel_bias, mix_norm_g, ffn_norm_g, final_norm_g, nsa_w_in, nsa_w_out,
              cmp_pos_k, cmp_w1_k, cmp_w2_k, cmp_pos_v, cmp_w1_v, cmp_w2_v,
              s5_A_re, s5_A_im, s5_log_dt, s5_B_re, s5_B_im, s5_C_re, s5_C_im, s5_D, s5_w_glu,
              ffn_w_in, ffn_w_out):
    h = x
    for i in range(DEPTH):
        hn = rmsnorm(h, mix_norm_g[i])
        li = i // N_MIXERS
        if i % N_MIXERS == 0:
            h = h + nsa_mixer(hn, rel_bias, nsa_w_in[li], nsa_w_out[li],
                              cmp_pos_k[li], cmp_w1_k[li], cmp_w2_k[li],
                              cmp_pos_v[li], cmp_w1_v[li], cmp_w2_v[li])
        else:
            h = h + s5_mixer(hn, s5_A_re[li], s5_A_im[li], s5_log_dt[li], s5_B_re[li], s5_B_im[li],
                             s5_C_re[li], s5_C_im[li], s5_D[li], s5_w_glu[li])
        h = h + swiglu(rmsnorm(h, ffn_norm_g[i]), ffn_w_in[i], ffn_w_out[i])
    return rmsnorm(h, final_norm_g)


def setup_inputs(seed=0):
    out = dict(first_inputs(seed))
    for name, value in second_inputs(seed + 1).items():
        if name != "x":
            out[name + "_2"] = value
    return out


def reference(
    x, mem, w_in, w_out, w_cq, w_ckv, w_co, w_ffn_in, w_ffn_out, mix_pre_g, mix_post_g,
    cross_pre_g, cross_post_g, mem_norm_g, ffn_pre_g, ffn_post_g, da_subln_g, hg_onorm_g,
    lambda_q1, lambda_k1, lambda_q2, lambda_k2, hg_lb_logits, rel_bias, rel_bias_2,
    mix_norm_g_2, ffn_norm_g_2, final_norm_g_2, nsa_w_in_2, nsa_w_out_2, cmp_pos_k_2,
    cmp_w1_k_2, cmp_w2_k_2, cmp_pos_v_2, cmp_w1_v_2, cmp_w2_v_2, s5_A_re_2, s5_A_im_2,
    s5_log_dt_2, s5_B_re_2, s5_B_im_2, s5_C_re_2, s5_C_im_2, s5_D_2, s5_w_glu_2, ffn_w_in_2,
    ffn_w_out_2,
):
    x = first_block(
        x, mem, w_in, w_out, w_cq, w_ckv, w_co, w_ffn_in, w_ffn_out, mix_pre_g, mix_post_g,
        cross_pre_g, cross_post_g, mem_norm_g, ffn_pre_g, ffn_post_g, da_subln_g, hg_onorm_g,
        lambda_q1, lambda_k1, lambda_q2, lambda_k2, hg_lb_logits, rel_bias,
    )
    return second_block(
        x, rel_bias_2, mix_norm_g_2, ffn_norm_g_2, final_norm_g_2, nsa_w_in_2, nsa_w_out_2,
        cmp_pos_k_2, cmp_w1_k_2, cmp_w2_k_2, cmp_pos_v_2, cmp_w1_v_2, cmp_w2_v_2, s5_A_re_2,
        s5_A_im_2, s5_log_dt_2, s5_B_re_2, s5_B_im_2, s5_C_re_2, s5_C_im_2, s5_D_2, s5_w_glu_2,
        ffn_w_in_2, ffn_w_out_2,
    )


_drawn_inputs = setup_inputs


def setup_inputs(seed=0):
    import zlib

    import numpy as np

    out = dict(_drawn_inputs(seed))
    spreads = {}
    factors = {'mix_post_g': 3.448,
     'cross_pre_g': 4.381,
     'cross_post_g': 4.263,
     'mem_norm_g': 2.83,
     'ffn_pre_g': 3.685,
     'ffn_post_g': 5.279,
     'da_subln_g': 4.14,
     'hg_onorm_g': 5.927,
     'rel_bias_2': 3.511,
     'mix_norm_g_2': 8.0,
     'ffn_norm_g_2': 6.915,
     'final_norm_g_2': 7.747,
     'cmp_pos_k_2': 8.0,
     'cmp_pos_v_2': 10.162}
    for name, (base, spread) in spreads.items():
        noise = np.random.default_rng([zlib.crc32(name.encode()), seed]).standard_normal(out[name].shape)
        drawn = base * np.exp(spread * noise) if base else spread * noise
        out[name] = __import__('jax').numpy.asarray(drawn.astype(out[name].dtype))
    for name, factor in factors.items():
        out[name] = (out[name] * factor).astype(out[name].dtype)
    return out
```

```python
from contextlib import ExitStack

import concourse.bass as bass
from concourse import mybir

F32 = mybir.dt.float32
F32R = mybir.dt.float32r
ALU = mybir.AluOpType
ACT = mybir.ActivationFunctionType
X = mybir.AxisListType.X

P = 128
D = 2048
T = 2
S = T * P
NB = 512
SLOTS = 4
UE = 1024
EPS = 1e-6

DA_H, DA_D = 8, 64
HG_H, HG_D = 8, 128
Q_DA, K_DA, V_DA, F_HG, Q_HG, I_HG, G_HG = (1024 * n for n in range(7))
IN1 = 7168
LAM_INIT = 0.2
CHUNK = 64
LEVELS = 8
CX_H = 4
CX_W = 512
FH = 5632
PAIRS = FH // NB
FKT = FH // P
N_H, N_G, HPG = 16, 4, 4
KC, VC, KS, VS, KW, VW, GL = 2048, 2560, 3072, 3584, 4096, 4608, 5120
IN2 = 5168
NC_, CSTR, CLEN, CHID = 15, 16, 32, 256
GB = N_G * NC_
MASKED = -1e30


def rel_rows():
    import math
    import numpy as np

    def bucket(n):
        if n < 16:
            return n
        return min(31, 16 + int(math.log(n / 16) / math.log(8.0) * 16))

    falling = np.zeros((33, 512), np.float32)
    rising = np.zeros((33, 512), np.float32)
    for m in range(512):
        d = 255 - m
        falling[bucket(d) if d >= 0 else 32, m] = 1
        d = m - 256
        rising[bucket(d) if d >= 0 else 32, m] = 1
    return falling, rising


def level_masks():
    import numpy as np
    s, t = np.arange(128)[:, None], np.arange(128)[None, :]
    m = np.zeros((128, 8, 128), np.float32)
    for l in range(7):
        w = 2 << l
        m[:, l, :] = (s // w == t // w) & (s % w < w // 2) & (t % w >= w // 2)
    m[:, 7, :] = s == t
    return m.reshape(128, 1024)


def cumsum_lhs():
    import numpy as np
    s, t = np.arange(128)[:, None], np.arange(128)[None, :]
    return ((s // CHUNK == t // CHUNK) & (s <= t)).astype(np.float32)


def build(nc, a, out):
    ctx = ExitStack()
    with ctx:
        base = (nc.sbuf_base + 31) // 32 * 32
        place = {}

        def at(name, shape, offset, dt=F32):
            return nc.alloc_sbuf_tensor_at(name, shape, dt, offset=base + offset)

        o_raw, o_wh, o_wl = 0, 16384, 32768
        o_ah, o_al = 49152, 65536
        o_x, o_ga, o_gb, o_r = 81920, 98304, 106496, 114688
        o_small = o_r + 2 * FKT * S * 4
        raw = at("raw", [P, SLOTS, UE], o_raw)
        wh = at("wh", [P, SLOTS, UE], o_wh, F32R)
        wl = at("wl", [P, SLOTS, UE], o_wl, F32R)
        act_hi = at("act_hi", [P, 16, S], o_ah, F32R)
        act_lo = at("act_lo", [P, 16, S], o_al, F32R)
        y_a = at("y_a", [P, T, D], o_ah)
        x = at("x", [P, T, D], o_x)
        g_a = at("g_a", [P, D], o_ga)
        g_b = at("g_b", [P, D], o_gb)
        b_da = at("b_da", [P, DA_H, S], o_ga)
        ff_s = at("ff_s", [P, T, NB], o_ga)
        ff_h = at("ff_h", [P, T, NB], o_ga + 4096)
        ht_hi = at("ht_hi", [P, FKT, S], o_r, F32R)
        ht_lo = at("ht_lo", [P, FKT, S], o_r + FKT * S * 4, F32R)
        y_r = at("y_r", [P, T, D], o_r)
        xn = at("xn", [P, T, D], o_r + 16384)
        memx = at("memx", [P, T, D], o_r + 32768)
        p1 = at("p1", [P, T, IN1], o_r)
        o = o_r + 57344
        kk = at("kk", [P, T, 1024], o); o += 8192
        masks = at("masks", [P, 1024], o); o += 4096
        dec = at("dec", [P, LEVELS, S], o)
        sc_da = at("sc_da", [P, 768], o); o += 8192
        mp = at("mp", [P, 1024], o); o += 4096
        lf_s = at("lf_s", [P, T, P], o); o += 1024
        q_s = at("q_s", [P, T, P], o); o += 1024
        k_s = at("k_s", [P, T, P], o); o += 1024
        bq = at("bq", [P, 512], o); o += 2048
        kt = at("kt", [P, S], o); o += 1024
        at3 = at("at3", [P, 3, P], o); o += 1536
        assert o <= o_small
        o = o_r + 49152
        kv = at("kv", [P, T, 1024], o); o += 8192
        qx = at("qx", [P, T, CX_W], o); o += 4096
        xq_s = at("xq_s", [P, T, P], o); o += 1024
        xk_s = at("xk_s", [P, T, P], o); o += 1024
        xqk = at("xqk", [P, 512], o); o += 2048
        xp = at("xp", [P, T, S], o); o += 2048
        xpt = at("xpt", [P, 4, P], o); o += 2048
        p2 = at("p2", [P, T, IN2], o_r)
        o = o_r + IN2 * T * 4
        kcc = at("kcc", [P, GB], o); o += 256
        vcc = at("vcc", [NC_, N_G * P], o); o += 2048
        gate = at("gate", [P, T, 48], o); o += 384
        b_n = at("b_n", [P, N_H, S], o)
        c0 = o
        ct = at("ct", [P, N_G, S], o); o += 4096
        post = at("post", [P, CLEN], o); o += 128
        pos_s = at("pos_s", [CLEN, 2, P], o); o += 1024
        blk = at("blk", [P, CLEN, GB], o); o += 7680
        blk_hi = at("blk_hi", [P, CLEN, GB], o, F32R); o += 7680
        blk_lo = at("blk_lo", [P, CLEN, GB], o, F32R); o += 7680
        gh = at("gh", [GB, 3, CHID], o); o += 3072
        ght = at("ght", [P, 2, GB], o); o += 512
        w2 = at("w2", [P, 2, 2, P], o); o += 2048
        assert o <= o_small
        o = c0 + 16384
        sn = at("sn", [P, 800], o); o += 3200
        pt = at("pt", [P, 1024], o); o += 4096
        ksw = at("ksw", [P, 512], o); o += 2048
        qn = at("qn", [P, S], o); o += 1024
        ns_q = at("ns_q", [P, T, P], o); o += 1024
        ns_ks = at("ns_ks", [P, T, P], o); o += 1024
        ns_kw = at("ns_kw", [P, T, P], o); o += 1024
        assert o <= o_small
        oh_f = at("oh_f", [33, 512], o_r + 32768)
        oh_r = at("oh_r", [33, 512], o_r + 34816)
        bt = at("bt", [24, 512], o_r + 36864)
        o = o_small
        ident = at("ident", [P, P], o); o += 512
        cums = at("cums", [P, P], o); o += 512
        bc = at("bc", [P, T, NC_, N_H], o); o += 1920
        tab = at("tab", [33, 24], o); o += 96
        sub_g = at("sub_g", [P, P], o); o += 512
        on_g = at("on_g", [P, P], o); o += 512
        lam4 = at("lam4", [P, 4, DA_D], o); o += 1024
        st = at("st", [P, 128], o); o += 512
        assert base + o <= nc.sbuf_usable_end

        ss = st[:, 0:2]
        rstd = st[:, 2:4]
        lam_d = st[:, 4:6]
        neg_lam = st[:, 6:7]
        nmx = st[:, 8:14]
        sm = st[:, 16:22]
        rc = st[:, 24:30]
        ss16 = st[:, 32:64]

        g = ctx.enter_context(nc.psum_tensor("g", [P, 4, NB], F32))
        m = ctx.enter_context(nc.psum_tensor("m", [P, 4, NB], F32))

        dram_bias = nc.dram_tensor("bias_rows", (24, P, S), F32, kind="Internal").ap()

        def sem(name):
            return ctx.enter_context(nc.semaphore(name))

        raw_full = [sem(f"raw_full{n}") for n in range(SLOTS)]
        hi_done, lo_done, unit_used = sem("hi_done"), sem("lo_done"), sem("unit_used")
        pair_free = [sem("pair_free0"), sem("pair_free1")]
        consts_in, masks_in, mem_in, x_in = sem("consts_in"), sem("masks_in"), sem("mem_in"), sem("x_in")
        ga_in, gb_in, bias_in = sem("ga_in"), sem("gb_in"), sem("bias_in")
        chain_a, chain_d, chain_p = sem("act_step"), sem("dve_step"), sem("pool_step")
        tab_ready, bt_ready, bt_sb, bc_sb, bt_stored = (
            sem("tab_ready"), sem("bt_ready"), sem("bt_sb"), sem("bc_sb"), sem("bt_stored"))
        ss_done, var_done, sqrt_done, xn_done = sem("ss_done"), sem("var_done"), sem("sqrt_done"), sem("xn_done")
        turned, hi_evac, lo_evac = sem("turned"), sem("hi_evac"), sem("lo_evac")
        x_done = sem("x_done")
        out_done = sem("out_done")

        def spec(w, units, chunks):
            return {"w": w.rearrange("(k p) n -> p k n", p=P), "units": units, "chunks": chunks}

        gemms = {
            "in1": spec(a["w_in"], 8, 14), "out1": spec(a["w_out"], 8, 4),
            "ckv": spec(a["w_ckv"], 8, 2), "cq": spec(a["w_cq"], 8, 1), "co": spec(a["w_co"], 2, 4),
            "ff1": spec(a["w_ffn_in"], 8, 22), "fo1": spec(a["w_ffn_out"], 22, 4),
            "in2": spec(a["nsa_w_in_2"], 8, 10), "cmp": {"units": 20, "chunks": 0},
            "out2": spec(a["nsa_w_out_2"], 8, 4),
            "ff2": spec(a["ffn_w_in_2"], 8, 22), "fo2": spec(a["ffn_w_out_2"], 22, 4),
        }
        at_unit, at_pair = 0, [0, 0]
        for name, s in gemms.items():
            s["u0"], s["pair0"] = at_unit, list(at_pair)
            if name == "cmp":
                at_unit += 20
                at_pair = [at_pair[0] + 1, at_pair[1]]
            else:
                at_unit += s["units"] * s["chunks"]
                at_pair = [at_pair[0] + (s["chunks"] + 1) // 2, at_pair[1] + s["chunks"] // 2]
            assert at_unit % SLOTS == 0

        def bodies(eng, s, body, step=2):
            n = s["chunks"]
            body(0, min(2, n), True)
            if n > 4:
                with eng.Fori(1, n // 2) as i:
                    body(i, 2, False)
            elif n == 4:
                body(1, 2, False)

        def sp_unit(sp, cyc, j, src, n=UE, shape=2):
            sp.wait_ge(lo_done, (cyc + j // SLOTS) * SLOTS + j % SLOTS + 1)
            sp.dma_start(raw[:, j % SLOTS, 0:n].rearrange("p (k n) -> p k n", k=shape), src)\
              .then_inc(raw_full[j % SLOTS], 16)

        def act_unit(act, cyc, j, n=UE):
            act.wait_ge(raw_full[j % SLOTS], (cyc + j // SLOTS) * 16 + 16)
            act.wait_ge(unit_used, (cyc + j // SLOTS) * SLOTS + j % SLOTS + 1)
            nc.scalar.activation(wh[:, j % SLOTS, 0:n], raw[:, j % SLOTS, 0:n], ACT.Copy).then_inc(hi_done, 1)

        def dve_unit(dve, cyc, j, n=UE):
            dve.wait_ge(hi_done, (cyc + j // SLOTS) * SLOTS + j % SLOTS + 1)
            nc.vector.tensor_tensor(wl[:, j % SLOTS, 0:n], raw[:, j % SLOTS, 0:n],
                                    wh[:, j % SLOTS, 0:n].bitcast(F32), ALU.subtract).then_inc(lo_done, 1)

        def pe_unit(pe, cyc, j, pair, hi, lo, k0, first, last):
            pe.wait_ge(lo_done, SLOTS + (cyc + j // SLOTS) * SLOTS + j % SLOTS + 1)
            for k in range(2):
                whk = wh[:, j % SLOTS, k * NB:(k + 1) * NB]
                wlk = wl[:, j % SLOTS, k * NB:(k + 1) * NB]
                for t in range(T):
                    dst = g[:, 2 * pair + t, :]
                    h = hi[:, k0 + k, t * P:(t + 1) * P]
                    l = lo[:, k0 + k, t * P:(t + 1) * P]
                    nc.tensor.matmul(dst, h, whk, start=(first and k == 0), stop=False)
                    nc.tensor.matmul(dst, h, wlk, start=False, stop=False)
                    ins = nc.tensor.matmul(dst, l, whk, start=False, stop=(last and k == 1))
            ins.then_inc(unit_used, 1)

        def used(s, chunk):
            return SLOTS + s["u0"] + s["units"] * (chunk + 1)

        def cyc_of(s, i):
            return s["u0"] // SLOTS + i * (2 * s["units"] // SLOTS)

        def sp_gemm(sp, name, col=lambda c: c * NB):
            s = gemms[name]

            def body(i, chunks, first):
                for j in range(chunks * s["units"]):
                    c, u = 2 * i + j // s["units"], j % s["units"]
                    sp_unit(sp, cyc_of(s, i), j, s["w"][:, 2 * u:2 * u + 2, bass.ds(col(c), NB)])
            bodies(sp, s, body)

        def act_gemm(act, name, dst):
            s = gemms[name]
            late = min(3, s["units"] - 1)

            def evac(i, c):
                chunk = 2 * i + c
                act.wait_ge(unit_used, used(s, chunk))
                nc.scalar.activation(dst(chunk), g[:, 2 * (c % 2):2 * (c % 2) + 2, :], ACT.Copy)\
                  .then_inc(pair_free[c % 2], 1)

            def body(i, chunks, first):
                for j in range(chunks * s["units"]):
                    act_unit(act, cyc_of(s, i), j)
                    if j == late and not first:
                        evac(i, -1)
                    if j == s["units"] + late:
                        evac(i, 0)
            bodies(act, s, body)
            n = s["chunks"]
            if n > 1:
                evac(n // 2, -1)
            else:
                evac(0, 0)

        def dve_gemm(dve, name):
            s = gemms[name]

            def body(i, chunks, first):
                for j in range(chunks * s["units"]):
                    dve_unit(dve, cyc_of(s, i), j)
            bodies(dve, s, body)

        def pe_gemm(pe, name, hi=None, lo=None):
            s = gemms[name]
            hi, lo = (act_hi, act_lo) if hi is None else (hi, lo)

            def body(i, chunks, first):
                for j in range(chunks * s["units"]):
                    c, u = j // s["units"], j % s["units"]
                    if u == 0:
                        pe.wait_ge(pair_free[c], s["pair0"][c] + i + 1)
                    pe_unit(pe, cyc_of(s, i), j, c, hi, lo, 2 * u, u == 0, u == s["units"] - 1)
            bodies(pe, s, body)

        CONSTS = 16 * 12
        NORM = {n: k for k, n in enumerate(["n1", "post1", "nmem", "ncx", "postcx", "nff", "postff", "n2", "nff2", "nfin"])}
        XN = {n: k for k, n in enumerate(["n1", "nmem", "ncx", "nff", "n2", "nff2"])}
        BANKS = {}
        bank_at = 0
        for n, banks in (("n1", 8), ("mix1", 8), ("nmem", 8), ("ncx", 8), ("cx", 2), ("nff", 8), ("ff1", 2 * PAIRS),
                         ("n2", 8), ("mix2", 8), ("nff2", 8), ("ff2", 2 * PAIRS)):
            BANKS[n] = bank_at
            bank_at += banks

        def act_stats(act, name, src, junk):
            n = NORM[name]
            for t in range(T):
                nc.scalar.activation(junk[:, t, :], src[:, t, :], ACT.Square, accum_out=ss[:, t:t + 1])\
                  .then_inc(ss_done, 1)
            act.wait_ge(var_done, n + 1)
            nc.scalar.activation(rstd, ss, ACT.Sqrt).then_inc(sqrt_done, 1)

        def dve_stats(dve, name):
            n = NORM[name]
            dve.wait_ge(ss_done, 2 * n + 2)
            nc.vector.tensor_scalar(ss, ss, 1.0 / D, EPS, ALU.mult, ALU.add).then_inc(var_done, 1)
            dve.wait_ge(sqrt_done, n + 1)
            link_d(dve, nc.vector.reciprocal(rstd, rstd))

        def dve_norm(dve, name, src, gains):
            dve_stats(dve, name)
            dve.wait_ge(ga_in, 16 * gains)
            for t in range(T):
                nc.vector.scalar_tensor_tensor(out=xn[:, t, :], in0=src[:, t, :], scalar=rstd[:, t:t + 1],
                                               in1=g_a[:, :], op0=ALU.mult, op1=ALU.mult).then_inc(xn_done, 1)

        def dve_post(dve, name, y, gains):
            dve_stats(dve, name)
            dve.wait_ge(gb_in, 16 * gains)
            for t in range(T):
                link_d(dve, nc.vector.scalar_tensor_tensor(out=y[:, t, :], in0=y[:, t, :], scalar=rstd[:, t:t + 1],
                                                           in1=g_b[:, :], op0=ALU.mult, op1=ALU.mult))
            for t in range(T):
                nc.vector.tensor_tensor(x[:, t, :], x[:, t, :], y[:, t, :], ALU.add).then_inc(x_done, 1)

        def pe_turn(pe, name, src, n=8):
            b0 = BANKS[name]
            for b in range(n):
                if b0 + b >= 4:
                    pe.wait_ge(lo_evac, b0 + b - 3)
                for k in range(2):
                    for t in range(T):
                        ins = nc.tensor.transpose(m[:, (b0 + b) % 4, (2 * k + t) * P:(2 * k + t + 1) * P],
                                                  src(2 * b + k, t), ident[:, :])
                ins.then_inc(turned, 1)

        def act_turn(act, name, n=8):
            b0 = BANKS[name]
            for b in range(n):
                act.wait_ge(turned, b0 + b + 1)
                nc.scalar.activation(act_hi[:, 2 * b:2 * b + 2, :], m[:, (b0 + b) % 4, :].rearrange("p (k n) -> p k n", k=2),
                                     ACT.Copy).then_inc(hi_evac, 1)

        def dve_turn(dve, name, n=8):
            b0 = BANKS[name]
            for b in range(n):
                dve.wait_ge(hi_evac, b0 + b + 1)
                nc.vector.tensor_tensor(act_lo[:, 2 * b:2 * b + 2, :],
                                        m[:, (b0 + b) % 4, :].rearrange("p (k n) -> p k n", k=2),
                                        act_hi[:, 2 * b:2 * b + 2, :].bitcast(F32), ALU.subtract).then_inc(lo_evac, 1)

        def turned_in(pe, name, n=8):
            pe.wait_ge(lo_evac, BANKS[name] + n)

        count = {"a": 0, "d": 0}

        def link_d(dve, ins):
            count["d"] += 1
            ins.then_inc(chain_d, 1)
            dve.wait_ge(chain_d, count["d"])

        def link_a(act, ins):
            count["a"] += 1
            ins.then_inc(chain_a, 1)
            act.wait_ge(chain_a, count["a"])


        def sp_gemm_cols(sp, name):
            s = gemms[name]

            def body(i, chunks, first):
                for j in range(16):
                    u = j % 8
                    sp_unit(sp, cyc_of(s, i), j, s["w"][:, 2 * u:2 * u + 2, bass.ds(i * NB + (j // 8) * FH, NB)])
            bodies(sp, s, body)

        def pe_ff_turn(pe, name, i):
            b0 = BANKS[name]
            pe.wait_ge(pair_free[1], gemms[name]["pair0"][1] + i + 2)
            for b in range(2):
                pe.wait_ge(lo_evac, b0 + 2 * i + b - 1)
                for k in range(2):
                    for t in range(T):
                        ins = nc.tensor.transpose(m[:, b, (2 * k + t) * P:(2 * k + t + 1) * P],
                                                  ff_h[:, t, (2 * b + k) * P:(2 * b + k + 1) * P], ident[:, :])
                ins.then_inc(turned, 1)

        def act_ff_turn(act, name, i):
            b0 = BANKS[name]
            for b in range(2):
                act.wait_ge(turned, b0 + 2 * i + b + 1)
                nc.scalar.activation(ht_hi[:, bass.ds(4 * i + 2 * b, 2), :], m[:, b, :]
                                     .rearrange("p (k n) -> p k n", k=2), ACT.Copy).then_inc(hi_evac, 1)

        def dve_ff_turn(dve, name, i):
            b0 = BANKS[name]
            for b in range(2):
                dve.wait_ge(hi_evac, b0 + 2 * i + b + 1)
                nc.vector.tensor_tensor(ht_lo[:, bass.ds(4 * i + 2 * b, 2), :], m[:, b, :]
                                        .rearrange("p (k n) -> p k n", k=2),
                                        ht_hi[:, bass.ds(4 * i + 2 * b, 2), :].bitcast(F32), ALU.subtract)\
                  .then_inc(lo_evac, 1)

        def pe_ffn_in(pe, name):
            s = gemms[name]

            def body(i, chunks, first):
                for j in range(16):
                    c, u = j // 8, j % 8
                    if u == 0:
                        pe.wait_ge(pair_free[c], s["pair0"][c] + i + 1)
                    if j == 8 and not first:
                        pe_ff_turn(pe, name, i - 1)
                    pe_unit(pe, cyc_of(s, i), j, c, act_hi, act_lo, 2 * u, u == 0, u == 7)
            bodies(pe, s, body)
            pe_ff_turn(pe, name, PAIRS - 1)

        def act_ffn_in(act, name):
            s = gemms[name]

            def body(i, chunks, first):
                for j in range(16):
                    act_unit(act, cyc_of(s, i), j)
                    if j == 11:
                        if not first:
                            act_ff_turn(act, name, i - 1)
                            act.wait_ge(pair_free[1], s["pair0"][1] + i + 1)
                        act.wait_ge(unit_used, s["u0"] + SLOTS + 16 * i + 8)
                        nc.scalar.activation(ff_s[:, :, :], g[:, 0:2, :], ACT.Silu).then_inc(pair_free[0], 1)
            bodies(act, s, body)
            act_ff_turn(act, name, PAIRS - 1)

        def dve_ffn_in(dve, name):
            s = gemms[name]

            def mul(i):
                dve.wait_ge(pair_free[0], s["pair0"][0] + i + 2)
                dve.wait_ge(unit_used, s["u0"] + SLOTS + 16 * i + 16)
                nc.vector.tensor_tensor(ff_h[:, :, :], g[:, 2:4, :], ff_s[:, :, :], ALU.mult).then_inc(pair_free[1], 1)

            def body(i, chunks, first):
                for j in range(16):
                    dve_unit(dve, cyc_of(s, i), j)
                    if j == 3 and not first:
                        mul(i - 1)
                    if j == 11 and not first:
                        dve_ff_turn(dve, name, i - 1)
            bodies(dve, s, body)
            mul(PAIRS - 1)
            dve_ff_turn(dve, name, PAIRS - 1)

        hg_gates, hg_bulk = sem("hg_gates"), sem("hg_bulk")
        hg_staged, hg_turned, hg_copied, hg_diffed = sem("hg_staged"), sem("hg_turned"), sem("hg_copied"), sem("hg_diffed")
        hg_decayed, hg_weighted, hg_scored, hg_masked = sem("hg_decayed"), sem("hg_weighted"), sem("hg_scored"), sem("hg_masked")
        hg_summed, hg_far, hg_out, hg_kept = sem("hg_summed"), sem("hg_far"), sem("hg_out"), sem("hg_kept")
        f_all, g_all = p1[:, :, F_HG:F_HG + 1024], p1[:, :, G_HG:G_HG + 1024]

        def act_hg_gates(act):
            act.wait_ge(pair_free[1], gemms["in1"]["pair0"][1] + 8)
            link_a(act, nc.scalar.activation(kk[:, :, :], f_all, ACT.Abs))
            link_a(act, nc.scalar.activation(kk[:, :, :], kk[:, :, :], ACT.Exp, scale=-1.0))
            nc.scalar.activation(kk[:, :, :], kk[:, :, :], ACT.Ln, bias=1.0).then_inc(hg_gates, 1)
            act.wait_ge(hg_bulk, 1)
            nc.scalar.activation(kk[:, :, :], f_all, ACT.Exp).then_inc(hg_gates, 1)
            nc.scalar.activation(g_all, g_all, ACT.Silu).then_inc(hg_gates, 1)

        def dve_hg_gates(dve):
            dve.wait_ge(hg_gates, 1)
            nc.vector.scalar_tensor_tensor(out=f_all, in0=f_all, scalar=0.0, in1=kk[:, :, :],
                                           op0=ALU.min, op1=ALU.subtract).then_inc(hg_bulk, 1)
            dve.wait_ge(hg_gates, 2)
            nc.vector.tensor_scalar(kk[:, :, :], kk[:, :, :], -1.0, 1.0, ALU.mult, ALU.add).then_inc(hg_bulk, 1)
            dve.wait_ge(hg_gates, 3)
            dve.wait_ge(consts_in, CONSTS)
            for t in range(T):
                link_d(dve, nc.vector.tensor_tensor(
                    p1[:, t, G_HG:G_HG + 1024].rearrange("p (h d) -> p h d", d=HG_D),
                    p1[:, t, G_HG:G_HG + 1024].rearrange("p (h d) -> p h d", d=HG_D),
                    on_g[:, :].rearrange("p (o d) -> p o d", o=1).broadcast_to([P, HG_H, HG_D]), ALU.mult))

        def pool_hg(pool):
            pool.wait_ge(hg_bulk, 2)
            with pool.Fori(0, HG_H) as h:
                pool.wait_ge(hg_turned, h + 1)
                for dst, src, col in ((lf_s, p1, F_HG), (q_s, p1, Q_HG), (k_s, kk, 0)):
                    nc.gpsimd.tensor_copy(dst[:, :, :], src[:, :, bass.ds(h * HG_D + col, HG_D)]).then_inc(hg_staged, 1)

        def pe_hg(pe):
            pe.wait_ge(consts_in, CONSTS)
            pe.sem_inc(hg_turned, 1)
            pe.sem_inc(hg_out, 1)
            with pe.Fori(0, HG_H) as h:
                pe.wait_ge(hg_staged, 3 * h + 3)
                pe.wait_ge(hg_kept, h + 1)
                for t in range(T):
                    nc.tensor.matmul(m[:, 0, t * P:(t + 1) * P], lf_s[:, t, :], cums[:, :], start=(t == 0), stop=(t == 1),
                                     skip_group_check=True)
                for t in range(T):
                    nc.tensor.transpose(m[:, 0, S + t * P:S + (t + 1) * P], q_s[:, t, :], ident[:, :])
                for t in range(T):
                    ins = nc.tensor.transpose(m[:, 1, t * P:(t + 1) * P], k_s[:, t, :], ident[:, :])
                ins.then_inc(hg_turned, 1)
                pe.wait_ge(hg_weighted, h + 2)
                nc.tensor.matmul(m[:, 1, S:S + P], dec[:, 7, 0:P], dec[:, 7, P:S], start=True, stop=True)
                for t in range(T):
                    pe.wait_ge(hg_masked, 2 * h + t + 1)
                    for l in range(8):
                        lhs = dec[:, l, t * P:(t + 1) * P] if l < 7 else kt[:, t * P:(t + 1) * P]
                        rhs = dec[:, l, t * P:(t + 1) * P] if l < 7 else bq[:, S + t * P:S + (t + 1) * P]
                        ins = nc.tensor.matmul(m[:, 2 + l // 4, (l % 4) * P:(l % 4 + 1) * P], lhs, rhs,
                                               start=(l % 4 == 0), stop=(l % 4 == 3), skip_group_check=True)
                    ins.then_inc(hg_scored, 1)
                pe.wait_ge(hg_summed, 2 * h + 3)
                pe.wait_ge(hg_far, h + 1)
                v = [p1[:, t, bass.ds(h * HG_D + I_HG, HG_D)] for t in range(T)]
                nc.tensor.matmul(m[:, 0, 0:P], at3[:, 0, :], v[0], start=True, stop=True)
                nc.tensor.matmul(m[:, 0, P:S], at3[:, 1, :], v[1], start=True, stop=False)
                nc.tensor.matmul(m[:, 0, P:S], at3[:, 2, :], v[0], start=False, stop=True).then_inc(hg_out, 1)

        def act_hg(act):
            act.sem_inc(hg_kept, 1)
            with act.Fori(0, HG_H) as h:
                act.wait_ge(hg_turned, h + 2)
                act.wait_ge(hg_weighted, h + 1)
                nc.scalar.activation(bq[:, :], m[:, 0, :], ACT.Copy).then_inc(hg_copied, 1)
                nc.scalar.activation(kt[:, :], m[:, 1, 0:S], ACT.Copy).then_inc(hg_copied, 1)
                act.wait_ge(hg_diffed, h + 1)
                nc.scalar.activation(dec[:, :, :], dec[:, :, :], ACT.Exp).then_inc(hg_decayed, 1)
                act.wait_ge(hg_scored, 2 * h + 1)
                act.wait_ge(hg_out, h + 1)
                nc.scalar.activation(at3[:, 2, :], m[:, 1, S:S + P], ACT.Copy).then_inc(hg_far, 1)
                act.wait_ge(hg_out, h + 2)
                nc.scalar.activation(p1[:, :, bass.ds(h * HG_D + Q_HG, HG_D)],
                                     m[:, 0, 0:S].rearrange("p (t d) -> p t d", t=T), ACT.Copy).then_inc(hg_kept, 1)

        HG_LINKS = 1

        def dve_hg(dve):
            dve.sem_inc(hg_weighted, 1)
            dve.sem_inc(hg_masked, 1)
            dve.sem_inc(hg_summed, 1)
            dve.wait_ge(masks_in, 16)
            b = bq[:, 0:S]
            c0 = count["d"]
            with dve.Fori(0, HG_H) as h:
                dve.wait_ge(hg_copied, 2 * h + 2)
                nc.vector.tensor_tensor(lam_d[:, 0:1], b[:, 63:64], b[:, 127:128], ALU.add).then_inc(chain_d, 1)
                for l in range(7):
                    w = 1 << l
                    bv = b.rearrange("p (n w) -> p n w", w=2 * w)
                    dv = dec[:, l, :].rearrange("p (n w) -> p n w", w=2 * w)
                    ref = bv[:, :, w - 1:w].broadcast_to([P, S // (2 * w), w])
                    nc.vector.tensor_tensor(dv[:, :, 0:w], ref, bv[:, :, 0:w], ALU.subtract)
                    if l < 6:
                        nc.vector.tensor_tensor(dv[:, :, w:2 * w], bv[:, :, w:2 * w], ref, ALU.subtract)
                    else:
                        nc.vector.tensor_copy(dv[:, :, w:2 * w], bv[:, :, w:2 * w])
                dve.wait_ge(chain_d, c0 + h + 1)
                nc.vector.tensor_scalar(dec[:, 7, 0:64], b[:, 0:64], -1.0, lam_d[:, 0:1], ALU.mult, ALU.add)
                nc.vector.tensor_scalar(dec[:, 7, 64:128], b[:, 64:128], -1.0, b[:, 127:128], ALU.mult, ALU.add)
                nc.vector.tensor_copy(dec[:, 7, 128:192], b[:, 128:192])
                nc.vector.tensor_scalar(dec[:, 7, 192:256], b[:, 192:256], b[:, 191:192], None, ALU.add)\
                  .then_inc(hg_diffed, 1)
                dve.wait_ge(hg_decayed, h + 1)
                for l in range(8):
                    w = 1 << l
                    dv = dec[:, l, :].rearrange("p (n w) -> p n w", w=2 * w)
                    kv_ = kt[:, :].rearrange("p (n w) -> p n w", w=2 * w)
                    qv = bq[:, S:2 * S].rearrange("p (n w) -> p n w", w=2 * w)
                    nc.vector.tensor_tensor(dv[:, :, 0:w], dv[:, :, 0:w], kv_[:, :, 0:w], ALU.mult)
                    ins = nc.vector.tensor_tensor(dv[:, :, w:2 * w], dv[:, :, w:2 * w], qv[:, :, w:2 * w], ALU.mult)
                ins.then_inc(hg_weighted, 1)
                dve.wait_ge(hg_out, h + 1)
                for t in range(T):
                    dve.wait_ge(hg_summed, 2 * h + t + 1)
                    dve.wait_ge(hg_scored, 2 * h + t + 1)
                    nc.vector.tensor_tensor(mp[:, :], m[:, 2:4, :].rearrange("p a n -> p (a n)"), masks[:, :], ALU.mult)\
                      .then_inc(hg_masked, 1)
                    dve.wait_ge(hg_masked, 2 * h + t + 2)
                    nc.vector.tensor_reduce(at3[:, t, :], mp[:, :].rearrange("p (l s) -> p s l", l=8), X, ALU.add)\
                      .then_inc(hg_summed, 1)
            count["d"] += HG_H

        da_staged, da_turned, da_copied, da_scored = sem("da_staged"), sem("da_turned"), sem("da_copied"), sem("da_scored")
        da_max, da_exp, da_mixed, da_back = sem("da_max"), sem("da_exp"), sem("da_mixed"), sem("da_back")
        da_at, da_out, da_kept = sem("da_at"), sem("da_out"), sem("da_kept")
        lam_step = sem("lam_step")
        mix_sq, mix_var, mix_sqrt, mix_done = sem("mix_sq"), sem("mix_var"), sem("mix_sqrt"), sem("mix_done")

        def dve_lambda(dve):
            dve.wait_ge(consts_in, CONSTS)
            for n in range(2):
                link_d(dve, nc.vector.tensor_tensor(lam4[:, 2 * n, :], lam4[:, 2 * n, :], lam4[:, 2 * n + 1, :], ALU.mult))
                link_d(dve, nc.vector.tensor_reduce(st[:, 70 + n:71 + n], lam4[:, 2 * n, :], X, ALU.add))
            nc.vector.tensor_scalar(sub_g[:, :], sub_g[:, :], 1.0 - LAM_INIT, None, ALU.mult).then_inc(lam_step, 1)
            dve.wait_ge(lam_step, 2)
            link_d(dve, nc.vector.tensor_tensor(neg_lam, st[:, 71:72], st[:, 70:71], ALU.subtract))
            link_d(dve, nc.vector.tensor_scalar(neg_lam, neg_lam, -LAM_INIT, None, ALU.add))

        def act_lambda(act):
            act.wait_ge(lam_step, 1)
            nc.scalar.activation(st[:, 70:72], st[:, 70:72], ACT.Exp).then_inc(lam_step, 1)

        def pool_da(pool):
            pool.wait_ge(hg_turned, HG_H + 1)
            pool.wait_ge(pair_free[1], gemms["in1"]["pair0"][1] + 8)
            with pool.Fori(0, DA_H) as h:
                pool.wait_ge(da_turned, h + 1)
                for dst, col in ((q_s, Q_DA), (k_s, K_DA)):
                    nc.gpsimd.tensor_copy(dst[:, :, :], p1[:, :, bass.ds(h * P + col, P)]).then_inc(da_staged, 1)

        def pe_da(pe):
            pe.wait_ge(hg_kept, HG_H + 1)
            pe.sem_inc(da_turned, 1)
            with pe.Fori(0, DA_H) as h:
                pe.wait_ge(da_staged, 2 * h + 2)
                pe.wait_ge(da_kept, h + 1)
                for n, src in enumerate((q_s, k_s)):
                    for t in range(T):
                        ins = nc.tensor.transpose(m[:, 0, (2 * n + t) * P:(2 * n + t + 1) * P], src[:, t, :], ident[:, :])
                ins.then_inc(da_turned, 1)
                pe.wait_ge(da_copied, h + 1)
                for q0, keys in ((0, P), (P, S)):
                    for i in range(2):
                        r = slice(i * DA_D, (i + 1) * DA_D)
                        ins = nc.tensor.matmul(m[:, 1 + i, q0:q0 + keys], bq[r, q0:q0 + P], bq[r, S:S + keys],
                                               start=(q0 == 0), stop=(q0 != 0), skip_group_check=True)
                ins.then_inc(da_scored, 1)
                pe.wait_ge(da_mixed, 2 * h + 2)
                nc.tensor.transpose(m[:, 3, 0:P], sc_da[:, 0:P], ident[:, :])
                nc.tensor.transpose(m[:, 3, P:2 * P], sc_da[:, S:S + P], ident[:, :])
                nc.tensor.transpose(m[:, 3, 2 * P:3 * P], sc_da[:, S + P:2 * S], ident[:, :]).then_inc(da_back, 1)
                pe.wait_ge(da_at, h + 1)
                v = [p1[:, t, bass.ds(h * P + V_DA, P)] for t in range(T)]
                nc.tensor.matmul(m[:, 0, 0:P], at3[:, 0, :], v[0], start=True, stop=True)
                nc.tensor.matmul(m[:, 0, P:S], at3[:, 1, :], v[0], start=True, stop=False)
                nc.tensor.matmul(m[:, 0, P:S], at3[:, 2, :], v[1], start=False, stop=True).then_inc(da_out, 1)

        def act_da(act):
            act.sem_inc(da_kept, 1)
            with act.Fori(0, DA_H) as h:
                act.wait_ge(da_turned, h + 2)
                nc.scalar.activation(bq[:, :], m[:, 0, :], ACT.Copy).then_inc(da_copied, 1)
                act.wait_ge(da_max, 2 * h + 2)
                for n, (o0, w) in enumerate(((0, P), (P, P), (S, S), (2 * S, S))):
                    ins = nc.scalar.activation(sc_da[:, o0:o0 + w], sc_da[:, o0:o0 + w], ACT.Exp,
                                               bias=nmx[:, n:n + 1], accum_out=sm[:, n:n + 1])
                    ins.then_inc(da_exp, 1)
                act.wait_ge(da_back, h + 1)
                nc.scalar.activation(at3[:, :, :], m[:, 3, 0:3 * P].rearrange("p (a n) -> p a n", a=3), ACT.Copy)\
                  .then_inc(da_at, 1)
                act.wait_ge(da_out, h + 1)
                nc.scalar.activation(p1[:, :, bass.ds(h * P, P)], m[:, 0, 0:S].rearrange("p (t d) -> p t d", t=T), ACT.Copy)\
                  .then_inc(da_kept, 1)

        def dve_da(dve):
            dve.wait_ge(bias_in, 16)
            steps = count["d"]
            n_steps = 5

            def link(h, k, ins):
                ins.then_inc(chain_d, 1)
                dve.wait_ge(chain_d, steps + h * n_steps + k + 1)

            with dve.Fori(0, DA_H) as h:
                dve.wait_ge(da_scored, h + 1)
                bias = b_da[:, bass.ds(h, 1), :]
                s0 = sc_da[:, 0:S].rearrange("p (i n) -> p i n", i=2)
                s1 = sc_da[:, S:3 * S].rearrange("p (i n) -> p i n", i=2)
                nc.vector.scalar_tensor_tensor(out=s0, in0=m[:, 1:3, 0:P],
                                               scalar=DA_D ** -0.5, in1=bias[:, :, P:S].broadcast_to([P, 2, P]),
                                               op0=ALU.mult, op1=ALU.add)
                link(h, 0, nc.vector.scalar_tensor_tensor(out=s1, in0=m[:, 1:3, P:P + S],
                                                          scalar=DA_D ** -0.5, in1=bias.broadcast_to([P, 2, S]),
                                                          op0=ALU.mult, op1=ALU.add))
                nc.vector.tensor_reduce(nmx[:, 0:2], s0, X, ALU.max, negate=True).then_inc(da_max, 1)
                nc.vector.tensor_reduce(nmx[:, 2:4], s1, X, ALU.max, negate=True).then_inc(da_max, 1)
                dve.wait_ge(da_exp, 4 * h + 4)
                link(h, 1, nc.vector.reciprocal(rc[:, 0:4], sm[:, 0:4]))
                link(h, 2, nc.vector.tensor_scalar(rc[:, 1:4:2], rc[:, 1:4:2], neg_lam, None, ALU.mult))
                nc.vector.tensor_scalar(sc_da[:, P:S], sc_da[:, P:S], rc[:, 1:2], None, ALU.mult).then_inc(chain_d, 1)
                link(h, 4, nc.vector.tensor_scalar(sc_da[:, 2 * S:3 * S], sc_da[:, 2 * S:3 * S], rc[:, 3:4], None, ALU.mult))
                nc.vector.scalar_tensor_tensor(out=sc_da[:, 0:P], in0=sc_da[:, 0:P], scalar=rc[:, 0:1], in1=sc_da[:, P:S],
                                               op0=ALU.mult, op1=ALU.add).then_inc(da_mixed, 1)
                nc.vector.scalar_tensor_tensor(out=sc_da[:, S:2 * S], in0=sc_da[:, S:2 * S], scalar=rc[:, 2:3],
                                               in1=sc_da[:, 2 * S:3 * S], op0=ALU.mult, op1=ALU.add).then_inc(da_mixed, 1)
            count["d"] += DA_H * n_steps

        HALVES = ((Q_DA, K_DA), (Q_HG, F_HG))

        def act_mix_norm(act):
            act.wait_ge(da_kept, DA_H + 1)
            act.wait_ge(hg_kept, HG_H + 1)
            for src, junk in HALVES:
                nc.scalar.activation(p1[:, :, junk:junk + 1024], p1[:, :, src:src + 1024], ACT.Square).then_inc(mix_sq, 1)
            act.wait_ge(mix_var, 1)
            nc.scalar.activation(ss16, ss16, ACT.Sqrt).then_inc(mix_sqrt, 1)

        def dve_mix_norm(dve):
            s3 = ss16.rearrange("p (n t h) -> p n t h", n=2, t=T)
            for n, (src, junk) in enumerate(HALVES):
                dve.wait_ge(mix_sq, n + 1)
                link_d(dve, nc.vector.tensor_reduce(
                    s3[:, n], p1[:, :, junk:junk + 1024].rearrange("p t (h d) -> p t h d", d=P), X, ALU.add))
            nc.vector.tensor_scalar(ss16, ss16, 1.0 / P, EPS, ALU.mult, ALU.add).then_inc(mix_var, 1)
            dve.wait_ge(mix_sqrt, 1)
            link_d(dve, nc.vector.reciprocal(ss16, ss16))
            for n, (src, junk) in enumerate(HALVES):
                for t in range(T):
                    rows = p1[:, t, src:src + 1024].rearrange("p (h d) -> p h d", d=P)
                    scale = s3[:, n, t, :].rearrange("p (h o) -> p h o", o=1).broadcast_to([P, 8, P])
                    gain = (p1[:, t, G_HG:G_HG + 1024].rearrange("p (h d) -> p h d", d=P) if n else
                            sub_g[:, :].rearrange("p (o d) -> p o d", o=1).broadcast_to([P, 8, P]))
                    link_d(dve, nc.vector.tensor_tensor(rows, rows, scale, ALU.mult))
                    nc.vector.tensor_tensor(rows, rows, gain, ALU.mult).then_inc(mix_done, 1)

        def mixed_rows(k, t):
            col = k * P if k < 8 else Q_HG + (k - 8) * P
            return p1[:, t, col:col + P]

        cx_staged, cx_turned, cx_copied, cx_scored = sem("cx_staged"), sem("cx_turned"), sem("cx_copied"), sem("cx_scored")
        cx_max, cx_exp, cx_soft, cx_back = sem("cx_max"), sem("cx_exp"), sem("cx_soft"), sem("cx_back")
        cx_pt, cx_out, cx_kept = sem("cx_pt"), sem("cx_out"), sem("cx_kept")
        CX_SCALE = P ** -0.5

        def pool_cx(pool):
            pool.wait_ge(pair_free[0], gemms["cq"]["pair0"][0] + 2)
            pool.wait_ge(pair_free[1], gemms["ckv"]["pair0"][1] + 2)
            with pool.Fori(0, CX_H) as h:
                pool.wait_ge(cx_turned, h + 1)
                nc.gpsimd.tensor_copy(xq_s[:, :, :], qx[:, :, bass.ds(h * P, P)]).then_inc(cx_staged, 1)
                nc.gpsimd.tensor_copy(xk_s[:, :, :], kv[:, :, bass.ds(h * P, P)]).then_inc(cx_staged, 1)

        def pe_cx(pe):
            pe.sem_inc(cx_turned, 1)
            with pe.Fori(0, CX_H) as h:
                pe.wait_ge(cx_staged, 2 * h + 2)
                for n, src in enumerate((xq_s, xk_s)):
                    for t in range(T):
                        ins = nc.tensor.transpose(m[:, 0, (2 * n + t) * P:(2 * n + t + 1) * P], src[:, t, :], ident[:, :])
                ins.then_inc(cx_turned, 1)
                pe.wait_ge(cx_copied, h + 1)
                for t in range(T):
                    ins = nc.tensor.matmul(m[:, 1, t * S:(t + 1) * S], xqk[:, t * P:(t + 1) * P], xqk[:, S:2 * S],
                                           start=(t == 0), stop=(t == 1), skip_group_check=True)
                ins.then_inc(cx_scored, 1)
                pe.wait_ge(cx_soft, 2 * h + 2)
                for k in range(2):
                    for t in range(T):
                        ins = nc.tensor.transpose(m[:, 2, (2 * k + t) * P:(2 * k + t + 1) * P],
                                                  xp[:, t, k * P:(k + 1) * P], ident[:, :])
                ins.then_inc(cx_back, 1)
                pe.wait_ge(cx_pt, h + 1)
                pe.wait_ge(cx_kept, h + 1)
                for t in range(T):
                    for k in range(2):
                        ins = nc.tensor.matmul(m[:, 3, t * P:(t + 1) * P], xpt[:, 2 * k + t, :],
                                               kv[:, k, bass.ds(h * P + CX_W, P)], start=(k == 0), stop=(k == 1))
                ins.then_inc(cx_out, 1)

        def act_cx(act):
            act.sem_inc(cx_kept, 1)
            with act.Fori(0, CX_H) as h:
                act.wait_ge(cx_turned, h + 2)
                nc.scalar.activation(xqk[:, :], m[:, 0, :], ACT.Copy).then_inc(cx_copied, 1)
                act.wait_ge(cx_max, h + 1)
                for t in range(T):
                    nc.scalar.activation(xp[:, t, :], m[:, 1, t * S:(t + 1) * S], ACT.Exp, bias=nmx[:, 2 + t:3 + t],
                                         scale=CX_SCALE, accum_out=sm[:, t:t + 1]).then_inc(cx_exp, 1)
                act.wait_ge(cx_back, h + 1)
                nc.scalar.activation(xpt[:, :, :], m[:, 2, :].rearrange("p (a n) -> p a n", a=4), ACT.Copy).then_inc(cx_pt, 1)
                act.wait_ge(cx_out, h + 1)
                nc.scalar.activation(qx[:, :, bass.ds(h * P, P)], m[:, 3, 0:S].rearrange("p (t d) -> p t d", t=T), ACT.Copy)\
                  .then_inc(cx_kept, 1)

        def dve_cx(dve):
            steps = count["d"]
            with dve.Fori(0, CX_H) as h:
                dve.wait_ge(cx_scored, h + 1)
                nc.vector.tensor_reduce(nmx[:, 0:2], m[:, 1, :].rearrange("p (t n) -> p t n", t=T), X, ALU.max, negate=True)\
                  .then_inc(chain_d, 1)
                dve.wait_ge(chain_d, steps + 2 * h + 1)
                nc.vector.tensor_scalar(nmx[:, 2:4], nmx[:, 0:2], CX_SCALE, None, ALU.mult).then_inc(cx_max, 1)
                dve.wait_ge(cx_exp, 2 * h + 2)
                nc.vector.reciprocal(rc[:, 0:2], sm[:, 0:2]).then_inc(chain_d, 1)
                dve.wait_ge(chain_d, steps + 2 * h + 2)
                for t in range(T):
                    nc.vector.tensor_scalar(xp[:, t, :], xp[:, t, :], rc[:, t:t + 1], None, ALU.mult).then_inc(cx_soft, 1)
            count["d"] += 2 * CX_H

        cp = gemms["cmp"]
        kc_turned, kc_copied, blk_sum, blk_split = sem("kc_turned"), sem("kc_copied"), sem("blk_sum"), sem("blk_split")
        cmp_in, gelu_step, gelu_act, g_turned, g_copied, cmp_out = (
            sem("cmp_in"), sem("gelu_step"), sem("gelu_act"), sem("g_turned"), sem("g_copied"), sem("cmp_out"))
        gate_done = sem("gate_done")

        def sp_cmp(sp):
            cyc = cp["u0"] // SLOTS
            wg = gemms["in2"]["w"]
            for j in range(4):
                sp_unit(sp, cyc, j, wg[:, 4 * j:4 * j + 4, GL:GL + 48], 4 * 48, 4)
            for b, w in enumerate((a["cmp_w1_k_2"], a["cmp_w1_v_2"])):
                wv = w.rearrange("(k p) n -> p k n", p=P)
                for j in range(8):
                    sp_unit(sp, cyc, 4 + 8 * b + j, wv[:, 4 * j:4 * j + 4, :], UE, 4)

        def act_cmp_units(act, j0, n, size=UE):
            for j in range(j0, j0 + n):
                act_unit(act, cp["u0"] // SLOTS, j, size)

        def dve_cmp_units(dve, j0, n, size=UE):
            for j in range(j0, j0 + n):
                dve_unit(dve, cp["u0"] // SLOTS, j, size)

        def pe_cmp(pe):
            cyc = cp["u0"] // SLOTS
            p0 = cp["pair0"][0]
            pe.wait_ge(pair_free[0], p0 + 1)
            for j in range(4):
                pe.wait_ge(lo_done, SLOTS + cp["u0"] + j + 1)
                for k in range(4):
                    for t in range(T):
                        h = act_hi[:, 4 * j + k, t * P:(t + 1) * P]
                        l = act_lo[:, 4 * j + k, t * P:(t + 1) * P]
                        whk, wlk = wh[:, j, k * 48:(k + 1) * 48], wl[:, j, k * 48:(k + 1) * 48]
                        dst = g[:, t, 0:48]
                        nc.tensor.matmul(dst, h, whk, start=(j == 0 and k == 0), stop=False)
                        nc.tensor.matmul(dst, h, wlk, start=False, stop=False)
                        ins = nc.tensor.matmul(dst, l, whk, start=False, stop=(j == 3 and k == 3))
                ins.then_inc(unit_used, 1)
            for b in range(2):
                pe.wait_ge(pair_free[1], gemms["in2"]["pair0"][1] + 6)
                for n in range(N_G):
                    if b == 1 and n == 0:
                        pe.wait_ge(kc_copied, 4)
                    for t in range(T):
                        ins = nc.tensor.transpose(m[:, n // 2, (n % 2) * S + t * P:(n % 2) * S + (t + 1) * P],
                                                  p2[:, t, KC + b * 512 + n * P:KC + b * 512 + (n + 1) * P], ident[:, :])
                if b == 0:
                    pe.wait_ge(cmp_in, 64)
                    pe.wait_ge(pair_free[0], p0 + 2)
                nc.tensor.transpose(m[:, 2, 0:CLEN], pos_s[:, b, :], ident[0:CLEN, 0:CLEN]).then_inc(kc_turned, 1)
                pe.wait_ge(blk_split, 2 * b + 2)
                for j in range(8):
                    u = 4 + 8 * b + j
                    pe.wait_ge(lo_done, SLOTS + cp["u0"] + u + 1)
                    for k in range(4):
                        h, l = blk_hi[:, 4 * j + k, :], blk_lo[:, 4 * j + k, :]
                        whk = wh[:, u % SLOTS, k * CHID:(k + 1) * CHID]
                        wlk = wl[:, u % SLOTS, k * CHID:(k + 1) * CHID]
                        dst = g[0:GB, 0, 0:CHID]
                        nc.tensor.matmul(dst, h, whk, start=(j == 0 and k == 0), stop=False)
                        nc.tensor.matmul(dst, h, wlk, start=False, stop=False)
                        ins = nc.tensor.matmul(dst, l, whk, start=False, stop=(j == 7 and k == 3))
                    ins.then_inc(unit_used, 1)
                pe.wait_ge(gelu_step, 4 * b + 4)
                for k in range(2):
                    ins = nc.tensor.transpose(m[:, 3, k * GB:(k + 1) * GB], gh[:, 0, k * P:(k + 1) * P], ident[0:GB, 0:GB])
                ins.then_inc(g_turned, 1)
                pe.wait_ge(g_copied, b + 1)
                if b == 0:
                    for k in range(2):
                        ins = nc.tensor.matmul(m[:, 2, 128:128 + GB], w2[:, 0, k, :], ght[:, k, :], start=(k == 0), stop=(k == 1))
                else:
                    for n in range(N_G):
                        for k in range(2):
                            ins = nc.tensor.matmul(m[0:NC_, 2, n * P:(n + 1) * P], ght[:, k, n * NC_:(n + 1) * NC_],
                                                   w2[:, 1, k, :], start=(k == 0), stop=(k == 1))
                ins.then_inc(cmp_out, 1)

        def act_cmp(act):
            p0 = cp["pair0"][0]
            act_cmp_units(act, 0, 4, 192)
            act.wait_ge(unit_used, SLOTS + cp["u0"] + 4)
            nc.scalar.activation(gate[:, :, :], g[:, 0:2, 0:48], ACT.Sigmoid).then_inc(pair_free[0], 1)
            for b in range(2):
                act.wait_ge(kc_turned, b + 1)
                nc.scalar.activation(ct[:, 0:2, :], m[:, 0, :].rearrange("p (n s) -> p n s", n=2), ACT.Copy).then_inc(kc_copied, 1)
                nc.scalar.activation(ct[:, 2:4, :], m[:, 1, :].rearrange("p (n s) -> p n s", n=2), ACT.Copy).then_inc(kc_copied, 1)
                nc.scalar.activation(post[:, :], m[:, 2, 0:CLEN], ACT.Copy).then_inc(kc_copied, 1)
                act.wait_ge(blk_sum, b + 1)
                nc.scalar.activation(blk_hi[:, :, :], blk[:, :, :], ACT.Copy).then_inc(blk_split, 1)
                act_cmp_units(act, 4 + 8 * b, 8)
                act.wait_ge(unit_used, SLOTS + cp["u0"] + 12 + 8 * b)
                nc.scalar.activation(gh[:, 1, :], g[0:GB, 0, 0:CHID], ACT.Square).then_inc(gelu_act, 1)
                act.wait_ge(gelu_step, 4 * b + 2)
                nc.scalar.activation(gh[:, 1, :], gh[:, 1, :], ACT.Tanh, scale=0.7978845608028654).then_inc(gelu_act, 1)
                act.wait_ge(g_turned, b + 1)
                nc.scalar.activation(ght[:, :, :], m[:, 3, 0:2 * GB].rearrange("p (k n) -> p k n", k=2), ACT.Copy)\
                  .then_inc(g_copied, 1)
                act.wait_ge(cmp_out, b + 1)
                if b == 0:
                    nc.scalar.activation(kcc[:, :], m[:, 2, 128:128 + GB], ACT.Copy).then_inc(kc_copied, 1)
                else:
                    nc.scalar.activation(vcc[:, :], m[0:NC_, 2, :], ACT.Copy).then_inc(kc_copied, 1)

        def dve_cmp(dve):
            dve_cmp_units(dve, 0, 4, 192)
            for b in range(2):
                dve.wait_ge(kc_copied, 4 * b + 3)
                if b == 1:
                    dve.wait_ge(unit_used, SLOTS + cp["u0"] + 12)
                for n in range(N_G):
                    src = ct[:, n, :]
                    win = bass.AP(tensor=src.tensor, offset=src.offset, ap=[list(src.ap[0]), [1, CLEN], [CSTR, NC_]])
                    ins = nc.vector.tensor_tensor(blk[:, :, n * NC_:(n + 1) * NC_], win,
                                                  post[:, :].rearrange("p (i o) -> p i o", o=1).broadcast_to([P, CLEN, NC_]),
                                                  ALU.add)
                ins.then_inc(blk_sum, 1)
                dve.wait_ge(blk_split, 2 * b + 1)
                nc.vector.tensor_tensor(blk_lo[:, :, :], blk[:, :, :], blk_hi[:, :, :].bitcast(F32), ALU.subtract)\
                  .then_inc(blk_split, 1)
                dve_cmp_units(dve, 4 + 8 * b, 8)
                dve.wait_ge(gelu_act, 2 * b + 1)
                link_d(dve, nc.vector.tensor_scalar(gh[:, 1, :], gh[:, 1, :], 0.044715, 1.0, ALU.mult, ALU.add))
                nc.vector.tensor_copy(gh[:, 2, :], g[0:GB, 0, 0:CHID]).then_inc(gelu_step, 1)
                dve.wait_ge(gelu_step, 4 * b + 1)
                nc.vector.tensor_tensor(gh[:, 1, :], gh[:, 1, :], gh[:, 2, :], ALU.mult).then_inc(gelu_step, 1)
                dve.wait_ge(gelu_act, 2 * b + 2)
                nc.vector.scalar_tensor_tensor(out=gh[:, 0, :], in0=gh[:, 1, :], scalar=1.0, in1=gh[:, 2, :],
                                               op0=ALU.add, op1=ALU.mult).then_inc(gelu_step, 1)
                dve.wait_ge(gelu_step, 4 * b + 3)
                nc.vector.tensor_scalar(gh[:, 0, :], gh[:, 0, :], 0.5, None, ALU.mult).then_inc(gelu_step, 1)

        ng_staged, ng_turned, ng_copied = sem("ng_staged"), sem("ng_turned"), sem("ng_copied")
        n_staged, n_turned, n_copied, n_scored = sem("n_staged"), sem("n_turned"), sem("n_copied"), sem("n_scored")
        n_max, n_exp, n_soft, n_back, n_pt, n_out, n_kept = (
            sem("n_max"), sem("n_exp"), sem("n_soft"), sem("n_back"), sem("n_pt"), sem("n_out"), sem("n_kept"))
        SEG = ((2 * P + 4 * P, 15, 0), (0, P, 1), (P, P, 2), (3 * S + 16, 15, 3), (S, S, 4), (2 * S, S, 5))
        C0, C1 = 3 * S, 3 * S + 16

        def pool_n(pool):
            pool.wait_ge(pair_free[1], gemms["in2"]["pair0"][1] + 6)
            pool.wait_ge(g_copied, 2)
            pool.wait_ge(cmp_out, 2)
            with pool.Fori(0, N_G) as gi:
                pool.wait_ge(ng_turned, gi + 1)
                nc.gpsimd.tensor_copy(ns_ks[:, :, :], p2[:, :, bass.ds(gi * P + KS, P)]).then_inc(ng_staged, 1)
                nc.gpsimd.tensor_copy(ns_kw[:, :, :], p2[:, :, bass.ds(gi * P + KW, P)]).then_inc(ng_staged, 1)
                with pool.Fori(0, HPG) as hj:
                    h = gi * HPG + hj
                    pool.wait_ge(n_turned, h + 1)
                    nc.gpsimd.tensor_copy(ns_q[:, :, :], p2[:, :, bass.ds(h * P, P)]).then_inc(n_staged, 1)

        def pe_n(pe):
            pe.wait_ge(kc_copied, 8)
            pe.sem_inc(ng_turned, 1)
            pe.sem_inc(n_turned, 1)
            with pe.Fori(0, N_G) as gi:
                pe.wait_ge(ng_staged, 2 * gi + 2)
                for n, src in enumerate((ns_ks, ns_kw)):
                    for t in range(T):
                        ins = nc.tensor.transpose(m[:, 0, (2 * n + t) * P:(2 * n + t + 1) * P], src[:, t, :], ident[:, :])
                ins.then_inc(ng_turned, 1)
                with pe.Fori(0, HPG) as hj:
                    h = gi * HPG + hj
                    pe.wait_ge(n_staged, h + 1)
                    for t in range(T):
                        ins = nc.tensor.transpose(m[:, 1, t * P:(t + 1) * P], ns_q[:, t, :], ident[:, :])
                    ins.then_inc(n_turned, 1)
                    pe.wait_ge(n_copied, h + 1)
                    pe.wait_ge(ng_copied, gi + 1)
                    pe.wait_ge(n_kept, h + 1)
                    q = [qn[:, t * P:(t + 1) * P] for t in range(T)]
                    kcg = kcc[:, bass.ds(gi * NC_, NC_)]
                    nc.tensor.matmul(m[:, 2, 0:P], q[0], ksw[:, 0:P], start=True, stop=False, skip_group_check=True)
                    nc.tensor.matmul(m[:, 2, P:S], q[0], ksw[:, S:S + P], start=False, stop=False, skip_group_check=True)
                    nc.tensor.matmul(m[:, 2, S:S + NC_], q[0], kcg, start=False, stop=False, skip_group_check=True)
                    nc.tensor.matmul(m[:, 2, S + 16:S + 16 + NC_], q[1], kcg, start=False, stop=True, skip_group_check=True)
                    nc.tensor.matmul(m[:, 3, :], q[1], ksw[:, :], start=True, stop=True).then_inc(n_scored, 1)
                    pe.wait_ge(n_soft, 6 * h + 6)
                    for n, o0 in enumerate((0, P, S, S + P, 2 * S, 2 * S + P)):
                        nc.tensor.transpose(m[:, n // 4, (n % 4) * P:(n % 4 + 1) * P], sn[:, o0:o0 + P], ident[:, :])
                    nc.tensor.transpose(m[0:NC_, 1, 2 * P:3 * P], sn[:, C0:C0 + NC_], ident[:, :])
                    nc.tensor.transpose(m[0:NC_, 1, 3 * P:4 * P], sn[:, C1:C1 + NC_], ident[:, :]).then_inc(n_back, 1)
                    pe.wait_ge(n_pt, 3 * h + 3)
                    vs = [p2[:, t, bass.ds(gi * P + VS, P)] for t in range(T)]
                    vw = [p2[:, t, bass.ds(gi * P + VW, P)] for t in range(T)]
                    vc = vcc[:, bass.ds(gi * P, P)]
                    p_ = [pt[:, n * P:(n + 1) * P] for n in range(6)] + [pt[0:NC_, n * P:(n + 1) * P] for n in (6, 7)]
                    for dst, terms in ((m[:, 2, 0:P], ((0, vs[0]), (1, vw[0]), (6, vc))),
                                       (m[:, 2, P:S], ((2, vs[0]), (3, vs[1]), (4, vw[0]), (5, vw[1]), (7, vc)))):
                        for n, (pn, v) in enumerate(terms):
                            ins = nc.tensor.matmul(dst, p_[pn], v, start=(n == 0), stop=(n == len(terms) - 1))
                    ins.then_inc(n_out, 1)

        def act_n(act):
            act.sem_inc(n_kept, 1)
            with act.Fori(0, N_G) as gi:
                act.wait_ge(ng_turned, gi + 2)
                nc.scalar.activation(ksw[:, :], m[:, 0, :], ACT.Copy).then_inc(ng_copied, 1)
                with act.Fori(0, HPG) as hj:
                    h = gi * HPG + hj
                    act.wait_ge(n_turned, h + 2)
                    nc.scalar.activation(qn[:, :], m[:, 1, 0:S], ACT.Copy, scale=P ** -0.5).then_inc(n_copied, 1)
                    act.wait_ge(n_max, h + 1)
                    for o0, w, n in SEG:
                        nc.scalar.activation(sn[:, o0:o0 + w], sn[:, o0:o0 + w], ACT.Exp, bias=nmx[:, n:n + 1],
                                             accum_out=sm[:, n:n + 1]).then_inc(n_exp, 1)
                    act.wait_ge(n_back, h + 1)
                    nc.scalar.activation(pt[:, 0:512], m[:, 0, :], ACT.Copy).then_inc(n_pt, 1)
                    nc.scalar.activation(pt[:, 512:768], m[:, 1, 0:S], ACT.Copy).then_inc(n_pt, 1)
                    nc.scalar.activation(pt[0:NC_, 768:1024], m[0:NC_, 1, S:2 * S], ACT.Copy).then_inc(n_pt, 1)
                    act.wait_ge(n_out, h + 1)
                    nc.scalar.activation(p2[:, :, bass.ds(h * P, P)], m[:, 2, 0:S].rearrange("p (t d) -> p t d", t=T),
                                         ACT.Copy).then_inc(n_kept, 1)

        def dve_n(dve):
            dve.wait_ge(bias_in, 32)
            steps = count["d"]
            n_steps = 4

            def link(h, k, ins):
                ins.then_inc(chain_d, 1)
                dve.wait_ge(chain_d, steps + h * n_steps + k + 1)

            with dve.Fori(0, N_G) as gi:
                with dve.Fori(0, HPG) as hj:
                    h = gi * HPG + hj
                    dve.wait_ge(n_scored, h + 1)
                    bias = b_n[:, bass.ds(h, 1), :]
                    s0 = sn[:, 0:S].rearrange("p (i n) -> p i n", i=2)
                    s1 = sn[:, S:3 * S].rearrange("p (i n) -> p i n", i=2)
                    sc = sn[:, C0:C0 + 32].rearrange("p (t n) -> p t n", t=2)[:, :, 0:NC_]
                    nc.vector.tensor_tensor(s0, m[:, 2, 0:S].rearrange("p (i n) -> p i n", i=2),
                                            bias[:, :, P:S].broadcast_to([P, 2, P]), ALU.add)
                    nc.vector.tensor_tensor(sc, m[:, 2, S:S + 32].rearrange("p (t n) -> p t n", t=2)[:, :, 0:NC_],
                                            bc[:, :, :, bass.ds(h, 1)].rearrange("p t c o -> p t (c o)"), ALU.add)
                    link(h, 0, nc.vector.tensor_tensor(s1, m[:, 3, :].rearrange("p (i n) -> p i n", i=2),
                                                       bias.broadcast_to([P, 2, S]), ALU.add))
                    mx = nmx[:, 0:6].rearrange("p (t b) -> p t b", b=3)
                    nc.vector.tensor_reduce(mx[:, :, 0], sc, X, ALU.max, negate=True)
                    nc.vector.tensor_reduce(mx[:, 0, 1:3], s0, X, ALU.max, negate=True)
                    link(h, 1, nc.vector.tensor_reduce(mx[:, 1, 1:3], s1, X, ALU.max, negate=True))
                    nc.vector.tensor_scalar(nmx[:, 0:6], nmx[:, 0:6], 1e29, None, ALU.min).then_inc(n_max, 1)
                    dve.wait_ge(n_exp, 6 * h + 6)
                    link(h, 2, nc.vector.tensor_scalar(rc[:, 0:6], sm[:, 0:6], 1e-30, None, ALU.max))
                    link(h, 3, nc.vector.reciprocal(rc[:, 0:6], rc[:, 0:6]))
                    gv = gate[:, :, :].rearrange("p t (b h) -> p t b h", b=3)[:, :, :, bass.ds(h, 1)]
                    nc.vector.tensor_tensor(rc[:, 0:6].rearrange("p (t b) -> p t b", b=3),
                                            rc[:, 0:6].rearrange("p (t b) -> p t b", b=3),
                                            gv.rearrange("p t b o -> p t (b o)"), ALU.mult).then_inc(gate_done, 1)
                    dve.wait_ge(gate_done, h + 1)
                    for o0, w, n in SEG:
                        nc.vector.tensor_scalar(sn[:, o0:o0 + w], sn[:, o0:o0 + w], rc[:, n:n + 1], None, ALU.mult)\
                          .then_inc(n_soft, 1)
            count["d"] += N_H * n_steps

        def bcast(ap1, n):
            return bass.AP(tensor=ap1.tensor, offset=ap1.offset, ap=[[0, P], [1, n]])

        block = ctx.enter_context(nc.Block())

        @block.sync
        def _(sp):
            sp.dma_start(x[:, :, :], a["x"].rearrange("(t p) d -> p t d", p=P)).then_inc(x_in, 16)
            sp.dma_start(ident[:, :], a["c_ident"]).then_inc(consts_in, 16)
            sp.dma_start(cums[:, :], a["c_cums"]).then_inc(consts_in, 16)
            sp.dma_start(oh_f[:, :], a["c_falling"]).then_inc(consts_in, 16)
            sp.dma_start(oh_r[:, :], a["c_rising"]).then_inc(consts_in, 16)
            sp.dma_start(tab[0:32, 0:8], a["rel_bias"]).then_inc(consts_in, 16)
            sp.dma_start(tab[0:32, 8:24], a["rel_bias_2"]).then_inc(consts_in, 16)
            sp.dma_start(sub_g[:, :], bcast(a["da_subln_g"], P)).then_inc(consts_in, 16)
            sp.dma_start(on_g[:, :], bcast(a["hg_onorm_g"], P)).then_inc(consts_in, 16)
            for n, k in enumerate(("lambda_q1", "lambda_k1", "lambda_q2", "lambda_k2")):
                sp.dma_start(lam4[:, n, :], bcast(a[k], DA_D)).then_inc(consts_in, 16)
            sp.dma_start(masks[:, :], a["c_masks"]).then_inc(masks_in, 16)
            sp_gemm(sp, "in1")
            sp_gemm(sp, "out1")
            sp_gemm(sp, "ckv")
            sp_gemm(sp, "cq")
            sp_gemm(sp, "co")
            sp_gemm_cols(sp, "ff1")
            sp_gemm(sp, "fo1")
            sp_gemm(sp, "in2")
            sp_cmp(sp)
            sp_gemm(sp, "out2")
            sp_gemm_cols(sp, "ff2")
            sp_gemm(sp, "fo2")
            sp.wait_ge(xn_done, 2 * len(XN) + 2)
            sp.dma_start(out.rearrange("(t p) d -> p t d", p=P), x[:, :, :]).then_inc(out_done, 16)
            sp.wait_ge(out_done, 16)

        @block.gpsimd
        def _(pool):
            pool.dma_start(g_a[:, :], bcast(a["mix_pre_g"], D)).then_inc(ga_in, 16)
            pool.dma_start(g_b[:, :], bcast(a["mix_post_g"], D)).then_inc(gb_in, 16)
            pool.wait_ge(bt_sb, 1)
            rows = bt[:, :]
            skewed = bass.AP(tensor=rows.tensor, offset=rows.offset + P - 1, ap=[list(rows.ap[0]), [-1, P], [1, S]])
            pool.dma_start(dram_bias, skewed).then_inc(bt_stored, 16)
            pool.wait_ge(bt_stored, 16)
            pool.wait_ge(xn_done, 2)
            pool.dma_start(b_da[:, :, :], dram_bias[0:DA_H].rearrange("h p k -> p h k")).then_inc(bias_in, 16)
            pool_hg(pool)
            pool_da(pool)
            pool.wait_ge(da_mixed, 2 * DA_H)
            pool.dma_start(g_a[:, :], bcast(a["mem_norm_g"], D)).then_inc(ga_in, 16)
            pool.wait_ge(x_done, 2)
            pool.dma_start(memx[:, :, :], a["mem"].rearrange("(t p) d -> p t d", p=P)).then_inc(mem_in, 16)
            pool.dma_start(g_b[:, :], bcast(a["cross_post_g"], D)).then_inc(gb_in, 16)
            pool.wait_ge(xn_done, 4)
            pool.dma_start(g_a[:, :], bcast(a["cross_pre_g"], D)).then_inc(ga_in, 16)
            pool_cx(pool)
            pool.wait_ge(xn_done, 6)
            pool.dma_start(g_a[:, :], bcast(a["ffn_pre_g"], D)).then_inc(ga_in, 16)
            pool.wait_ge(x_done, 4)
            pool.dma_start(g_b[:, :], bcast(a["ffn_post_g"], D)).then_inc(gb_in, 16)
            pool.wait_ge(lo_evac, BANKS["ff1"] + 2 * PAIRS)
            pool.dma_start(g_a[:, :], bcast(a["mix_norm_g_2"], D)).then_inc(ga_in, 16)
            pool.wait_ge(lo_evac, BANKS["n2"] + 8)
            for n, k in enumerate(("cmp_pos_k_2", "cmp_pos_v_2")):
                pool.dma_start(pos_s[:, n, :], a[k]).then_inc(cmp_in, 16)
            for n, k in enumerate(("cmp_w2_k_2", "cmp_w2_v_2")):
                pool.dma_start(w2[:, n, :, :], a[k].rearrange("(k p) d -> p k d", p=P)).then_inc(cmp_in, 16)
            pool.wait_ge(cmp_out, 2)
            pool.wait_ge(kc_copied, 8)
            pool.dma_start(b_n[:, :, :], dram_bias[DA_H:DA_H + N_H].rearrange("h p k -> p h k")).then_inc(bias_in, 16)
            pool.dma_start(g_a[:, :], bcast(a["ffn_norm_g_2"], D)).then_inc(ga_in, 16)
            pool_n(pool)
            pool.wait_ge(lo_evac, BANKS["ff2"] + 2 * PAIRS)
            pool.dma_start(g_a[:, :], bcast(a["final_norm_g_2"], D)).then_inc(ga_in, 16)

        @block.tensor
        def _(pe):
            pe.sem_inc(unit_used, SLOTS)
            pe.wait_ge(consts_in, CONSTS)
            pe.wait_ge(tab_ready, 1)
            nc.tensor.matmul(g[0:24, 0, :], tab[:, :], oh_f[:, :], start=True, stop=True).then_inc(bt_ready, 1)
            for t in range(T):
                for c in range(NC_):
                    o0 = P * t - CSTR * c - (CLEN - 1) + 256
                    ins = nc.tensor.matmul(g[:, 1, (t * NC_ + c) * N_H:(t * NC_ + c + 1) * N_H], oh_r[:, o0:o0 + P], tab[:, 8:24],
                                           start=(t == 0 and c == 0), stop=(t == 1 and c == NC_ - 1), skip_group_check=True)
            ins.then_inc(bt_ready, 1)
            pe.wait_ge(xn_done, 2)
            pe_turn(pe, "n1", lambda k, t: xn[:, t, k * P:(k + 1) * P])
            turned_in(pe, "n1")
            pe.wait_ge(bt_sb, 1)
            pe.wait_ge(bc_sb, 1)
            pe_gemm(pe, "in1")
            pe_hg(pe)
            pe_da(pe)
            pe.wait_ge(mix_done, 4)
            pe_turn(pe, "mix1", mixed_rows)
            turned_in(pe, "mix1")
            pe_gemm(pe, "out1")
            pe.wait_ge(xn_done, 4)
            pe_turn(pe, "nmem", lambda k, t: xn[:, t, k * P:(k + 1) * P])
            turned_in(pe, "nmem")
            pe_gemm(pe, "ckv")
            pe.wait_ge(xn_done, 6)
            pe_turn(pe, "ncx", lambda k, t: xn[:, t, k * P:(k + 1) * P])
            turned_in(pe, "ncx")
            pe_gemm(pe, "cq")
            pe_cx(pe)
            pe.wait_ge(cx_kept, CX_H + 1)
            pe_turn(pe, "cx", lambda k, t: qx[:, t, k * P:(k + 1) * P], 2)
            turned_in(pe, "cx", 2)
            pe_gemm(pe, "co")
            pe.wait_ge(xn_done, 8)
            pe_turn(pe, "nff", lambda k, t: xn[:, t, k * P:(k + 1) * P])
            turned_in(pe, "nff")
            pe_ffn_in(pe, "ff1")
            turned_in(pe, "ff1", 2 * PAIRS)
            pe_gemm(pe, "fo1", ht_hi, ht_lo)
            pe.wait_ge(xn_done, 10)
            pe_turn(pe, "n2", lambda k, t: xn[:, t, k * P:(k + 1) * P])
            turned_in(pe, "n2")
            pe_gemm(pe, "in2")
            pe_cmp(pe)
            pe_n(pe)
            pe.wait_ge(n_kept, N_H + 1)
            pe_turn(pe, "mix2", lambda k, t: p2[:, t, k * P:(k + 1) * P])
            turned_in(pe, "mix2")
            pe_gemm(pe, "out2")
            pe.wait_ge(xn_done, 12)
            pe_turn(pe, "nff2", lambda k, t: xn[:, t, k * P:(k + 1) * P])
            turned_in(pe, "nff2")
            pe_ffn_in(pe, "ff2")
            turned_in(pe, "ff2", 2 * PAIRS)
            pe_gemm(pe, "fo2", ht_hi, ht_lo)

        def cols(dst):
            return lambda c: dst[:, :, bass.ds(c * NB, NB)]

        @block.scalar
        def _(act):
            act.sem_inc(pair_free[0], 1)
            act.sem_inc(pair_free[1], 1)
            act.wait_ge(x_in, 16)
            act_stats(act, "n1", x, y_r)
            act_turn(act, "n1")
            act.wait_ge(bt_ready, 2)
            nc.scalar.activation(bt[:, :], g[0:24, 0, :], ACT.Copy).then_inc(bt_sb, 1)
            act_lambda(act)
            act.wait_ge(bt_stored, 16)
            act_gemm(act, "in1", cols(p1))
            act_hg_gates(act)
            act_hg(act)
            act_da(act)
            act_mix_norm(act)
            act_turn(act, "mix1")
            act_gemm(act, "out1", cols(y_r))
            act.wait_ge(pair_free[1], gemms["out1"]["pair0"][1] + 3)
            act_stats(act, "post1", y_r, xn)
            act.wait_ge(mem_in, 16)
            act_stats(act, "nmem", memx, xn)
            act_turn(act, "nmem")
            act_gemm(act, "ckv", cols(kv))
            act_stats(act, "ncx", x, xn)
            act_turn(act, "ncx")
            act_gemm(act, "cq", cols(qx))
            act_cx(act)
            act_turn(act, "cx", 2)
            act_gemm(act, "co", cols(y_r))
            act.wait_ge(pair_free[1], gemms["co"]["pair0"][1] + 3)
            act_stats(act, "postcx", y_r, xn)
            act.wait_ge(x_done, 4)
            act_stats(act, "nff", x, xn)
            act_turn(act, "nff")
            act_ffn_in(act, "ff1")
            act_gemm(act, "fo1", cols(y_a))
            act.wait_ge(pair_free[1], gemms["fo1"]["pair0"][1] + 3)
            act_stats(act, "postff", y_a, xn)
            act.wait_ge(x_done, 6)
            act_stats(act, "n2", x, xn)
            act_turn(act, "n2")
            act_gemm(act, "in2", cols(p2))
            act_cmp(act)
            act_n(act)
            act_turn(act, "mix2")
            act_gemm(act, "out2", cols(y_r))
            act.wait_ge(x_done, 8)
            act_stats(act, "nff2", x, xn)
            act_turn(act, "nff2")
            act_ffn_in(act, "ff2")
            act_gemm(act, "fo2", cols(y_a))
            act.wait_ge(x_done, 10)
            act_stats(act, "nfin", x, xn)

        def dve_residual(dve, y, name):
            dve.wait_ge(pair_free[1], gemms[name]["pair0"][1] + 3)
            for t in range(T):
                nc.vector.tensor_tensor(x[:, t, :], x[:, t, :], y[:, t, :], ALU.add).then_inc(x_done, 1)

        @block.vector
        def _(dve):
            dve.sem_inc(lo_done, SLOTS)
            nc.vector.memset(tab[32:33, :], MASKED).then_inc(tab_ready, 1)
            dve.wait_ge(x_in, 16)
            dve_norm(dve, "n1", x, 1)
            dve_turn(dve, "n1")
            dve.wait_ge(bt_ready, 2)
            nc.vector.tensor_copy(bc[:, :, :, :].rearrange("p t c h -> p (t c h)"), g[:, 1, 0:T * NC_ * N_H]).then_inc(bc_sb, 1)
            dve_lambda(dve)
            dve_gemm(dve, "in1")
            dve_hg_gates(dve)
            dve_hg(dve)
            dve_da(dve)
            dve_mix_norm(dve)
            dve_turn(dve, "mix1")
            dve_gemm(dve, "out1")
            dve_post(dve, "post1", y_r, 1)
            dve_norm(dve, "nmem", memx, 2)
            dve_turn(dve, "nmem")
            dve_gemm(dve, "ckv")
            dve_norm(dve, "ncx", x, 3)
            dve_turn(dve, "ncx")
            dve_gemm(dve, "cq")
            dve_cx(dve)
            dve_turn(dve, "cx", 2)
            dve_gemm(dve, "co")
            dve_post(dve, "postcx", y_r, 2)
            dve_norm(dve, "nff", x, 4)
            dve_turn(dve, "nff")
            dve_ffn_in(dve, "ff1")
            dve_gemm(dve, "fo1")
            dve_post(dve, "postff", y_a, 3)
            dve_norm(dve, "n2", x, 5)
            dve_turn(dve, "n2")
            dve_gemm(dve, "in2")
            dve_cmp(dve)
            dve_n(dve)
            dve_turn(dve, "mix2")
            dve_gemm(dve, "out2")
            dve_residual(dve, y_r, "out2")
            dve_norm(dve, "nff2", x, 6)
            dve_turn(dve, "nff2")
            dve_ffn_in(dve, "ff2")
            dve_gemm(dve, "fo2")
            dve_residual(dve, y_a, "fo2")
            dve_stats(dve, "nfin")
            dve.wait_ge(ga_in, 16 * 7)
            for t in range(T):
                nc.vector.scalar_tensor_tensor(out=x[:, t, :], in0=x[:, t, :], scalar=rstd[:, t:t + 1],
                                               in1=g_a[:, :], op0=ALU.mult, op1=ALU.mult).then_inc(xn_done, 1)


_INS = ["x", "mem", "w_in", "w_out", "w_cq", "w_ckv", "w_co", "w_ffn_in", "w_ffn_out", "mix_pre_g", "mix_post_g",
        "cross_pre_g", "cross_post_g", "mem_norm_g", "ffn_pre_g", "ffn_post_g", "da_subln_g", "hg_onorm_g",
        "lambda_q1", "lambda_k1", "lambda_q2", "lambda_k2", "rel_bias", "rel_bias_2", "mix_norm_g_2", "ffn_norm_g_2",
        "final_norm_g_2", "nsa_w_in_2", "nsa_w_out_2", "cmp_pos_k_2", "cmp_w1_k_2", "cmp_w2_k_2", "cmp_pos_v_2",
        "cmp_w1_v_2", "cmp_w2_v_2", "ffn_w_in_2", "ffn_w_out_2"]
_WHOLE = ("rel_bias", "rel_bias_2", "final_norm_g_2")


def kernel(**inputs):
    import numpy as _np
    import concourse.bacc as _bacc
    from concourse import mybir as _mybir
    from concourse.bass_utils import run_bass_kernel_spmd as _run

    nc = _bacc.Bacc("TRN2", target_bir_lowering=False, num_devices=1)
    arrays, aps = {}, {}
    for name in _INS:
        v = _np.ascontiguousarray(inputs[name])
        arrays[f"in_{name}"] = v if name in _WHOLE else v.reshape(v.shape[1:])
    falling, rising = rel_rows()
    for name, v in (("c_ident", _np.eye(128, dtype=_np.float32)), ("c_cums", cumsum_lhs()), ("c_masks", level_masks()),
                    ("c_falling", falling), ("c_rising", rising)):
        arrays[f"in_{name}"] = v
    for key, v in arrays.items():
        aps[key[3:]] = nc.dram_tensor(key, v.shape, _mybir.dt.float32, kind="ExternalInput").ap()
    out = nc.dram_tensor("out_x", (256, 2048), _mybir.dt.float32, kind="ExternalOutput").ap()
    build(nc, aps, out)
    r = _run(nc, [arrays], core_ids=[0])
    return r.results[0]["out_x"].reshape(1, 256, 2048)
```

```python
from contextlib import ExitStack

import concourse.bass as bass
from concourse import mybir

F32 = mybir.dt.float32
F32R = mybir.dt.float32r
ALU = mybir.AluOpType
ACT = mybir.ActivationFunctionType
X = mybir.AxisListType.X

P = 128
D = 2048
T = 2
S = T * P
NB = 512
HB = 256
SLOTS = 4
UE = 1024
EPS = 1e-6

DA_H, DA_D = 8, 64
HG_H, HG_D = 8, 128
Q_DA, K_DA, V_DA, F_HG, Q_HG, I_HG, G_HG = (1024 * n for n in range(7))
IN1 = 7168
LAM_INIT = 0.2
CHUNK = 64
LEVELS = 8
CX_H = 4
CX_W = 512
FH = 5632
PAIRS = FH // NB
FKT = FH // P
KV = F_HG
N_H, N_G, HPG = 16, 4, 4
KC, VC, KS, VS, KW, VW, GL = 2048, 2560, 3072, 3584, 4096, 4608, 5120
IN2 = 5168
NC_, CSTR, CLEN, CHID = 15, 16, 32, 256
GB = N_G * NC_
MASKED = -1e30


def rel_rows():
    import math
    import numpy as np

    def bucket(n):
        if n < 16:
            return n
        return min(31, 16 + int(math.log(n / 16) / math.log(8.0) * 16))

    falling = np.zeros((33, 512), np.float32)
    rising = np.zeros((33, 512), np.float32)
    for m in range(512):
        d = 255 - m
        falling[bucket(d) if d >= 0 else 32, m] = 1
        d = m - 256
        rising[bucket(d) if d >= 0 else 32, m] = 1
    return falling, rising


def level_masks():
    import numpy as np
    s, t = np.arange(128)[:, None], np.arange(128)[None, :]
    m = np.zeros((128, 8, 128), np.float32)
    for l in range(7):
        w = 2 << l
        m[:, l, :] = (s // w == t // w) & (s % w < w // 2) & (t % w >= w // 2)
    m[:, 7, :] = s == t
    return m.reshape(128, 1024)


def cumsum_lhs():
    import numpy as np
    s, t = np.arange(128)[:, None], np.arange(128)[None, :]
    return ((s // CHUNK == t // CHUNK) & (s <= t)).astype(np.float32)


def build(nc, a, out):
    ctx = ExitStack()
    with ctx:
        base = (nc.sbuf_base + 31) // 32 * 32
        place = {}

        def at(name, shape, offset, dt=F32):
            return nc.alloc_sbuf_tensor_at(name, shape, dt, offset=base + offset)

        o_raw, o_wh, o_wl = 0, 16384, 32768
        o_ah, o_al = 49152, 65536
        o_x, o_ga, o_gb, o_r = 81920, 98304, 106496, 114688
        o_small = o_r + 2 * FKT * S * 4
        raw = at("raw", [P, SLOTS, UE], o_raw)
        wh = at("wh", [P, SLOTS, UE], o_wh, F32R)
        wl = at("wl", [P, SLOTS, UE], o_wl, F32R)
        act_hi = at("act_hi", [P, 16, S], o_ah, F32R)
        act_lo = at("act_lo", [P, 16, S], o_al, F32R)
        y_a = at("y_a", [P, 8, T, HB], o_al)
        junk_a = at("junk_a", [P, 2, T, NB], o_ah)
        x = at("x", [P, T, D], o_x)
        g_a = at("g_a", [P, D], o_ga)
        memx = at("memx", [P, T, D], o_ga)
        g_b = at("g_b", [P, D], o_gb)
        b_da = at("b_da", [P, DA_H, S], o_ga)
        ff_s = at("ff_s", [P, T, NB], o_ga)
        ff_h = at("ff_h", [P, T, NB], o_ga + 4096)
        ht_hi = at("ht_hi", [P, FKT, S], o_r, F32R)
        ht_lo = at("ht_lo", [P, FKT, S], o_r + FKT * S * 4, F32R)
        junk_r = at("junk_r", [P, 2, T, NB], o_r)
        junk_x = at("junk_x", [P, T, D], o_r + 16384)
        y_r = at("y_r", [P, 8, T, HB], o_r + 45056)
        p1 = at("p1", [P, T, IN1], o_r)
        o = o_r + 57344
        kk = at("kk", [P, T, 1024], o)
        o += 8192
        masks = at("masks", [P, 1024], o); o += 4096
        dec = at("dec", [P, LEVELS, S], o)
        junk_m1 = at("junk_m1", [P, D], o)
        sc_da = at("sc_da", [P, 768], o); o += 8192
        junk_m0 = at("junk_m0", [P, D], o)
        mp = at("mp", [P, 1024], o); o += 4096
        lf_s = at("lf_s", [P, T, P], o); o += 1024
        q_s = at("q_s", [P, T, P], o); o += 1024
        k_s = at("k_s", [P, T, P], o); o += 1024
        bq = at("bq", [P, 512], o); o += 2048
        kt = at("kt", [P, S], o); o += 1024
        at3 = at("at3", [P, 3, P], o); o += 1536
        assert o <= o_small
        o = o_r + 57344
        q_s1 = at("q_s1", [P, T, P], o); o += 1024
        k_s1 = at("k_s1", [P, T, P], o); o += 1024
        bq1 = at("bq1", [P, 512], o); o += 2048
        sc_da1 = at("sc_da1", [P, 768], o); o += 3072
        o += 1024
        at31 = at("at31", [P, 3, P], o)
        o = o_r
        qx = at("qx", [P, T, CX_W], o); o += 4096
        xq_s = at("xq_s", [P, T, P], o); o += 1024
        xk_s = at("xk_s", [P, T, P], o); o += 1024
        xqk = at("xqk", [P, 512], o); o += 2048
        xp = at("xp", [P, T, S], o); o += 2048
        xpt = at("xpt", [P, 4, P], o); o += 2048
        p2 = at("p2", [P, T, IN2], o_r)
        o = o_r + IN2 * T * 4
        kcc = at("kcc", [P, GB], o); o += 256
        vcc = at("vcc", [NC_, N_G * P], o); o += 2048
        gate = at("gate", [P, T, 48], o); o += 384
        b_n = at("b_n", [P, N_H, S], o)
        c0 = o
        blk_hi, blk_lo = [], []
        for n in range(2):
            if n == 1:
                post = at("post", [P, 2, CLEN], o); o += 256
                pos_s = at("pos_s", [CLEN, 2, P], o); o += 1024
            blk_hi.append(at(f"blk_hi{n}", [P, CLEN, GB], o, F32R)); o += 7680
            blk_lo.append(at(f"blk_lo{n}", [P, CLEN, GB], o, F32R)); o += 7680
        blk = at("blk", [P, CLEN, GB], o)
        gh = at("gh", [GB, 3, 2, CHID], o)
        ght = at("ght", [P, 2, 2, GB], o + 6144); o += 7680
        w2 = at("w2", [P, 2, 2, P], o); o += 2048
        assert o <= o_small
        o = c0 + 16384
        sn = at("sn", [P, 800], o); o += 3200
        pt = at("pt", [P, 1024], o); o += 4096
        ksw = at("ksw", [P, 512], o); o += 2048
        qn = at("qn", [P, S], o); o += 1024
        ns_q = at("ns_q", [P, T, P], o); o += 1024
        ns_ks = at("ns_ks", [P, T, P], o); o += 1024
        ns_kw = at("ns_kw", [P, T, P], o); o += 1024
        sn1 = at("sn1", [P, 800], o); o += 3200
        pt1 = at("pt1", [P, 1024], o); o += 4096
        qn1 = at("qn1", [P, S], o); o += 1024
        ns_q1 = at("ns_q1", [P, T, P], o); o += 1024
        assert o <= o_small
        oh_f = at("oh_f", [33, 512], o_r + 32768)
        oh_r = at("oh_r", [33, 512], o_r + 34816)
        bt = at("bt", [24, 512], o_r + 36864)
        g_rows = at("g_rows", [6 * 16, P], o_r + 38912)
        o = o_small
        ident = at("ident", [P, P], o); o += 512
        cums = at("cums", [P, P], o); o += 512
        bc = at("bc", [P, T, NC_, N_H], o); o += 1920
        tab = at("tab", [33, 24], o); o += 96
        sub_g = at("sub_g", [P, P], o); o += 512
        on_g = at("on_g", [P, P], o); o += 512
        lam4 = at("lam4", [P, 4, DA_D], o); o += 1024
        st = at("st", [P, 256], o); o += 1024
        g_cols = at("g_cols", [P, 6 * 16], o); o += 384
        assert base + o <= nc.sbuf_usable_end

        ss = st[:, 0:2]
        ss8 = st[:, 96:104].rearrange("p (t c) -> p t c", t=T)
        ss_y = st[:, 104:106]
        lam_d = st[:, 4:6]
        neg_lam = st[:, 6:7]
        nmx = st[:, 8:14]
        sm = st[:, 16:22]
        rc = st[:, 24:30]
        ss16 = st[:, 32:64]
        nmx_l, sm_l, rc_l = ([st[:, o1 + 64 * l:o1 + 64 * l + 6] for l in range(2)] for o1 in (128, 136, 144))

        g = ctx.enter_context(nc.psum_tensor("g", [P, 4, NB], F32))
        m = ctx.enter_context(nc.psum_tensor("m", [P, 4, NB], F32))

        dram_bias = nc.dram_tensor("bias_rows", (24, P, S), F32, kind="Internal").ap()

        def sem(name):
            return ctx.enter_context(nc.semaphore(name))

        raw_full = [sem(f"raw_full{n}") for n in range(SLOTS)]
        hi_done, lo_done, unit_used = sem("hi_done"), sem("lo_done"), sem("unit_used")
        pair_free = [sem("pair_free0"), sem("pair_free1")]
        consts_in, masks_in, mem_in = sem("consts_in"), sem("masks_in"), sem("mem_in")
        tables_in, ident_in = sem("tables_in"), sem("ident_in")
        x_in = [sem(f"x_in{n}") for n in range(4)]
        ga_in, gb_in, bias_in = sem("ga_in"), sem("gb_in"), sem("bias_in")
        gains_in, gains_turned, gains_ready = sem("gains_in"), sem("gains_turned"), sem("gains_ready")
        chain_a, chain_d, chain_p = sem("act_step"), sem("dve_step"), sem("pool_step")
        tab_ready, bt_ready, bt_sb, bc_sb, bt_stored = (
            sem("tab_ready"), sem("bt_ready"), sem("bt_sb"), sem("bc_sb"), sem("bt_stored"))
        ss_done, var_done, sqrt_done, rstd_done = sem("ss_done"), sem("var_done"), sem("sqrt_done"), sem("rstd_done")
        turned, hi_evac, lo_evac = sem("turned"), sem("hi_evac"), sem("lo_evac")
        x_done, fin_done = sem("x_done"), sem("fin_done")
        out_done = sem("out_done")

        def spec(w, units, chunks):
            return {"w": w.rearrange("(k p) n -> p k n", p=P), "units": units, "chunks": chunks}

        gemms = {
            "in1f": spec(a["w_in"], 8, 2), "in1g": spec(a["w_in"], 8, 2), "in1q": spec(a["w_in"], 8, 4), "in1b": spec(a["w_in"], 8, 6),
            "ckv": spec(a["w_ckv"], 8, 2), "out1": spec(a["w_out"], 8, 4), "cq": spec(a["w_cq"], 8, 1), "co": spec(a["w_co"], 2, 4),
            "ff1": spec(a["w_ffn_in"], 8, 22), "fo1": spec(a["w_ffn_out"], 22, 4),
            "in2c": spec(a["nsa_w_in_2"], 8, 2), "in2k": spec(a["nsa_w_in_2"], 8, 4), "cmp": {"units": 20, "chunks": 0},
            "in2q": spec(a["nsa_w_in_2"], 8, 1), "in2r": spec(a["nsa_w_in_2"], 8, 3),
            "out2": spec(a["nsa_w_out_2"], 8, 4),
            "ff2": spec(a["ffn_w_in_2"], 8, 22), "fo2": spec(a["ffn_w_out_2"], 22, 4),
        }
        at_unit, at_pair = 0, [0, 0]
        for name, s in gemms.items():
            s["u0"], s["pair0"] = at_unit, list(at_pair)
            if name == "cmp":
                at_unit += 20
                at_pair = [at_pair[0] + 1, at_pair[1] + 1]
            elif name == "in2r":
                at_unit += 24
                at_pair = [at_pair[0] + 3, at_pair[1]]
            else:
                at_unit += s["units"] * s["chunks"]
                at_pair = [at_pair[0] + (s["chunks"] + 1) // 2, at_pair[1] + s["chunks"] // 2]
            assert at_unit % SLOTS == 0

        def bodies(eng, s, body, step=2):
            n = s["chunks"]
            body(0, min(2, n), True)
            if n > 4:
                with eng.Fori(1, n // 2) as i:
                    body(i, 2, False)
            elif n == 4:
                body(1, 2, False)

        def sp_unit(sp, cyc, j, src, n=UE, shape=2):
            sp.wait_ge(lo_done, (cyc + j // SLOTS) * SLOTS + j % SLOTS + 1)
            sp.dma_start(raw[:, j % SLOTS, 0:n].rearrange("p (k n) -> p k n", k=shape), src)\
              .then_inc(raw_full[j % SLOTS], 16)

        def act_unit(act, cyc, j, n=UE):
            act.wait_ge(raw_full[j % SLOTS], (cyc + j // SLOTS) * 16 + 16)
            act.wait_ge(unit_used, (cyc + j // SLOTS) * SLOTS + j % SLOTS + 1)
            nc.scalar.activation(wh[:, j % SLOTS, 0:n], raw[:, j % SLOTS, 0:n], ACT.Copy).then_inc(hi_done, 1)

        def dve_unit(dve, cyc, j, n=UE):
            dve.wait_ge(hi_done, (cyc + j // SLOTS) * SLOTS + j % SLOTS + 1)
            nc.vector.tensor_tensor(wl[:, j % SLOTS, 0:n], raw[:, j % SLOTS, 0:n],
                                    wh[:, j % SLOTS, 0:n].bitcast(F32), ALU.subtract).then_inc(lo_done, 1)

        def pe_unit(pe, cyc, j, pair, hi, lo, k0, first, last):
            pe.wait_ge(lo_done, SLOTS + (cyc + j // SLOTS) * SLOTS + j % SLOTS + 1)
            for k in range(2):
                whk = wh[:, j % SLOTS, k * NB:(k + 1) * NB]
                wlk = wl[:, j % SLOTS, k * NB:(k + 1) * NB]
                for t in range(T):
                    dst = g[:, 2 * pair + t, :]
                    h = hi[:, k0 + k, t * P:(t + 1) * P]
                    l = lo[:, k0 + k, t * P:(t + 1) * P]
                    nc.tensor.matmul(dst, h, whk, start=(first and k == 0), stop=False)
                    nc.tensor.matmul(dst, h, wlk, start=False, stop=False)
                    ins = nc.tensor.matmul(dst, l, whk, start=False, stop=(last and k == 1))
            ins.then_inc(unit_used, 1)

        def used(s, chunk):
            return SLOTS + s["u0"] + s["units"] * (chunk + 1)

        def cyc_of(s, i):
            return s["u0"] // SLOTS + i * (2 * s["units"] // SLOTS)

        def sp_gemm(sp, name, col=lambda c: c * NB):
            s = gemms[name]

            def body(i, chunks, first):
                for j in range(chunks * s["units"]):
                    c, u = 2 * i + j // s["units"], j % s["units"]
                    sp_unit(sp, cyc_of(s, i), j, s["w"][:, 2 * u:2 * u + 2, bass.ds(col(c), NB)])
            bodies(sp, s, body)

        def act_gemm(act, name, evac, turn=None, held=None, hold=False, also={}, done=0):
            s = gemms[name]
            late = min(3, s["units"] - 1)

            def body(i, chunks, first):
                for j in range(chunks * s["units"]):
                    if not (first and j < done):
                        act_unit(act, cyc_of(s, i), j)
                    if first and turn:
                        act_lead_in(act, turn, j)
                    if first and held and j == late:
                        held()
                    if first and j in also:
                        also[j]()
                    if j == late and not first:
                        evac(i, -1)
                    if j == s["units"] + late:
                        evac(i, 0)
                if first and turn:
                    act_lead_in_rest(act, turn, chunks * s["units"])
            bodies(act, s, body)
            n = s["chunks"]
            if not hold:
                evac(*((n // 2, -1) if n > 1 else (0, 0)))

        AHEAD = 3

        def ahead(unit, eng, name, n=AHEAD):
            for j in range(n):
                unit(eng, gemms[name]["u0"] // SLOTS, j)

        def act_copy_out(act, name, dst, norm=None):
            s = gemms[name]

            def evac(i, c):
                chunk = 2 * i + c
                act.wait_ge(unit_used, used(s, chunk))
                if norm is None:
                    nc.scalar.activation(dst(chunk), g[:, 2 * (c % 2):2 * (c % 2) + 2, :], ACT.Copy)\
                      .then_inc(pair_free[c % 2], 1)
                    return
                act.wait_ge(rstd_done, NORM[norm] + 1)
                for t in range(T):
                    ins = nc.scalar.activation(dst(chunk)[:, t, :], g[:, 2 * (c % 2) + t, :], ACT.Copy,
                                               scale=rstd(norm)[:, t:t + 1])
                ins.then_inc(pair_free[c % 2], 1)
            return evac

        def act_squares_out(act, name, post, junk):
            s = gemms[name]

            def evac(i, c):
                chunk = 2 * i + c
                act.wait_ge(unit_used, used(s, chunk))
                for t in range(T):
                    nc.scalar.activation(junk[:, c % 2, t, :], g[:, 2 * (c % 2) + t, :], ACT.Square,
                                         accum_out=ss8[:, t, bass.ds(chunk, 1)]).then_inc(ss_done, 1)
            return evac

        def act_squares_x(act, name, junk):
            s = gemms[name]

            def evac(i, c):
                chunk = 2 * i + c
                act.wait_ge(pair_free[c % 2], s["pair0"][c % 2] + i + (2 if c >= 0 else 1))
                for t in range(T):
                    nc.scalar.activation(junk[:, c % 2, t, :], x[:, t, bass.ds(chunk * NB, NB)], ACT.Square,
                                         accum_out=ss8[:, t, bass.ds(chunk, 1)]).then_inc(ss_done, 1)
            return evac

        def dve_gemm(dve, name, evac=None, turn=None, also={}, done=0):
            s = gemms[name]
            late = min(3, s["units"] - 1)

            def body(i, chunks, first):
                if first and turn:
                    dve_add_block(dve, turn, 0)
                for j in range(chunks * s["units"]):
                    if not (first and j < done):
                        dve_unit(dve, cyc_of(s, i), j)
                    if first and turn:
                        dve_lead_in(dve, turn, j)
                    if first and j in also:
                        also[j]()
                    if evac and j == late and not first:
                        evac(i, -1)
                    if evac and j == s["units"] + late:
                        evac(i, 0)
                if first and turn:
                    dve_lead_in_rest(dve, turn, chunks * s["units"])
            bodies(dve, s, body)
            if evac:
                evac(s["chunks"] // 2, -1, True)

        def dve_scale_out(dve, name, post, y, gains):
            s = gemms[name]

            def evac(i, c, last=False):
                chunk = 2 * i + c
                dve.wait_ge(ss_done, SS[post] + T * chunk + T)
                if last:
                    link_d(dve, nc.vector.tensor_reduce(ss_y, ss8, X, ALU.add))
                    nc.vector.tensor_scalar(ss_y, ss_y, 1.0 / D, EPS, ALU.mult, ALU.add).then_inc(var_done, 1)
                dve.wait_ge(gb_in, 16 * gains)
                nc.vector.tensor_tensor(y[:, bass.ds(2 * chunk, 2), :, :],
                                        g[:, 2 * (c % 2):2 * (c % 2) + 2, :].rearrange("p t (b n) -> p b t n", b=2),
                                        g_b[:, bass.ds(chunk * NB, NB)].rearrange("p (b o n) -> p b o n", b=2, o=1)
                                        .broadcast_to([P, 2, T, HB]), ALU.mult).then_inc(pair_free[c % 2], 1)
                if last:
                    dve_rstd(dve, post)
                    dve.wait_ge(pair_free[0], s["pair0"][0] + s["chunks"] // 2 + 1)
                    dve.wait_ge(pair_free[1], s["pair0"][1] + s["chunks"] // 2 + 1)
            return evac

        def dve_add_out(dve, name):
            s = gemms[name]

            def evac(i, c, last=False):
                chunk = 2 * i + c
                dve.wait_ge(unit_used, used(s, chunk))
                xc = x[:, :, bass.ds(chunk * NB, NB)]
                nc.vector.tensor_tensor(xc, g[:, 2 * (c % 2):2 * (c % 2) + 2, :], xc, ALU.add).then_inc(pair_free[c % 2], 1)
            return evac

        def pe_gemm(pe, name, hi=None, lo=None, turn=None, also={}):
            s = gemms[name]
            hi, lo = (act_hi, act_lo) if hi is None else (hi, lo)

            def body(i, chunks, first):
                for j in range(chunks * s["units"]):
                    c, u = j // s["units"], j % s["units"]
                    if u == 0:
                        pe.wait_ge(pair_free[c], s["pair0"][c] + i + 1)
                    if first and turn:
                        pe_lead_in(pe, turn, j)
                    if first and j in also:
                        also[j]()
                    pe_unit(pe, cyc_of(s, i), j, c, hi, lo, 2 * u, u == 0, u == s["units"] - 1)
            bodies(pe, s, body)

        CONSTS = 16 * 7
        NORM, SS = {}, {}
        at_ss = 0
        for n, parts in (("n1", 2), ("nmem", 2), ("post1", 8), ("ncx", 2), ("postcx", 8), ("nff", 2), ("postff", 8),
                         ("n2", 2), ("nff2", 2), ("nfin", 8)):
            NORM[n], SS[n] = len(NORM), at_ss
            at_ss += parts
        BANKS = {}
        bank_at = 0
        for n, banks in (("n1", 8), ("nmem", 8), ("mix1", 8), ("ncx", 8), ("cx", 2), ("nff", 8), ("ff1", 2 * PAIRS),
                         ("n2", 8), ("mix2", 8), ("nff2", 8), ("ff2", 2 * PAIRS)):
            BANKS[n] = bank_at
            bank_at += banks
        GAIN = {"n1": 0, "nmem": 1, "ncx": 2, "nff": 3, "n2": 4, "nff2": 5}
        ADDED = {"ncx": ("post1", 0, y_r), "nff": ("postcx", 16, y_r), "n2": ("postff", 32, y_a)}

        def rstd(name):
            return st[:, 72 + 2 * NORM[name]:74 + 2 * NORM[name]]

        def act_squares(act, name, src, junk):
            for t in range(T):
                nc.scalar.activation(junk[t], src[:, t, :], ACT.Square, accum_out=ss[:, t:t + 1]).then_inc(ss_done, 1)

        def act_sqrt(act, name, sums=ss):
            act.wait_ge(var_done, NORM[name] + 1)
            nc.scalar.activation(rstd(name), sums, ACT.Sqrt).then_inc(sqrt_done, 1)

        def dve_var(dve, name):
            dve.wait_ge(ss_done, SS[name] + 2)
            nc.vector.tensor_scalar(ss, ss, 1.0 / D, EPS, ALU.mult, ALU.add).then_inc(var_done, 1)

        def dve_rstd(dve, name):
            dve.wait_ge(sqrt_done, NORM[name] + 1)
            nc.vector.reciprocal(rstd(name), rstd(name)).then_inc(rstd_done, 1)
            dve.wait_ge(rstd_done, NORM[name] + 1)

        def dve_add_block(dve, name, b):
            if name in ADDED:
                post, _, y = ADDED[name]
                for t in range(T):
                    xb = x[:, t, b * HB:(b + 1) * HB]
                    nc.vector.scalar_tensor_tensor(out=xb, in0=y[:, b, t, :], scalar=rstd(post)[:, t:t + 1], in1=xb,
                                                   op0=ALU.mult, op1=ALU.add).then_inc(x_done, 1)

        def pe_lead_in(pe, name, j):
            n = TURNS[name][0]
            if j == 0:
                pe_turn_bank(pe, name, 0)
            if j + 1 < n:
                pe_turn_bank(pe, name, j + 1)
            if j < n:
                pe.wait_ge(lo_evac, BANKS[name] + j + 1)

        def act_lead_in(act, name, j):
            n = TURNS[name][0]
            if j < n:
                act_turn_bank(act, name, j)
            if name in GAIN:
                if j == n - 1:
                    if name in ADDED:
                        act.wait_ge(x_done, ADDED[name][1] + 16)
                    act_squares(act, name, x, [junk_x[:, 0, :], junk_x[:, 1, :]])
                if j == n + 2:
                    act_sqrt(act, name)

        def act_lead_in_rest(act, name, units):
            if name in GAIN and units < TURNS[name][0] + 3:
                act_sqrt(act, name)

        def dve_lead_in(dve, name, j):
            n = TURNS[name][0]
            if j + 1 < n:
                dve_add_block(dve, name, j + 1)
            if j < n:
                dve_turn_bank(dve, name, j)
            if name in GAIN and j == n + 1:
                dve_var(dve, name)
            if name in GAIN and j == n + 2:
                dve_rstd(dve, name)

        def dve_lead_in_rest(dve, name, units):
            if name in GAIN and units < TURNS[name][0] + 3:
                dve_var(dve, name)
                dve_rstd(dve, name)

        def pe_turn_bank(pe, name, b):
            n, src, ready = TURNS[name]
            bank = BANKS[name] + b
            ready(pe, b)
            if bank >= 4:
                pe.wait_ge(lo_evac, bank - 3)
            for k in range(2):
                for t in range(T):
                    ins = nc.tensor.transpose(m[:, bank % 4, (2 * k + t) * P:(2 * k + t + 1) * P], src(2 * b + k, t),
                                              ident[:, :])
            ins.then_inc(turned, 1)

        def act_turn_bank(act, name, b):
            bank = BANKS[name] + b
            act.wait_ge(turned, bank + 1)
            src = m[:, bank % 4, :].rearrange("p (k n) -> p k n", k=2)
            if name not in GAIN:
                nc.scalar.activation(act_hi[:, 2 * b:2 * b + 2, :], src, ACT.Copy).then_inc(hi_evac, 1)
                return
            act.wait_ge(gains_ready, 1)
            for k in range(2):
                gk = g_cols[:, 16 * GAIN[name] + 2 * b + k:16 * GAIN[name] + 2 * b + k + 1]
                ins = nc.scalar.activation(act_hi[:, 2 * b + k, :], src[:, k, :], ACT.Copy, scale=gk)
            ins.then_inc(hi_evac, 1)

        def dve_turn_bank(dve, name, b):
            bank = BANKS[name] + b
            dve.wait_ge(hi_evac, bank + 1)
            src = m[:, bank % 4, :].rearrange("p (k n) -> p k n", k=2)
            hi = act_hi[:, 2 * b:2 * b + 2, :].bitcast(F32)
            if name not in GAIN:
                nc.vector.tensor_tensor(act_lo[:, 2 * b:2 * b + 2, :], src, hi, ALU.subtract).then_inc(lo_evac, 1)
                return
            for k in range(2):
                gk = g_cols[:, 16 * GAIN[name] + 2 * b + k:16 * GAIN[name] + 2 * b + k + 1]
                ins = nc.vector.scalar_tensor_tensor(out=act_lo[:, 2 * b + k, :], in0=src[:, k, :], scalar=gk,
                                                     in1=hi[:, k, :], op0=ALU.mult, op1=ALU.subtract)
            ins.then_inc(lo_evac, 1)

        def x_rows(k, t):
            return x[:, t, k * P:(k + 1) * P]

        def after_add(name):
            return lambda pe, b: pe.wait_ge(x_done, ADDED[name][1] + 2 * b + 2)

        def after_out2(pe, b):
            c, s = b // 2, gemms["out2"]
            pe.wait_ge(pair_free[c % 2], s["pair0"][c % 2] + c // 2 + 2)

        TURNS = {
            "n1": (8, x_rows, lambda pe, b: pe.wait_ge(x_in[b // 2], 16)),
            "nmem": (8, lambda k, t: memx[:, t, k * P:(k + 1) * P], lambda pe, b: pe.wait_ge(mem_in, 16)),
            "mix1": (8, lambda k, t: mixed_rows(k, t), lambda pe, b: pe.wait_ge(mix_done, 2 if b < 4 else 4)),
            "ncx": (8, x_rows, after_add("ncx")),
            "cx": (2, lambda k, t: qx[:, t, k * P:(k + 1) * P], lambda pe, b: pe.wait_ge(cx_kept, CX_H + 1)),
            "nff": (8, x_rows, after_add("nff")),
            "n2": (8, x_rows, after_add("n2")),
            "mix2": (8, lambda k, t: p2[:, t, k * P:(k + 1) * P],
                     lambda pe, b: [pe.wait_ge(n_kept[l], N_H // 2 + 1) for l in LANES]),
            "nff2": (8, x_rows, after_out2),
        }

        count = {"a": 0, "d": 0}

        def turned_in(pe, name, n=8):
            pe.wait_ge(lo_evac, BANKS[name] + n)

        def link_d(dve, ins):
            count["d"] += 1
            ins.then_inc(chain_d, 1)
            dve.wait_ge(chain_d, count["d"])

        def link_a(act, ins):
            count["a"] += 1
            ins.then_inc(chain_a, 1)
            act.wait_ge(chain_a, count["a"])


        def sp_gemm_cols(sp, name):
            s = gemms[name]

            def body(i, chunks, first):
                for j in range(16):
                    u = j % 8
                    sp_unit(sp, cyc_of(s, i), j, s["w"][:, 2 * u:2 * u + 2, bass.ds(i * NB + (j // 8) * FH, NB)])
            bodies(sp, s, body)

        def pe_ff_turn(pe, name, i):
            b0 = BANKS[name]
            pe.wait_ge(pair_free[1], gemms[name]["pair0"][1] + i + 2)
            for b in range(2):
                pe.wait_ge(lo_evac, b0 + 2 * i + b - 1)
                for k in range(2):
                    for t in range(T):
                        ins = nc.tensor.transpose(m[:, b, (2 * k + t) * P:(2 * k + t + 1) * P],
                                                  ff_h[:, t, (2 * b + k) * P:(2 * b + k + 1) * P], ident[:, :])
                ins.then_inc(turned, 1)

        def act_ff_turn(act, name, i):
            b0 = BANKS[name]
            for b in range(2):
                act.wait_ge(turned, b0 + 2 * i + b + 1)
                nc.scalar.activation(ht_hi[:, bass.ds(4 * i + 2 * b, 2), :], m[:, b, :]
                                     .rearrange("p (k n) -> p k n", k=2), ACT.Copy).then_inc(hi_evac, 1)

        def dve_ff_turn(dve, name, i):
            b0 = BANKS[name]
            for b in range(2):
                dve.wait_ge(hi_evac, b0 + 2 * i + b + 1)
                nc.vector.tensor_tensor(ht_lo[:, bass.ds(4 * i + 2 * b, 2), :], m[:, b, :]
                                        .rearrange("p (k n) -> p k n", k=2),
                                        ht_hi[:, bass.ds(4 * i + 2 * b, 2), :].bitcast(F32), ALU.subtract)\
                  .then_inc(lo_evac, 1)

        def pe_ffn_in(pe, name, turn):
            s = gemms[name]

            def body(i, chunks, first):
                for j in range(16):
                    c, u = j // 8, j % 8
                    if u == 0:
                        pe.wait_ge(pair_free[c], s["pair0"][c] + i + 1)
                    if first:
                        pe_lead_in(pe, turn, j)
                    if j == 8 and not first:
                        pe_ff_turn(pe, name, i - 1)
                    pe_unit(pe, cyc_of(s, i), j, c, act_hi, act_lo, 2 * u, u == 0, u == 7)
            bodies(pe, s, body)
            pe_ff_turn(pe, name, PAIRS - 1)

        def act_ffn_in(act, name, turn):
            s = gemms[name]

            def body(i, chunks, first):
                for j in range(16):
                    act_unit(act, cyc_of(s, i), j)
                    if first:
                        act_lead_in(act, turn, j)
                    if j == 11:
                        if not first:
                            act_ff_turn(act, name, i - 1)
                            act.wait_ge(pair_free[1], s["pair0"][1] + i + 1)
                        act.wait_ge(unit_used, s["u0"] + SLOTS + 16 * i + 8)
                        act.wait_ge(rstd_done, NORM[turn] + 1)
                        for t in range(T):
                            ins = nc.scalar.activation(ff_s[:, t, :], g[:, t, :], ACT.Silu, scale=rstd(turn)[:, t:t + 1])
                        ins.then_inc(pair_free[0], 1)
            bodies(act, s, body)
            act_ff_turn(act, name, PAIRS - 1)

        def dve_ffn_in(dve, name, turn):
            s = gemms[name]

            def mul(i):
                dve.wait_ge(pair_free[0], s["pair0"][0] + i + 2)
                dve.wait_ge(unit_used, s["u0"] + SLOTS + 16 * i + 16)
                for t in range(T):
                    ins = nc.vector.scalar_tensor_tensor(out=ff_h[:, t, :], in0=g[:, 2 + t, :], scalar=rstd(turn)[:, t:t + 1],
                                                         in1=ff_s[:, t, :], op0=ALU.mult, op1=ALU.mult)
                ins.then_inc(pair_free[1], 1)

            def body(i, chunks, first):
                if first:
                    dve_add_block(dve, turn, 0)
                for j in range(16):
                    dve_unit(dve, cyc_of(s, i), j)
                    if first:
                        dve_lead_in(dve, turn, j)
                    if j == 3 and not first:
                        mul(i - 1)
                    if j == 11 and not first:
                        dve_ff_turn(dve, name, i - 1)
            bodies(dve, s, body)
            mul(PAIRS - 1)
            dve_ff_turn(dve, name, PAIRS - 1)

        hg_gates, hg_bulk = sem("hg_gates"), sem("hg_bulk")
        hg_staged, hg_turned, hg_copied, hg_diffed = sem("hg_staged"), sem("hg_turned"), sem("hg_copied"), sem("hg_diffed")
        hg_decayed, hg_weighted, hg_scored, hg_masked = sem("hg_decayed"), sem("hg_weighted"), sem("hg_scored"), sem("hg_masked")
        hg_summed, hg_far, hg_out, hg_kept = sem("hg_summed"), sem("hg_far"), sem("hg_out"), sem("hg_kept")
        f_all, g_all = p1[:, :, F_HG:F_HG + 1024], p1[:, :, G_HG:G_HG + 1024]

        def act_gates(act):
            def on_f(t, func, out=kk, src=None, done=False, **kw):
                def step():
                    ins = nc.scalar.activation(out[:, t, :], kk[:, t, :] if src is None else src[:, t, :], func, **kw)
                    ins.then_inc(hg_gates, 1) if done else link_a(act, ins)
                return step

            def first_abs():
                act.wait_ge(pair_free[1], gemms["in1f"]["pair0"][1] + 2)
                on_f(0, ACT.Abs, src=f_all)()

            def mem_squares(t, junk):
                return lambda: nc.scalar.activation(junk[:, :], memx[:, t, :], ACT.Square, accum_out=ss[:, t:t + 1])\
                    .then_inc(ss_done, 1)

            def mem_squares_first():
                act.wait_ge(mem_in, 16)
                mem_squares(0, junk_m0)()

            def after_bulk(t):
                def step():
                    act.wait_ge(hg_bulk, t + 1)
                    on_f(t, ACT.Exp, src=f_all, done=True)()
                return step

            def silu(t):
                def step():
                    act.wait_ge(pair_free[1], gemms["in1g"]["pair0"][1] + 2)
                    nc.scalar.activation(g_all[:, t, :], g_all[:, t, :], ACT.Silu).then_inc(hg_gates, 1)
                return step

            with_g = {4: first_abs, 5: on_f(1, ACT.Abs, src=f_all), 6: on_f(0, ACT.Exp, scale=-1.0),
                      7: on_f(1, ACT.Exp, scale=-1.0), 8: on_f(0, ACT.Ln, bias=1.0, done=True),
                      9: on_f(1, ACT.Ln, bias=1.0, done=True), 12: mem_squares_first, 13: mem_squares(1, junk_m1)}
            with_q = {1: lambda: act_sqrt(act, "nmem"), 4: after_bulk(0), 5: after_bulk(1), 6: silu(0), 7: silu(1)}
            return with_g, with_q

        def dve_gates(dve):
            def log_f(t):
                def step():
                    dve.wait_ge(hg_gates, t + 1)
                    nc.vector.scalar_tensor_tensor(out=f_all[:, t, :], in0=f_all[:, t, :], scalar=0.0, in1=kk[:, t, :],
                                                   op0=ALU.min, op1=ALU.subtract).then_inc(hg_bulk, 1)
                return step

            def one_less_f(t):
                def step():
                    dve.wait_ge(hg_gates, 3 + t)
                    nc.vector.tensor_scalar(kk[:, t, :], kk[:, t, :], -1.0, 1.0, ALU.mult, ALU.add).then_inc(hg_bulk, 1)
                return step

            def gain(t):
                def step():
                    dve.wait_ge(hg_gates, 5 + t)
                    dve.wait_ge(consts_in, CONSTS)
                    link_d(dve, nc.vector.tensor_tensor(
                        p1[:, t, G_HG:G_HG + 1024].rearrange("p (h d) -> p h d", d=HG_D),
                        p1[:, t, G_HG:G_HG + 1024].rearrange("p (h d) -> p h d", d=HG_D),
                        on_g[:, :].rearrange("p (o d) -> p o d", o=1).broadcast_to([P, HG_H, HG_D]), ALU.mult))
                return step

            with_g = {10: log_f(0), 11: log_f(1)}
            with_q = {0: lambda: dve_var(dve, "nmem"), 2: lambda: dve_rstd(dve, "nmem"), 5: one_less_f(0),
                      6: one_less_f(1), 7: gain(0), 8: gain(1)}
            return with_g, with_q

        def pool_hg(pool):
            pool.wait_ge(hg_bulk, 4)
            with pool.Fori(0, HG_H) as h:
                pool.wait_ge(hg_turned, h + 1)
                for dst, src, col in ((lf_s, p1, F_HG), (q_s, p1, Q_HG), (k_s, kk, 0)):
                    nc.gpsimd.tensor_copy(dst[:, :, :], src[:, :, bass.ds(h * HG_D + col, HG_D)]).then_inc(hg_staged, 1)

        def hg_heads(eng, head, turn):
            with eng.Fori(0, 3) as i:
                for c in range(2):
                    head(gemms["in1b"], 2 * i + c, i, c)
            for b in range(8):
                turn(eng, "nmem", b)
            for c in range(2):
                head(gemms["ckv"], 6 + c, 0, c)

        def pe_hg(pe):
            pe.wait_ge(consts_in, CONSTS)
            pe.sem_inc(hg_turned, 1)
            pe.sem_inc(hg_out, 1)

            def head(s, h, i, c):
                def units(first, n):
                    if first == 0:
                        pe.wait_ge(pair_free[c], s["pair0"][c] + i + 1)
                    for u in range(first, first + n):
                        pe_unit(pe, cyc_of(s, i), 8 * c + u, c, act_hi, act_lo, 2 * u, u == 0, u == 7)

                units(0, 1)
                pe.wait_ge(hg_staged, 3 * h + 3)
                pe.wait_ge(hg_kept, h + 1)
                for t in range(T):
                    nc.tensor.matmul(m[:, 0, t * P:(t + 1) * P], lf_s[:, t, :], cums[:, :], start=(t == 0), stop=(t == 1),
                                     skip_group_check=True)
                for t in range(T):
                    nc.tensor.transpose(m[:, 0, S + t * P:S + (t + 1) * P], q_s[:, t, :], ident[:, :])
                for t in range(T):
                    ins = nc.tensor.transpose(m[:, 1, t * P:(t + 1) * P], k_s[:, t, :], ident[:, :])
                ins.then_inc(hg_turned, 1)
                units(1, 5)
                pe.wait_ge(hg_weighted, h + 2)
                nc.tensor.matmul(m[:, 1, S:S + P], dec[:, 7, 0:P], dec[:, 7, P:S], start=True, stop=True)
                for t in range(T):
                    pe.wait_ge(hg_masked, 2 * h + t + 1)
                    for l in range(8):
                        lhs = dec[:, l, t * P:(t + 1) * P] if l < 7 else kt[:, t * P:(t + 1) * P]
                        rhs = dec[:, l, t * P:(t + 1) * P] if l < 7 else bq[:, S + t * P:S + (t + 1) * P]
                        ins = nc.tensor.matmul(m[:, 2 + l // 4, (l % 4) * P:(l % 4 + 1) * P], lhs, rhs,
                                               start=(l % 4 == 0), stop=(l % 4 == 3), skip_group_check=True)
                    ins.then_inc(hg_scored, 1)
                    units(6 + t, 1)
                pe.wait_ge(hg_summed, 2 * h + 3)
                pe.wait_ge(hg_far, h + 1)
                v = [p1[:, t, bass.ds(h * HG_D + I_HG, HG_D)] for t in range(T)]
                nc.tensor.matmul(m[:, 0, 0:P], at3[:, 0, :], v[0], start=True, stop=True)
                nc.tensor.matmul(m[:, 0, P:S], at3[:, 1, :], v[1], start=True, stop=False)
                nc.tensor.matmul(m[:, 0, P:S], at3[:, 2, :], v[0], start=False, stop=True).then_inc(hg_out, 1)

            def turn(pe, name, b):
                if b == 0:
                    pe.wait_ge(hg_kept, 7)
                    pe.wait_ge(hg_masked, 13)
                pe_turn_bank(pe, name, b)
                if b == 7:
                    turned_in(pe, name)

            hg_heads(pe, head, turn)

        def act_hg(act):
            act.sem_inc(hg_kept, 1)

            def head(s, h, i, c):
                def units(first, n):
                    for u in range(first, first + n):
                        act_unit(act, cyc_of(s, i), 8 * c + u)

                act.wait_ge(hg_turned, h + 2)
                act.wait_ge(hg_weighted, h + 1)
                nc.scalar.activation(bq[:, :], m[:, 0, :], ACT.Copy).then_inc(hg_copied, 1)
                nc.scalar.activation(kt[:, :], m[:, 1, 0:S], ACT.Copy).then_inc(hg_copied, 1)
                units(4, 2)
                act.wait_ge(hg_diffed, h + 1)
                nc.scalar.activation(dec[:, :, :], dec[:, :, :], ACT.Exp).then_inc(hg_decayed, 1)
                units(6, 4)
                act.wait_ge(hg_scored, 2 * h + 1)
                act.wait_ge(hg_out, h + 1)
                nc.scalar.activation(at3[:, 2, :], m[:, 1, S:S + P], ACT.Copy).then_inc(hg_far, 1)
                units(10, 1)
                mem = s is gemms["ckv"]
                dst = p1[:, :, bass.ds((2 * i + c) * NB + (KV if mem else 0), NB)]
                act_copy_out(act, "ckv" if mem else "in1b", lambda chunk: dst, "nmem" if mem else "n1")(i, c)
                act.wait_ge(hg_out, h + 2)
                nc.scalar.activation(p1[:, :, bass.ds(h * HG_D + Q_HG, HG_D)],
                                     m[:, 0, 0:S].rearrange("p (t d) -> p t d", t=T), ACT.Copy).then_inc(hg_kept, 1)
                units(11, 1)

            hg_heads(act, head, act_turn_bank)

        def dve_hg(dve):
            dve.sem_inc(hg_weighted, 1)
            dve.sem_inc(hg_masked, 1)
            dve.sem_inc(hg_summed, 1)
            dve.wait_ge(masks_in, 16)
            b = bq[:, 0:S]
            c0 = count["d"]

            def head(s, h, i, c):
                def units(first, n):
                    for u in range(first, first + n):
                        dve_unit(dve, cyc_of(s, i), 8 * c + u)

                dve.wait_ge(hg_copied, 2 * h + 2)
                nc.vector.tensor_tensor(lam_d[:, 0:1], b[:, 63:64], b[:, 127:128], ALU.add).then_inc(chain_d, 1)
                for l in range(7):
                    w = 1 << l
                    bv = b.rearrange("p (n w) -> p n w", w=2 * w)
                    dv = dec[:, l, :].rearrange("p (n w) -> p n w", w=2 * w)
                    ref = bv[:, :, w - 1:w].broadcast_to([P, S // (2 * w), w])
                    nc.vector.tensor_tensor(dv[:, :, 0:w], ref, bv[:, :, 0:w], ALU.subtract)
                    if l < 6:
                        nc.vector.tensor_tensor(dv[:, :, w:2 * w], bv[:, :, w:2 * w], ref, ALU.subtract)
                    else:
                        nc.vector.tensor_copy(dv[:, :, w:2 * w], bv[:, :, w:2 * w])
                dve.wait_ge(chain_d, c0 + h + 1)
                nc.vector.tensor_scalar(dec[:, 7, 0:64], b[:, 0:64], -1.0, lam_d[:, 0:1], ALU.mult, ALU.add)
                nc.vector.tensor_scalar(dec[:, 7, 64:128], b[:, 64:128], -1.0, b[:, 127:128], ALU.mult, ALU.add)
                nc.vector.tensor_copy(dec[:, 7, 128:192], b[:, 128:192])
                nc.vector.tensor_scalar(dec[:, 7, 192:256], b[:, 192:256], b[:, 191:192], None, ALU.add)\
                  .then_inc(hg_diffed, 1)
                units(4, 1)
                dve.wait_ge(hg_decayed, h + 1)
                for l in range(8):
                    w = 1 << l
                    dv = dec[:, l, :].rearrange("p (n w) -> p n w", w=2 * w)
                    kv_ = kt[:, :].rearrange("p (n w) -> p n w", w=2 * w)
                    qv = bq[:, S:2 * S].rearrange("p (n w) -> p n w", w=2 * w)
                    nc.vector.tensor_tensor(dv[:, :, 0:w], dv[:, :, 0:w], kv_[:, :, 0:w], ALU.mult)
                    ins = nc.vector.tensor_tensor(dv[:, :, w:2 * w], dv[:, :, w:2 * w], qv[:, :, w:2 * w], ALU.mult)
                ins.then_inc(hg_weighted, 1)
                units(5, 3)
                dve.wait_ge(hg_out, h + 1)
                for t in range(T):
                    dve.wait_ge(hg_summed, 2 * h + t + 1)
                    dve.wait_ge(hg_scored, 2 * h + t + 1)
                    nc.vector.tensor_tensor(mp[:, :], m[:, 2:4, :].rearrange("p a n -> p (a n)"), masks[:, :], ALU.mult)\
                      .then_inc(hg_masked, 1)
                    if t == 0:
                        units(8, 1)
                    dve.wait_ge(hg_masked, 2 * h + t + 2)
                    nc.vector.tensor_reduce(at3[:, t, :], mp[:, :].rearrange("p (l s) -> p s l", l=8), X, ALU.add)\
                      .then_inc(hg_summed, 1)
                units(9, 3)

            hg_heads(dve, head, dve_turn_bank)
            count["d"] += HG_H

        LANES = range(2)
        banks = [m, g]

        def lane_sems(name):
            return [sem(f"{name}{l}") for l in LANES]

        da_staged, da_turned, da_copied, da_scored = (lane_sems(n) for n in ("da_staged", "da_turned", "da_copied", "da_scored"))
        da_max, da_exp, da_mixed, da_back = (lane_sems(n) for n in ("da_max", "da_exp", "da_mixed", "da_back"))
        da_at, da_out, da_kept = (lane_sems(n) for n in ("da_at", "da_out", "da_kept"))
        da_q, da_k, da_qk, da_sc, da_w = [q_s, q_s1], [k_s, k_s1], [bq, bq1], [sc_da, sc_da1], [at3, at31]
        lam_step = sem("lam_step")
        mix_sq, mix_var, mix_sqrt, mix_done = sem("mix_sq"), sem("mix_var"), sem("mix_sqrt"), sem("mix_done")

        def dve_lambda(dve):
            dve.wait_ge(consts_in, CONSTS)
            for n in range(2):
                link_d(dve, nc.vector.tensor_tensor(lam4[:, 2 * n, :], lam4[:, 2 * n, :], lam4[:, 2 * n + 1, :], ALU.mult))
                link_d(dve, nc.vector.tensor_reduce(st[:, 70 + n:71 + n], lam4[:, 2 * n, :], X, ALU.add))
            nc.vector.tensor_scalar(sub_g[:, :], sub_g[:, :], 1.0 - LAM_INIT, None, ALU.mult).then_inc(lam_step, 1)
            dve.wait_ge(lam_step, 2)
            link_d(dve, nc.vector.tensor_tensor(neg_lam, st[:, 71:72], st[:, 70:71], ALU.subtract))
            link_d(dve, nc.vector.tensor_scalar(neg_lam, neg_lam, -LAM_INIT, None, ALU.add))

        def act_lambda(act):
            act.wait_ge(lam_step, 1)
            nc.scalar.activation(st[:, 70:72], st[:, 70:72], ACT.Exp).then_inc(lam_step, 1)

        def pool_da(pool):
            pool.wait_ge(hg_kept, HG_H + 1)
            pool.wait_ge(pair_free[1], gemms["in1b"]["pair0"][1] + 4)
            with pool.Fori(0, DA_H // 2) as i:
                for l in LANES:
                    pool.wait_ge(da_turned[l], i + 1)
                    for dst, col in ((da_q[l], Q_DA), (da_k[l], K_DA)):
                        nc.gpsimd.tensor_copy(dst[:, :, :], p1[:, :, bass.ds((2 * i + l) * P + col, P)])\
                          .then_inc(da_staged[l], 1)

        def pe_da(pe):
            pe.wait_ge(hg_kept, HG_H + 1)
            for l in LANES:
                pe.sem_inc(da_turned[l], 1)
            with pe.Fori(0, DA_H // 2) as i:
                for l in LANES:
                    pe.wait_ge(da_staged[l], 2 * i + 2)
                    pe.wait_ge(da_kept[l], i + 1)
                    for n, src in enumerate((da_q[l], da_k[l])):
                        for t in range(T):
                            ins = nc.tensor.transpose(banks[l][:, 0, (2 * n + t) * P:(2 * n + t + 1) * P], src[:, t, :],
                                                      ident[:, :])
                    ins.then_inc(da_turned[l], 1)
                for l in LANES:
                    pe.wait_ge(da_copied[l], i + 1)
                    for q0, keys in ((0, P), (P, S)):
                        for j in range(2):
                            r = slice(j * DA_D, (j + 1) * DA_D)
                            ins = nc.tensor.matmul(banks[l][:, 1 + j, q0:q0 + keys], da_qk[l][r, q0:q0 + P],
                                                   da_qk[l][r, S:S + keys], start=(q0 == 0), stop=(q0 != 0),
                                                   skip_group_check=True)
                    ins.then_inc(da_scored[l], 1)
                for l in LANES:
                    pe.wait_ge(da_mixed[l], 2 * i + 2)
                    for n, o1 in enumerate((0, S, S + P)):
                        ins = nc.tensor.transpose(banks[l][:, 3, n * P:(n + 1) * P], da_sc[l][:, o1:o1 + P], ident[:, :])
                    ins.then_inc(da_back[l], 1)
                for l in LANES:
                    pe.wait_ge(da_at[l], i + 1)
                    v = [p1[:, t, bass.ds((2 * i + l) * P + V_DA, P)] for t in range(T)]
                    nc.tensor.matmul(banks[l][:, 0, 0:P], da_w[l][:, 0, :], v[0], start=True, stop=True)
                    nc.tensor.matmul(banks[l][:, 0, P:S], da_w[l][:, 1, :], v[0], start=True, stop=False)
                    nc.tensor.matmul(banks[l][:, 0, P:S], da_w[l][:, 2, :], v[1], start=False, stop=True)\
                      .then_inc(da_out[l], 1)

        def act_da(act):
            for l in LANES:
                act.sem_inc(da_kept[l], 1)
            with act.Fori(0, DA_H // 2) as i:
                for l in LANES:
                    act.wait_ge(da_turned[l], i + 2)
                    nc.scalar.activation(da_qk[l][:, :], banks[l][:, 0, :], ACT.Copy).then_inc(da_copied[l], 1)
                for l in LANES:
                    act.wait_ge(da_max[l], 2 * i + 2)
                    for n, (o1, w) in enumerate(((0, P), (P, P), (S, S), (2 * S, S))):
                        nc.scalar.activation(da_sc[l][:, o1:o1 + w], da_sc[l][:, o1:o1 + w], ACT.Exp,
                                             bias=nmx_l[l][:, n:n + 1], accum_out=sm_l[l][:, n:n + 1])\
                          .then_inc(da_exp[l], 1)
                for l in LANES:
                    act.wait_ge(da_back[l], i + 1)
                    nc.scalar.activation(da_w[l][:, :, :], banks[l][:, 3, 0:3 * P].rearrange("p (a n) -> p a n", a=3), ACT.Copy)\
                      .then_inc(da_at[l], 1)
                for l in LANES:
                    act.wait_ge(da_out[l], i + 1)
                    nc.scalar.activation(p1[:, :, bass.ds((2 * i + l) * P, P)],
                                         banks[l][:, 0, 0:S].rearrange("p (t d) -> p t d", t=T), ACT.Copy)\
                      .then_inc(da_kept[l], 1)

        def dve_da(dve):
            dve.wait_ge(bias_in, 16)
            steps = count["d"]
            n_steps = 5 * 2

            def link(i, k, ins):
                ins.then_inc(chain_d, 1)
                dve.wait_ge(chain_d, steps + i * n_steps + k + 1)

            with dve.Fori(0, DA_H // 2) as i:
                for l in LANES:
                    dve.wait_ge(da_scored[l], i + 1)
                    bias = b_da[:, bass.ds(2 * i + l, 1), :]
                    s0 = da_sc[l][:, 0:S].rearrange("p (i n) -> p i n", i=2)
                    s1 = da_sc[l][:, S:3 * S].rearrange("p (i n) -> p i n", i=2)
                    nc.vector.scalar_tensor_tensor(out=s0, in0=banks[l][:, 1:3, 0:P], scalar=DA_D ** -0.5,
                                                   in1=bias[:, :, P:S].broadcast_to([P, 2, P]),
                                                   op0=ALU.mult, op1=ALU.add)
                    link(i, l, nc.vector.scalar_tensor_tensor(out=s1, in0=banks[l][:, 1:3, P:P + S], scalar=DA_D ** -0.5,
                                                              in1=bias.broadcast_to([P, 2, S]),
                                                              op0=ALU.mult, op1=ALU.add))
                    nc.vector.tensor_reduce(nmx_l[l][:, 0:2], s0, X, ALU.max, negate=True).then_inc(da_max[l], 1)
                    nc.vector.tensor_reduce(nmx_l[l][:, 2:4], s1, X, ALU.max, negate=True).then_inc(da_max[l], 1)
                for l in LANES:
                    rc_, sc_ = rc_l[l], da_sc[l]
                    dve.wait_ge(da_exp[l], 4 * i + 4)
                    link(i, 2 + 4 * l, nc.vector.reciprocal(rc_[:, 0:4], sm_l[l][:, 0:4]))
                    link(i, 3 + 4 * l, nc.vector.tensor_scalar(rc_[:, 1:4:2], rc_[:, 1:4:2], neg_lam, None, ALU.mult))
                    nc.vector.tensor_scalar(sc_[:, P:S], sc_[:, P:S], rc_[:, 1:2], None, ALU.mult).then_inc(chain_d, 1)
                    link(i, 5 + 4 * l, nc.vector.tensor_scalar(sc_[:, 2 * S:3 * S], sc_[:, 2 * S:3 * S], rc_[:, 3:4], None,
                                                               ALU.mult))
                    nc.vector.scalar_tensor_tensor(out=sc_[:, 0:P], in0=sc_[:, 0:P], scalar=rc_[:, 0:1], in1=sc_[:, P:S],
                                                   op0=ALU.mult, op1=ALU.add).then_inc(da_mixed[l], 1)
                    nc.vector.scalar_tensor_tensor(out=sc_[:, S:2 * S], in0=sc_[:, S:2 * S], scalar=rc_[:, 2:3],
                                                   in1=sc_[:, 2 * S:3 * S], op0=ALU.mult, op1=ALU.add)\
                      .then_inc(da_mixed[l], 1)
            count["d"] += DA_H // 2 * n_steps

        HALVES = ((Q_DA, K_DA), (Q_HG, I_HG))

        def act_mix_norm(act):
            for l in LANES:
                act.wait_ge(da_kept[l], DA_H // 2 + 1)
            act.wait_ge(hg_kept, HG_H + 1)
            for src, junk in HALVES:
                nc.scalar.activation(p1[:, :, junk:junk + 1024], p1[:, :, src:src + 1024], ACT.Square).then_inc(mix_sq, 1)
            act.wait_ge(mix_var, 1)
            nc.scalar.activation(ss16, ss16, ACT.Sqrt).then_inc(mix_sqrt, 1)

        def dve_mix_norm(dve):
            s3 = ss16.rearrange("p (n t h) -> p n t h", n=2, t=T)
            for n, (src, junk) in enumerate(HALVES):
                dve.wait_ge(mix_sq, n + 1)
                link_d(dve, nc.vector.tensor_reduce(
                    s3[:, n], p1[:, :, junk:junk + 1024].rearrange("p t (h d) -> p t h d", d=P), X, ALU.add))
            nc.vector.tensor_scalar(ss16, ss16, 1.0 / P, EPS, ALU.mult, ALU.add).then_inc(mix_var, 1)
            dve.wait_ge(mix_sqrt, 1)
            link_d(dve, nc.vector.reciprocal(ss16, ss16))
            for n, (src, junk) in enumerate(HALVES):
                for t in range(T):
                    rows = p1[:, t, src:src + 1024].rearrange("p (h d) -> p h d", d=P)
                    scale = s3[:, n, t, :].rearrange("p (h o) -> p h o", o=1).broadcast_to([P, 8, P])
                    gain = (p1[:, t, G_HG:G_HG + 1024].rearrange("p (h d) -> p h d", d=P) if n else
                            sub_g[:, :].rearrange("p (o d) -> p o d", o=1).broadcast_to([P, 8, P]))
                    link_d(dve, nc.vector.tensor_tensor(rows, rows, scale, ALU.mult))
                    nc.vector.tensor_tensor(rows, rows, gain, ALU.mult).then_inc(mix_done, 1)

        def mixed_rows(k, t):
            col = k * P if k < 8 else Q_HG + (k - 8) * P
            return p1[:, t, col:col + P]

        cx_staged, cx_turned, cx_copied, cx_scored = sem("cx_staged"), sem("cx_turned"), sem("cx_copied"), sem("cx_scored")
        cx_max, cx_exp, cx_soft, cx_back = sem("cx_max"), sem("cx_exp"), sem("cx_soft"), sem("cx_back")
        cx_pt, cx_out, cx_kept = sem("cx_pt"), sem("cx_out"), sem("cx_kept")
        CX_SCALE = P ** -0.5

        def pool_cx(pool):
            pool.wait_ge(pair_free[0], gemms["cq"]["pair0"][0] + 2)
            pool.wait_ge(pair_free[1], gemms["ckv"]["pair0"][1] + 2)
            with pool.Fori(0, CX_H) as h:
                pool.wait_ge(cx_turned, h + 1)
                nc.gpsimd.tensor_copy(xq_s[:, :, :], qx[:, :, bass.ds(h * P, P)]).then_inc(cx_staged, 1)
                nc.gpsimd.tensor_copy(xk_s[:, :, :], p1[:, :, bass.ds(h * P + KV, P)]).then_inc(cx_staged, 1)

        def pe_cx(pe):
            pe.sem_inc(cx_turned, 1)
            with pe.Fori(0, CX_H) as h:
                pe.wait_ge(cx_staged, 2 * h + 2)
                for n, src in enumerate((xq_s, xk_s)):
                    for t in range(T):
                        ins = nc.tensor.transpose(m[:, 0, (2 * n + t) * P:(2 * n + t + 1) * P], src[:, t, :], ident[:, :])
                ins.then_inc(cx_turned, 1)
                pe.wait_ge(cx_copied, h + 1)
                for t in range(T):
                    ins = nc.tensor.matmul(m[:, 1, t * S:(t + 1) * S], xqk[:, t * P:(t + 1) * P], xqk[:, S:2 * S],
                                           start=(t == 0), stop=(t == 1), skip_group_check=True)
                ins.then_inc(cx_scored, 1)
                pe.wait_ge(cx_soft, 2 * h + 2)
                for k in range(2):
                    for t in range(T):
                        ins = nc.tensor.transpose(m[:, 2, (2 * k + t) * P:(2 * k + t + 1) * P],
                                                  xp[:, t, k * P:(k + 1) * P], ident[:, :])
                ins.then_inc(cx_back, 1)
                pe.wait_ge(cx_pt, h + 1)
                pe.wait_ge(cx_kept, h + 1)
                for t in range(T):
                    for k in range(2):
                        ins = nc.tensor.matmul(m[:, 3, t * P:(t + 1) * P], xpt[:, 2 * k + t, :],
                                               p1[:, k, bass.ds(h * P + KV + CX_W, P)], start=(k == 0), stop=(k == 1))
                ins.then_inc(cx_out, 1)

        def act_cx(act):
            act.sem_inc(cx_kept, 1)
            with act.Fori(0, CX_H) as h:
                act.wait_ge(cx_turned, h + 2)
                nc.scalar.activation(xqk[:, :], m[:, 0, :], ACT.Copy).then_inc(cx_copied, 1)
                act.wait_ge(cx_max, h + 1)
                for t in range(T):
                    nc.scalar.activation(xp[:, t, :], m[:, 1, t * S:(t + 1) * S], ACT.Exp, bias=nmx[:, 2 + t:3 + t],
                                         scale=CX_SCALE, accum_out=sm[:, t:t + 1]).then_inc(cx_exp, 1)
                act.wait_ge(cx_back, h + 1)
                nc.scalar.activation(xpt[:, :, :], m[:, 2, :].rearrange("p (a n) -> p a n", a=4), ACT.Copy).then_inc(cx_pt, 1)
                act.wait_ge(cx_out, h + 1)
                nc.scalar.activation(qx[:, :, bass.ds(h * P, P)], m[:, 3, 0:S].rearrange("p (t d) -> p t d", t=T), ACT.Copy)\
                  .then_inc(cx_kept, 1)

        def dve_cx(dve):
            steps = count["d"]
            with dve.Fori(0, CX_H) as h:
                dve.wait_ge(cx_scored, h + 1)
                nc.vector.tensor_reduce(nmx[:, 0:2], m[:, 1, :].rearrange("p (t n) -> p t n", t=T), X, ALU.max, negate=True)\
                  .then_inc(chain_d, 1)
                dve.wait_ge(chain_d, steps + 2 * h + 1)
                nc.vector.tensor_scalar(nmx[:, 2:4], nmx[:, 0:2], CX_SCALE, None, ALU.mult).then_inc(cx_max, 1)
                dve.wait_ge(cx_exp, 2 * h + 2)
                nc.vector.reciprocal(rc[:, 0:2], sm[:, 0:2]).then_inc(chain_d, 1)
                dve.wait_ge(chain_d, steps + 2 * h + 2)
                for t in range(T):
                    nc.vector.tensor_scalar(xp[:, t, :], xp[:, t, :], rc[:, t:t + 1], None, ALU.mult).then_inc(cx_soft, 1)
            count["d"] += 2 * CX_H

        cp = gemms["cmp"]
        kc_turned, kc_copied, blk_sum, blk_split = sem("kc_turned"), sem("kc_copied"), sem("blk_sum"), sem("blk_split")
        cmp_in, gelu_step, gelu_act, g_turned, g_copied, cmp_out = (
            sem("cmp_in"), sem("gelu_step"), sem("gelu_act"), sem("g_turned"), sem("g_copied"), sem("cmp_out"))

        def sp_cmp(sp):
            cyc = cp["u0"] // SLOTS
            wg = gemms["in2k"]["w"]
            for j in range(4):
                sp_unit(sp, cyc, j, wg[:, 4 * j:4 * j + 4, GL:GL + 48], 4 * 48, 4)
            for b, w in enumerate((a["cmp_w1_k_2"], a["cmp_w1_v_2"])):
                wv = w.rearrange("(k p) n -> p k n", p=P)
                for j in range(8):
                    sp_unit(sp, cyc, 4 + 8 * b + j, wv[:, 4 * j:4 * j + 4, :], UE, 4)

        BLK_BANKS = ((1, 2), (3, 0))

        def pe_blocks(pe):
            def turn_pos():
                pe.wait_ge(cmp_in, 64)
                for b in range(2):
                    ins = nc.tensor.transpose(m[:, 0, b * CLEN:(b + 1) * CLEN], pos_s[:, b, :], ident[0:CLEN, 0:CLEN])
                ins.then_inc(kc_turned, 1)

            def turn(b):
                def step():
                    pe.wait_ge(pair_free[b], gemms["in2c"]["pair0"][b] + 2)
                    if b == 1:
                        pe.wait_ge(kc_copied, 1)
                    for n in range(N_G):
                        for t in range(T):
                            ins = nc.tensor.transpose(
                                m[:, BLK_BANKS[b][n // 2], (n % 2) * S + t * P:(n % 2) * S + (t + 1) * P],
                                p2[:, t, KC + b * 512 + n * P:KC + b * 512 + (n + 1) * P], ident[:, :])
                    ins.then_inc(kc_turned, 1)
                return step
            return {2: turn_pos, 4: turn(0), 7: turn(1)}

        def act_blocks(act):
            def copy_pos():
                act.wait_ge(kc_turned, 1)
                nc.scalar.activation(post[:, :, :], m[:, 0, 0:2 * CLEN].rearrange("p (b i) -> p b i", b=2), ACT.Copy)\
                  .then_inc(kc_copied, 1)

            def split(b):
                def step():
                    act.wait_ge(blk_sum, b + 1)
                    nc.scalar.activation(blk_hi[b][:, :, :], blk[:, :, :], ACT.Copy).then_inc(blk_split, 1)
                return step
            return {6: copy_pos, 9: split(0), 13: split(1)}

        def dve_blocks(dve):
            def build_blk(b):
                def step():
                    dve.wait_ge(kc_copied, 1)
                    dve.wait_ge(kc_turned, b + 2)
                    if b == 1:
                        dve.wait_ge(blk_split, 2)
                    for n in range(N_G):
                        src = m[:, BLK_BANKS[b][n // 2], (n % 2) * S:(n % 2 + 1) * S]
                        win = bass.AP(tensor=src.tensor, offset=src.offset, ap=[list(src.ap[0]), [1, CLEN], [CSTR, NC_]])
                        ins = nc.vector.tensor_tensor(blk[:, :, n * NC_:(n + 1) * NC_], win,
                                                      post[:, b, :].rearrange("p (i o) -> p i o", o=1)
                                                      .broadcast_to([P, CLEN, NC_]), ALU.add)
                    ins.then_inc(blk_sum, 1)
                return step

            def rest(b):
                def step():
                    dve.wait_ge(blk_split, 2 * b + 1)
                    nc.vector.tensor_tensor(blk_lo[b][:, :, :], blk[:, :, :], blk_hi[b][:, :, :].bitcast(F32), ALU.subtract)\
                      .then_inc(blk_split, 1)
                return step
            return {8: build_blk(0), 10: rest(0), 12: build_blk(1), 14: rest(1)}

        def pe_cmp(pe):
            pe.wait_ge(pair_free[0], cp["pair0"][0] + 1)
            for j in range(4):
                pe.wait_ge(lo_done, SLOTS + cp["u0"] + j + 1)
                for k in range(4):
                    for t in range(T):
                        h = act_hi[:, 4 * j + k, t * P:(t + 1) * P]
                        l = act_lo[:, 4 * j + k, t * P:(t + 1) * P]
                        whk, wlk = wh[:, j, k * 48:(k + 1) * 48], wl[:, j, k * 48:(k + 1) * 48]
                        dst = g[:, t, 0:48]
                        nc.tensor.matmul(dst, h, whk, start=(j == 0 and k == 0), stop=False)
                        nc.tensor.matmul(dst, h, wlk, start=False, stop=False)
                        ins = nc.tensor.matmul(dst, l, whk, start=False, stop=(j == 3 and k == 3))
                ins.then_inc(unit_used, 1)
            pe.wait_ge(pair_free[1], cp["pair0"][1] + 1)
            for b in range(2):
                pe.wait_ge(blk_split, 2 * b + 2)
                for j in range(8):
                    u = 4 + 8 * b + j
                    pe.wait_ge(lo_done, SLOTS + cp["u0"] + u + 1)
                    for k in range(4):
                        h, l = blk_hi[b][:, 4 * j + k, :], blk_lo[b][:, 4 * j + k, :]
                        whk = wh[:, u % SLOTS, k * CHID:(k + 1) * CHID]
                        wlk = wl[:, u % SLOTS, k * CHID:(k + 1) * CHID]
                        dst = g[0:GB, 2 + b, 0:CHID]
                        nc.tensor.matmul(dst, h, whk, start=(j == 0 and k == 0), stop=False)
                        nc.tensor.matmul(dst, h, wlk, start=False, stop=False)
                        ins = nc.tensor.matmul(dst, l, whk, start=False, stop=(j == 7 and k == 3))
                    ins.then_inc(unit_used, 1)

        def act_cmp(act, held):
            for j in range(20):
                act_unit(act, cp["u0"] // SLOTS, j, 192 if j < 4 else UE)
                if j == 3:
                    held()
                if j == 7:
                    act.wait_ge(unit_used, SLOTS + cp["u0"] + 4)
                    for t in range(T):
                        ins = nc.scalar.activation(gate[:, t, :], g[:, t, 0:48], ACT.Sigmoid, scale=rstd("n2")[:, t:t + 1])
                    ins.then_inc(pair_free[0], 1)

        def dve_cmp(dve):
            for j in range(20):
                dve_unit(dve, cp["u0"] // SLOTS, j, 192 if j < 4 else UE)

        gx, gt, gr = gh[:, 2, :, :], gh[:, 1, :, :], gh[:, 0, :, :]
        hidden = g[0:GB, 2:4, 0:CHID]

        def pe_hidden(pe):
            def turn():
                pe.wait_ge(gelu_step, 3)
                for b in range(2):
                    for k in range(2):
                        ins = nc.tensor.transpose(m[:, 3, (2 * b + k) * GB:(2 * b + k + 1) * GB],
                                                  gh[:, 0, b, k * P:(k + 1) * P], ident[0:GB, 0:GB])
                ins.then_inc(g_turned, 1)

            def product():
                pe.wait_ge(g_copied, 1)
                for k in range(2):
                    nc.tensor.matmul(m[:, 2, 0:GB], w2[:, 0, k, :], ght[:, 0, k, :], start=(k == 0), stop=(k == 1))
                for n in range(N_G):
                    for k in range(2):
                        ins = nc.tensor.matmul(m[0:NC_, 1, n * P:(n + 1) * P], ght[:, 1, k, n * NC_:(n + 1) * NC_],
                                               w2[:, 1, k, :], start=(k == 0), stop=(k == 1))
                ins.then_inc(cmp_out, 1)
            return {3: turn, 5: product}

        def act_hidden(act):
            def square():
                act.wait_ge(unit_used, SLOTS + cp["u0"] + 20)
                nc.scalar.activation(gt, hidden, ACT.Square).then_inc(gelu_act, 1)

            def tanh():
                act.wait_ge(gelu_step, 2)
                nc.scalar.activation(gt, gt, ACT.Tanh, scale=0.7978845608028654).then_inc(gelu_act, 1)

            def copy():
                act.wait_ge(g_turned, 1)
                nc.scalar.activation(ght[:, :, :, :], m[:, 3, 0:4 * GB].rearrange("p (b k n) -> p b k n", b=2, k=2), ACT.Copy)\
                  .then_inc(g_copied, 1)
            return {3: square, 4: tanh, 6: copy}

        def act_compressed(act):
            act.wait_ge(cmp_out, 1)
            nc.scalar.activation(kcc[:, :], m[:, 2, 0:GB], ACT.Copy).then_inc(kc_copied, 1)
            nc.scalar.activation(vcc[:, :], m[0:NC_, 1, :], ACT.Copy).then_inc(kc_copied, 1)

        def dve_hidden(dve):
            def cubic():
                dve.wait_ge(gelu_act, 1)
                nc.vector.tensor_copy(gx, hidden).then_inc(pair_free[1], 1)
                link_d(dve, nc.vector.tensor_scalar(gt, gt, 0.044715, 1.0, ALU.mult, ALU.add))
                dve.wait_ge(pair_free[1], cp["pair0"][1] + 2)
                nc.vector.tensor_tensor(gt, gt, gx, ALU.mult).then_inc(gelu_step, 2)

            def gelu():
                dve.wait_ge(gelu_act, 2)
                link_d(dve, nc.vector.scalar_tensor_tensor(out=gr, in0=gt, scalar=1.0, in1=gx, op0=ALU.add, op1=ALU.mult))
                nc.vector.tensor_scalar(gr, gr, 0.5, None, ALU.mult).then_inc(gelu_step, 1)
            return {3: cubic, 4: gelu}

        ng_staged, ng_turned, ng_copied = sem("ng_staged"), sem("ng_turned"), sem("ng_copied")
        n_staged, n_turned, n_copied, n_scored = (lane_sems(n) for n in ("n_staged", "n_turned", "n_copied", "n_scored"))
        n_max, n_exp, n_soft, n_back, n_pt, n_out, n_kept, n_gated = (
            lane_sems(n) for n in ("n_max", "n_exp", "n_soft", "n_back", "n_pt", "n_out", "n_kept", "n_gated"))
        n_q, n_qt, n_sc, n_w = [ns_q, ns_q1], [qn, qn1], [sn, sn1], [pt, pt1]
        SEG = ((2 * P + 4 * P, 15, 0), (0, P, 1), (P, P, 2), (3 * S + 16, 15, 3), (S, S, 4), (2 * S, S, 5))
        C0, C1 = 3 * S, 3 * S + 16

        n_banks = [[m[:, 0, :], m[:, 1, :], m[:, 2, :]], [m[:, 3, :], g[:, 2, :], g[:, 3, :]]]
        nr = gemms["in2r"]

        def n_groups(eng, group):
            with eng.Fori(0, N_G - 1) as gi:
                group(gi, True)
            group(N_G - 1, False)

        def n_unit(fn, eng, gi, hj, streams, first, n=1, **kw):
            if streams:
                for u in range(4 * hj + first, 4 * hj + first + n):
                    fn(eng, nr["u0"] // SLOTS + 2 * gi, u, **kw)

        def n_split(fn, eng, gi, hj, streams, first, n=1):
            if streams:
                for u in range(4 * hj + first + AHEAD, 4 * hj + first + AHEAD + n):
                    fn(eng, nr["u0"] // SLOTS + 2 * gi, u)

        def sp_queries(sp):
            with sp.Fori(0, N_G - 1) as gi:
                for u in range(8):
                    sp_unit(sp, nr["u0"] // SLOTS + 2 * gi, u, nr["w"][:, 2 * u:2 * u + 2, bass.ds(gi * NB + NB, NB)])

        def pool_n(pool):
            pool.wait_ge(pair_free[1], nr["pair0"][1] + 1)
            pool.wait_ge(cmp_out, 1)
            with pool.Fori(0, N_G) as gi:
                pool.wait_ge(ng_turned, gi + 1)
                nc.gpsimd.tensor_copy(ns_ks[:, :, :], p2[:, :, bass.ds(gi * P + KS, P)]).then_inc(ng_staged, 1)
                pool.wait_ge(pair_free[0], nr["pair0"][0] + gi + 1)
                nc.gpsimd.tensor_copy(ns_kw[:, :, :], p2[:, :, bass.ds(gi * P + KW, P)]).then_inc(ng_staged, 1)
                with pool.Fori(0, HPG // 2) as hj:
                    i = gi * 2 + hj
                    for l in LANES:
                        pool.wait_ge(n_turned[l], i + 1)
                        nc.gpsimd.tensor_copy(n_q[l][:, :, :], p2[:, :, bass.ds((2 * i + l) * P, P)]).then_inc(n_staged[l], 1)

        def pe_n(pe):
            pe.wait_ge(kc_copied, 3)
            pe.wait_ge(pair_free[1], nr["pair0"][1] + 1)
            pe.sem_inc(ng_turned, 1)
            for l in LANES:
                pe.sem_inc(n_turned[l], 1)

            def unit(eng, cyc, u):
                pe_unit(eng, cyc, u, 0, act_hi, act_lo, 2 * u, u == 0, u == 7)

            def group(gi, streams):
                if streams:
                    pe.wait_ge(pair_free[0], nr["pair0"][0] + gi + 1)
                n_unit(unit, pe, gi, 0, streams, 0)
                pe.wait_ge(ng_staged, 2 * gi + 2)
                pe.wait_ge(n_kept[0], 2 * gi + 1)
                for n, src in enumerate((ns_ks, ns_kw)):
                    for t in range(T):
                        ins = nc.tensor.transpose(n_banks[0][2][:, (2 * n + t) * P:(2 * n + t + 1) * P], src[:, t, :],
                                                  ident[:, :])
                ins.then_inc(ng_turned, 1)
                for hj in range(HPG // 2):
                    i = gi * 2 + hj
                    for l in LANES:
                        pe.wait_ge(n_staged[l], i + 1)
                        pe.wait_ge(n_kept[l], i + 1)
                        for t in range(T):
                            ins = nc.tensor.transpose(n_banks[l][0][:, t * P:(t + 1) * P], n_q[l][:, t, :], ident[:, :])
                        ins.then_inc(n_turned[l], 1)
                    n_unit(unit, pe, gi, hj, streams, 1 - hj)
                    for l in LANES:
                        bk = n_banks[l]
                        pe.wait_ge(n_copied[l], i + 1)
                        pe.wait_ge(ng_copied, gi + 1)
                        q = [n_qt[l][:, t * P:(t + 1) * P] for t in range(T)]
                        kcg = kcc[:, bass.ds(gi * NC_, NC_)]
                        for dst, qt, keys in ((bk[1][:, 0:P], q[0], ksw[:, 0:P]), (bk[1][:, P:S], q[0], ksw[:, S:S + P]),
                                              (bk[1][:, S:S + NC_], q[0], kcg), (bk[1][:, S + 16:S + 16 + NC_], q[1], kcg)):
                            nc.tensor.matmul(dst, qt, keys, start=True, stop=True, skip_group_check=True)
                        nc.tensor.matmul(bk[2], q[1], ksw[:, :], start=True, stop=True).then_inc(n_scored[l], 1)
                    n_unit(unit, pe, gi, hj, streams, 2 - hj, 2 + hj)
                    for l in LANES:
                        bk, sc_ = n_banks[l], n_sc[l]
                        pe.wait_ge(n_soft[l], 6 * i + 6)
                        for n, o1 in enumerate((0, P, S, S + P, 2 * S, 2 * S + P)):
                            nc.tensor.transpose(bk[n // 4][:, (n % 4) * P:(n % 4 + 1) * P], sc_[:, o1:o1 + P], ident[:, :])
                        nc.tensor.transpose(bk[1][0:NC_, 2 * P:3 * P], sc_[:, C0:C0 + NC_], ident[:, :])
                        nc.tensor.transpose(bk[1][0:NC_, 3 * P:4 * P], sc_[:, C1:C1 + NC_], ident[:, :]).then_inc(n_back[l], 1)
                    for l in LANES:
                        bk, w = n_banks[l], n_w[l]
                        pe.wait_ge(n_pt[l], 3 * i + 3)
                        vs = [p2[:, t, bass.ds(gi * P + VS, P)] for t in range(T)]
                        vw = [p2[:, t, bass.ds(gi * P + VW, P)] for t in range(T)]
                        vc = vcc[:, bass.ds(gi * P, P)]
                        p_ = [w[:, n * P:(n + 1) * P] for n in range(6)] + [w[0:NC_, n * P:(n + 1) * P] for n in (6, 7)]
                        for dst, terms in ((bk[2][:, 0:P], ((0, vs[0]), (1, vw[0]), (6, vc))),
                                           (bk[2][:, P:S], ((2, vs[0]), (3, vs[1]), (4, vw[0]), (5, vw[1]), (7, vc)))):
                            for n, (pn, v) in enumerate(terms):
                                ins = nc.tensor.matmul(dst, p_[pn], v, start=(n == 0), stop=(n == len(terms) - 1))
                        ins.then_inc(n_out[l], 1)

            n_groups(pe, group)

        def act_n(act):
            for l in LANES:
                act.sem_inc(n_kept[l], 1)

            def group(gi, streams):
                for hj in range(HPG // 2):
                    i = gi * 2 + hj
                    if hj == 0:
                        act.wait_ge(ng_turned, gi + 2)
                        nc.scalar.activation(ksw[:, :], n_banks[0][2], ACT.Copy).then_inc(ng_copied, 1)
                    for l in LANES:
                        act.wait_ge(n_turned[l], i + 2)
                        nc.scalar.activation(n_qt[l][:, :], n_banks[l][0][:, 0:S], ACT.Copy, scale=P ** -0.5)\
                          .then_inc(n_copied[l], 1)
                    n_split(act_unit, act, gi, hj, streams, 0)
                    for l in LANES:
                        sc_ = n_sc[l]
                        act.wait_ge(n_max[l], i + 1)
                        for o1, w, n in SEG:
                            nc.scalar.activation(sc_[:, o1:o1 + w], sc_[:, o1:o1 + w], ACT.Exp, bias=nmx_l[l][:, n:n + 1],
                                                 accum_out=sm_l[l][:, n:n + 1]).then_inc(n_exp[l], 1)
                    n_split(act_unit, act, gi, hj, streams, 1, 3)
                    for l in LANES:
                        bk, w = n_banks[l], n_w[l]
                        act.wait_ge(n_back[l], i + 1)
                        nc.scalar.activation(w[:, 0:512], bk[0], ACT.Copy).then_inc(n_pt[l], 1)
                        nc.scalar.activation(w[:, 512:768], bk[1][:, 0:S], ACT.Copy).then_inc(n_pt[l], 1)
                        nc.scalar.activation(w[0:NC_, 768:1024], bk[1][0:NC_, S:2 * S], ACT.Copy).then_inc(n_pt[l], 1)
                    if hj == 1 and streams:
                        act.wait_ge(unit_used, used(nr, gi))
                        for t in range(T):
                            ins = nc.scalar.activation(p2[:, t, bass.ds(gi * NB + NB, NB)], g[:, t, :], ACT.Copy,
                                                       scale=rstd("n2")[:, t:t + 1])
                        ins.then_inc(pair_free[0], 1)
                    for l in LANES:
                        act.wait_ge(n_out[l], i + 1)
                        nc.scalar.activation(p2[:, :, bass.ds((2 * i + l) * P, P)],
                                             n_banks[l][2][:, 0:S].rearrange("p (t d) -> p t d", t=T), ACT.Copy)\
                          .then_inc(n_kept[l], 1)

            n_groups(act, group)

        def dve_n(dve):
            dve.wait_ge(bias_in, 32)
            steps = count["d"]
            n_steps = 4 * 2

            def link(i, k, ins):
                ins.then_inc(chain_d, 1)
                dve.wait_ge(chain_d, steps + i * n_steps + k + 1)

            def group(gi, streams):
                for hj in range(HPG // 2):
                    i = gi * 2 + hj
                    n_split(dve_unit, dve, gi, hj, streams, 0)
                    for l in LANES:
                        bk, sc_ = n_banks[l], n_sc[l]
                        dve.wait_ge(n_scored[l], i + 1)
                        bias = b_n[:, bass.ds(2 * i + l, 1), :]
                        s0 = sc_[:, 0:S].rearrange("p (i n) -> p i n", i=2)
                        s1 = sc_[:, S:3 * S].rearrange("p (i n) -> p i n", i=2)
                        sc = sc_[:, C0:C0 + 32].rearrange("p (t n) -> p t n", t=2)[:, :, 0:NC_]
                        nc.vector.tensor_tensor(s0, bk[1][:, 0:S].rearrange("p (i n) -> p i n", i=2),
                                                bias[:, :, P:S].broadcast_to([P, 2, P]), ALU.add)
                        nc.vector.tensor_tensor(sc, bk[1][:, S:S + 32].rearrange("p (t n) -> p t n", t=2)[:, :, 0:NC_],
                                                bc[:, :, :, bass.ds(2 * i + l, 1)].rearrange("p t c o -> p t (c o)"), ALU.add)
                        link(i, 2 * l, nc.vector.tensor_tensor(s1, bk[2].rearrange("p (i n) -> p i n", i=2),
                                                               bias.broadcast_to([P, 2, S]), ALU.add))
                        mx = nmx_l[l][:, 0:6].rearrange("p (t b) -> p t b", b=3)
                        nc.vector.tensor_reduce(mx[:, :, 0], sc, X, ALU.max, negate=True)
                        nc.vector.tensor_reduce(mx[:, 0, 1:3], s0, X, ALU.max, negate=True)
                        link(i, 2 * l + 1, nc.vector.tensor_reduce(mx[:, 1, 1:3], s1, X, ALU.max, negate=True))
                        nc.vector.tensor_scalar(nmx_l[l][:, 0:6], nmx_l[l][:, 0:6], 1e29, None, ALU.min).then_inc(n_max[l], 1)
                    n_split(dve_unit, dve, gi, hj, streams, 1)
                    for l in LANES:
                        sc_, rc_ = n_sc[l], rc_l[l]
                        dve.wait_ge(n_exp[l], 6 * i + 6)
                        link(i, 4 + 2 * l, nc.vector.tensor_scalar(rc_[:, 0:6], sm_l[l][:, 0:6], 1e-30, None, ALU.max))
                        link(i, 5 + 2 * l, nc.vector.reciprocal(rc_[:, 0:6], rc_[:, 0:6]))
                        gv = gate[:, :, :].rearrange("p t (b h) -> p t b h", b=3)[:, :, :, bass.ds(2 * i + l, 1)]
                        nc.vector.tensor_tensor(rc_[:, 0:6].rearrange("p (t b) -> p t b", b=3),
                                                rc_[:, 0:6].rearrange("p (t b) -> p t b", b=3),
                                                gv.rearrange("p t b o -> p t (b o)"), ALU.mult).then_inc(n_gated[l], 1)
                        dve.wait_ge(n_gated[l], i + 1)
                        for o1, w, n in SEG:
                            nc.vector.tensor_scalar(sc_[:, o1:o1 + w], sc_[:, o1:o1 + w], rc_[:, n:n + 1], None, ALU.mult)\
                              .then_inc(n_soft[l], 1)
                    n_split(dve_unit, dve, gi, hj, streams, 2, 2)

            n_groups(dve, group)
            count["d"] += N_H // 2 * n_steps

        def bcast(ap1, n):
            return bass.AP(tensor=ap1.tensor, offset=ap1.offset, ap=[[0, P], [1, n]])

        block = ctx.enter_context(nc.Block())

        @block.sync
        def _(sp):
            sp.dma_start(oh_r[:, :], a["c_rising"]).then_inc(tables_in, 16)
            sp.dma_start(tab[0:32, 0:8], a["rel_bias"]).then_inc(tables_in, 16)
            sp.dma_start(tab[0:32, 8:24], a["rel_bias_2"]).then_inc(tables_in, 16)
            sp.dma_start(oh_f[:, :], a["c_falling"]).then_inc(tables_in, 16)
            sp.dma_start(ident[:, :], a["c_ident"]).then_inc(ident_in, 16)
            sp.dma_start(x[:, :, 0:NB], a["x"].rearrange("(t p) d -> p t d", p=P)[:, :, 0:NB]).then_inc(x_in[0], 16)
            for n, k in enumerate(("mix_pre_g", "mem_norm_g", "cross_pre_g", "ffn_pre_g", "mix_norm_g_2", "ffn_norm_g_2")):
                sp.dma_start(g_rows[16 * n:16 * n + 16, :], a[k].rearrange("(k p) -> k p", p=P)).then_inc(gains_in, 16)
            for n in range(1, 4):
                sp.dma_start(x[:, :, n * NB:(n + 1) * NB], a["x"].rearrange("(t p) d -> p t d", p=P)[:, :, n * NB:(n + 1) * NB])\
                  .then_inc(x_in[n], 16)
            sp_gemm(sp, "in1f", lambda c: c * NB + F_HG)
            sp_gemm(sp, "in1g", lambda c: c * NB + G_HG)
            sp_gemm(sp, "in1q", lambda c: c * NB + Q_HG)
            sp_gemm(sp, "in1b")
            sp_gemm(sp, "ckv")
            sp_gemm(sp, "out1")
            sp_gemm(sp, "cq")
            sp_gemm(sp, "co")
            sp_gemm_cols(sp, "ff1")
            sp_gemm(sp, "fo1")
            sp_gemm(sp, "in2c", lambda c: c * NB + KC)
            sp_gemm(sp, "in2k", lambda c: c * NB + KS)
            sp_cmp(sp)
            sp_gemm(sp, "in2q")
            sp_queries(sp)
            sp_gemm(sp, "out2")
            sp_gemm_cols(sp, "ff2")
            sp_gemm(sp, "fo2")
            for t in range(T):
                sp.wait_ge(fin_done, t + 1)
                sp.dma_start(out.rearrange("(t p) d -> p t d", p=P)[:, t, :], x[:, t, :]).then_inc(out_done, 16)
            sp.wait_ge(out_done, 32)

        @block.gpsimd
        def _(pool):
            pool.dma_start(cums[:, :], a["c_cums"]).then_inc(consts_in, 16)
            pool.dma_start(sub_g[:, :], bcast(a["da_subln_g"], P)).then_inc(consts_in, 16)
            pool.dma_start(on_g[:, :], bcast(a["hg_onorm_g"], P)).then_inc(consts_in, 16)
            for n, k in enumerate(("lambda_q1", "lambda_k1", "lambda_q2", "lambda_k2")):
                pool.dma_start(lam4[:, n, :], bcast(a[k], DA_D)).then_inc(consts_in, 16)
            pool.wait_ge(x_in[3], 16)
            pool.dma_start(masks[:, :], a["c_masks"]).then_inc(masks_in, 16)
            pool.dma_start(memx[:, :, :], a["mem"].rearrange("(t p) d -> p t d", p=P)).then_inc(mem_in, 16)
            pool.wait_ge(bt_sb, 1)
            rows = bt[:, :]
            skewed = bass.AP(tensor=rows.tensor, offset=rows.offset + P - 1, ap=[list(rows.ap[0]), [-1, P], [1, S]])
            pool.dma_start(dram_bias, skewed).then_inc(bt_stored, 16)
            pool_hg(pool)
            pool.wait_ge(bt_stored, 16)
            pool.wait_ge(lo_evac, BANKS["nmem"] + 8)
            pool.dma_start(b_da[:, :, :], dram_bias[0:DA_H].rearrange("h p k -> p h k")).then_inc(bias_in, 16)
            pool.dma_start(g_b[:, :], bcast(a["mix_post_g"], D)).then_inc(gb_in, 16)
            pool_da(pool)
            pool.wait_ge(pair_free[1], gemms["out1"]["pair0"][1] + 3)
            pool.dma_start(g_b[:, :], bcast(a["cross_post_g"], D)).then_inc(gb_in, 16)
            pool_cx(pool)
            pool.wait_ge(pair_free[1], gemms["co"]["pair0"][1] + 3)
            pool.dma_start(g_b[:, :], bcast(a["ffn_post_g"], D)).then_inc(gb_in, 16)
            pool.wait_ge(lo_evac, BANKS["n2"] + 8)
            for n, k in enumerate(("cmp_pos_k_2", "cmp_pos_v_2")):
                pool.dma_start(pos_s[:, n, :], a[k]).then_inc(cmp_in, 16)
            for n, k in enumerate(("cmp_w2_k_2", "cmp_w2_v_2")):
                pool.dma_start(w2[:, n, :, :], a[k].rearrange("(k p) d -> p k d", p=P)).then_inc(cmp_in, 16)
            pool.wait_ge(unit_used, SLOTS + cp["u0"] + 12)
            pool.dma_start(b_n[:, :, :], dram_bias[DA_H:DA_H + N_H].rearrange("h p k -> p h k")).then_inc(bias_in, 16)
            pool_n(pool)
            pool.wait_ge(lo_evac, BANKS["ff2"] + 2 * PAIRS)
            pool.dma_start(g_a[:, :], bcast(a["final_norm_g_2"], D)).then_inc(ga_in, 16)

        @block.tensor
        def _(pe):
            pe.sem_inc(unit_used, SLOTS)
            pe.wait_ge(tables_in, 16 * 4)
            pe.wait_ge(tab_ready, 1)
            nc.tensor.matmul(g[0:24, 0, :], tab[:, :], oh_f[:, :], start=True, stop=True).then_inc(bt_ready, 1)
            for t in range(T):
                for c in range(NC_):
                    o0 = P * t - CSTR * c - (CLEN - 1) + 256
                    ins = nc.tensor.matmul(g[:, 1, (t * NC_ + c) * N_H:(t * NC_ + c + 1) * N_H], oh_r[:, o0:o0 + P], tab[:, 8:24],
                                           start=(t == 0 and c == 0), stop=(t == 1 and c == NC_ - 1), skip_group_check=True)
            ins.then_inc(bt_ready, 1)
            pe.wait_ge(ident_in, 16)
            pe.wait_ge(gains_in, 16 * 6)
            nc.tensor.transpose(g[:, 2, 0:6 * 16], g_rows[:, :], ident[0:6 * 16, 0:6 * 16]).then_inc(gains_turned, 1)
            pe.wait_ge(gains_ready, 1)
            pe.wait_ge(bt_sb, 1)
            pe.wait_ge(bc_sb, 1)
            pe_gemm(pe, "in1f", turn="n1")
            pe_gemm(pe, "in1g")
            pe_gemm(pe, "in1q")
            pe_hg(pe)
            pe_da(pe)
            pe_gemm(pe, "out1", turn="mix1")
            pe_gemm(pe, "cq", turn="ncx")
            pe_cx(pe)
            pe_gemm(pe, "co", turn="cx")
            pe_ffn_in(pe, "ff1", "nff")
            turned_in(pe, "ff1", 2 * PAIRS)
            pe_gemm(pe, "fo1", ht_hi, ht_lo)
            pe_gemm(pe, "in2c", turn="n2")
            pe_gemm(pe, "in2k", also=pe_blocks(pe))
            pe_cmp(pe)
            pe_gemm(pe, "in2q", also=pe_hidden(pe))
            pe_n(pe)
            pe_gemm(pe, "out2", turn="mix2")
            pe_ffn_in(pe, "ff2", "nff2")
            turned_in(pe, "ff2", 2 * PAIRS)
            pe_gemm(pe, "fo2", ht_hi, ht_lo)

        def cols(dst):
            return lambda c: dst[:, :, bass.ds(c * NB, NB)]

        @block.scalar
        def _(act):
            act.sem_inc(pair_free[0], 1)
            act.sem_inc(pair_free[1], 1)
            act.wait_ge(bt_ready, 2)
            nc.scalar.activation(bt[:, :], g[0:24, 0, :], ACT.Copy).then_inc(bt_sb, 1)
            for n in range(4):
                act.wait_ge(x_in[n], 16)
            with_g, with_q = act_gates(act)
            f_out = act_copy_out(act, "in1f", lambda c: p1[:, :, bass.ds(c * NB + F_HG, NB)], "n1")
            g_out = act_copy_out(act, "in1g", lambda c: p1[:, :, bass.ds(c * NB + G_HG, NB)], "n1")
            act_gemm(act, "in1f", f_out, "n1", hold=True)
            act_gemm(act, "in1g", g_out, held=lambda: f_out(1, -1), hold=True, also=with_g)
            act_gemm(act, "in1q", act_copy_out(act, "in1q", lambda c: p1[:, :, bass.ds(c * NB + Q_HG, NB)], "n1"),
                     held=lambda: g_out(1, -1), also=with_q)
            act_lambda(act)
            act.wait_ge(bt_stored, 16)
            ahead(act_unit, act, "in1b", SLOTS)
            act_hg(act)
            act_da(act)
            act_mix_norm(act)
            act_gemm(act, "out1", act_squares_out(act, "out1", "post1", junk_r), "mix1", done=SLOTS)
            act_sqrt(act, "post1", ss_y)
            act_gemm(act, "cq", act_copy_out(act, "cq", cols(qx), "ncx"), "ncx")
            ahead(act_unit, act, "co", SLOTS)
            act_cx(act)
            act_gemm(act, "co", act_squares_out(act, "co", "postcx", junk_r), "cx", done=SLOTS)
            act_sqrt(act, "postcx", ss_y)
            act_ffn_in(act, "ff1", "nff")
            act_gemm(act, "fo1", act_squares_out(act, "fo1", "postff", junk_a))
            act_sqrt(act, "postff", ss_y)
            c_out = act_copy_out(act, "in2c", lambda c: p2[:, :, bass.ds(c * NB + KC, NB)], "n2")
            k_out = act_copy_out(act, "in2k", lambda c: p2[:, :, bass.ds(c * NB + KS, NB)], "n2")
            act_gemm(act, "in2c", c_out, "n2", hold=True)
            act_gemm(act, "in2k", k_out, held=lambda: c_out(1, -1), hold=True, also=act_blocks(act))
            act_cmp(act, lambda: k_out(2, -1))
            act_gemm(act, "in2q", act_copy_out(act, "in2q", cols(p2), "n2"), also=act_hidden(act))
            act_compressed(act)
            ahead(act_unit, act, "in2r")
            act_n(act)
            act_gemm(act, "out2", lambda i, c: None, "mix2", done=AHEAD)
            act_ffn_in(act, "ff2", "nff2")
            act_gemm(act, "fo2", act_squares_x(act, "fo2", junk_a))
            act_sqrt(act, "nfin", ss_y)

        @block.vector
        def _(dve):
            dve.sem_inc(lo_done, SLOTS)
            nc.vector.memset(tab[32:33, :], MASKED).then_inc(tab_ready, 1)
            dve.wait_ge(bt_ready, 2)
            nc.vector.tensor_copy(bc[:, :, :, :].rearrange("p t c h -> p (t c h)"), g[:, 1, 0:T * NC_ * N_H]).then_inc(bc_sb, 1)
            dve.wait_ge(gains_turned, 1)
            nc.vector.tensor_copy(g_cols[:, :], g[:, 2, 0:6 * 16]).then_inc(gains_ready, 1)
            dve.wait_ge(gains_ready, 1)
            with_g, with_q = dve_gates(dve)
            dve_gemm(dve, "in1f", turn="n1")
            dve_gemm(dve, "in1g", also=with_g)
            dve_gemm(dve, "in1q", also=with_q)
            dve_lambda(dve)
            ahead(dve_unit, dve, "in1b", SLOTS)
            dve_hg(dve)
            dve_da(dve)
            dve_mix_norm(dve)
            dve_gemm(dve, "out1", dve_scale_out(dve, "out1", "post1", y_r, 1), "mix1", done=SLOTS)
            dve_gemm(dve, "cq", turn="ncx")
            ahead(dve_unit, dve, "co", SLOTS)
            dve_cx(dve)
            dve_gemm(dve, "co", dve_scale_out(dve, "co", "postcx", y_r, 2), "cx", done=SLOTS)
            dve_ffn_in(dve, "ff1", "nff")
            dve_gemm(dve, "fo1", dve_scale_out(dve, "fo1", "postff", y_a, 3))
            dve_gemm(dve, "in2c", turn="n2")
            dve_gemm(dve, "in2k", also=dve_blocks(dve))
            dve_cmp(dve)
            dve_gemm(dve, "in2q", also=dve_hidden(dve))
            ahead(dve_unit, dve, "in2r")
            dve_n(dve)
            dve_gemm(dve, "out2", dve_add_out(dve, "out2"), "mix2", done=AHEAD)
            dve_ffn_in(dve, "ff2", "nff2")
            dve_gemm(dve, "fo2", dve_add_out(dve, "fo2"))
            dve.wait_ge(ss_done, SS["nfin"] + 8)
            link_d(dve, nc.vector.tensor_reduce(ss_y, ss8, X, ALU.add))
            nc.vector.tensor_scalar(ss_y, ss_y, 1.0 / D, EPS, ALU.mult, ALU.add).then_inc(var_done, 1)
            dve_rstd(dve, "nfin")
            dve.wait_ge(ga_in, 16)
            for t in range(T):
                nc.vector.scalar_tensor_tensor(out=x[:, t, :], in0=x[:, t, :], scalar=rstd("nfin")[:, t:t + 1],
                                               in1=g_a[:, :], op0=ALU.mult, op1=ALU.mult).then_inc(fin_done, 1)


_INS = ["x", "mem", "w_in", "w_out", "w_cq", "w_ckv", "w_co", "w_ffn_in", "w_ffn_out", "mix_pre_g", "mix_post_g",
        "cross_pre_g", "cross_post_g", "mem_norm_g", "ffn_pre_g", "ffn_post_g", "da_subln_g", "hg_onorm_g",
        "lambda_q1", "lambda_k1", "lambda_q2", "lambda_k2", "rel_bias", "rel_bias_2", "mix_norm_g_2", "ffn_norm_g_2",
        "final_norm_g_2", "nsa_w_in_2", "nsa_w_out_2", "cmp_pos_k_2", "cmp_w1_k_2", "cmp_w2_k_2", "cmp_pos_v_2",
        "cmp_w1_v_2", "cmp_w2_v_2", "ffn_w_in_2", "ffn_w_out_2"]
_WHOLE = ("rel_bias", "rel_bias_2", "final_norm_g_2")


def kernel(**inputs):
    import numpy as _np
    import concourse.bacc as _bacc
    from concourse import mybir as _mybir
    from concourse.bass_utils import run_bass_kernel_spmd as _run

    nc = _bacc.Bacc("TRN2", target_bir_lowering=False, num_devices=1)
    arrays, aps = {}, {}
    for name in _INS:
        v = _np.ascontiguousarray(inputs[name])
        arrays[f"in_{name}"] = v if name in _WHOLE else v.reshape(v.shape[1:])
    falling, rising = rel_rows()
    for name, v in (("c_ident", _np.eye(128, dtype=_np.float32)), ("c_cums", cumsum_lhs()), ("c_masks", level_masks()),
                    ("c_falling", falling), ("c_rising", rising)):
        arrays[f"in_{name}"] = v
    for key, v in arrays.items():
        aps[key[3:]] = nc.dram_tensor(key, v.shape, _mybir.dt.float32, kind="ExternalInput").ap()
    out = nc.dram_tensor("out_x", (256, 2048), _mybir.dt.float32, kind="ExternalOutput").ap()
    build(nc, aps, out)
    r = _run(nc, [arrays], core_ids=[0])
    return r.results[0]["out_x"].reshape(1, 256, 2048)
```

```python
from contextlib import ExitStack

import concourse.bass as bass
from concourse import mybir

F32 = mybir.dt.float32
F32R = mybir.dt.float32r
ALU = mybir.AluOpType
ACT = mybir.ActivationFunctionType
X = mybir.AxisListType.X

P = 128
D = 2048
T = 2
S = T * P
NB = 512
HB = 256
SLOTS = 4
UE = 1024
EPS = 1e-6

DA_H, DA_D = 8, 64
HG_H, HG_D = 8, 128
Q_DA, K_DA, V_DA, F_HG, Q_HG, I_HG, G_HG = (1024 * n for n in range(7))
IN1 = 7168
LAM_INIT = 0.2
CHUNK = 64
LEVELS = 8
CX_H = 4
CX_W = 512
FH = 5632
PAIRS = FH // NB
FKT = FH // P
KV = F_HG
N_H, N_G, HPG = 16, 4, 4
KC, VC, KS, VS, KW, VW, GL = 2048, 2560, 3072, 3584, 4096, 4608, 5120
IN2 = 5168
NC_, CSTR, CLEN, CHID = 15, 16, 32, 256
GB = N_G * NC_
MASKED = -1e30


def rel_rows():
    import math
    import numpy as np

    def bucket(n):
        if n < 16:
            return n
        return min(31, 16 + int(math.log(n / 16) / math.log(8.0) * 16))

    falling = np.zeros((33, 512), np.float32)
    rising = np.zeros((33, 512), np.float32)
    for m in range(512):
        d = 255 - m
        falling[bucket(d) if d >= 0 else 32, m] = 1
        d = m - 256
        rising[bucket(d) if d >= 0 else 32, m] = 1
    return falling, rising


def level_masks():
    import numpy as np
    s, t = np.arange(128)[:, None], np.arange(128)[None, :]
    m = np.zeros((128, 8, 128), np.float32)
    for l in range(7):
        w = 2 << l
        m[:, l, :] = (s // w == t // w) & (s % w < w // 2) & (t % w >= w // 2)
    m[:, 7, :] = s == t
    return m.reshape(128, 1024)


def cumsum_lhs():
    import numpy as np
    s, t = np.arange(128)[:, None], np.arange(128)[None, :]
    return ((s // CHUNK == t // CHUNK) & (s <= t)).astype(np.float32)


def build(nc, a, out):
    ctx = ExitStack()
    with ctx:
        base = (nc.sbuf_base + 31) // 32 * 32
        place = {}

        def at(name, shape, offset, dt=F32):
            return nc.alloc_sbuf_tensor_at(name, shape, dt, offset=base + offset)

        o_raw, o_wh, o_wl = 0, 16384, 32768
        o_ah, o_al = 49152, 65536
        o_x, o_ga, o_gb, o_r = 81920, 98304, 106496, 114688
        o_small = o_r + 2 * FKT * S * 4
        raw = at("raw", [P, SLOTS, UE], o_raw)
        wh = at("wh", [P, SLOTS, UE], o_wh, F32R)
        wl = at("wl", [P, SLOTS, UE], o_wl, F32R)
        act_hi = at("act_hi", [P, 16, S], o_ah, F32R)
        act_lo = at("act_lo", [P, 16, S], o_al, F32R)
        y_a = at("y_a", [P, 8, T, HB], o_al)
        junk_a = at("junk_a", [P, 2, T, NB], o_ah)
        x = at("x", [P, T, D], o_x)
        g_a = at("g_a", [P, D], o_ga)
        memx = at("memx", [P, T, D], o_ga)
        g_b = at("g_b", [P, D], o_gb)
        b_da = at("b_da", [P, DA_H, S], o_ga)
        ff_s = at("ff_s", [P, T, NB], o_ga)
        ff_h = at("ff_h", [P, T, NB], o_ga + 4096)
        ht_hi = at("ht_hi", [P, FKT, S], o_r, F32R)
        ht_lo = at("ht_lo", [P, FKT, S], o_r + FKT * S * 4, F32R)
        junk_r = at("junk_r", [P, 2, T, NB], o_r)
        junk_x = at("junk_x", [P, T, D], o_r + 16384)
        y_r = at("y_r", [P, 8, T, HB], o_r + 57344)
        p1 = at("p1", [P, T, IN1], o_r)
        o = o_r + 57344
        kk = at("kk", [P, T, 1024], o)
        o += 8192
        masks = at("masks", [P, 1024], o); o += 4096
        dec = at("dec", [P, LEVELS, S], o)
        junk_m1 = at("junk_m1", [P, D], o)
        sc_da = at("sc_da", [P, 768], o); o += 8192
        junk_m0 = at("junk_m0", [P, D], o)
        mp = at("mp", [P, 1024], o); o += 4096
        lf_s = at("lf_s", [P, T, P], o); o += 1024
        q_s = at("q_s", [P, T, P], o); o += 1024
        k_s = at("k_s", [P, T, P], o); o += 1024
        bq = at("bq", [P, 512], o); o += 2048
        kt = at("kt", [P, S], o); o += 1024
        at3 = at("at3", [P, 3, P], o); o += 1536
        assert o <= o_small
        o = o_r + 57344
        q_s1 = at("q_s1", [P, T, P], o); o += 1024
        k_s1 = at("k_s1", [P, T, P], o); o += 1024
        bq1 = at("bq1", [P, 512], o); o += 2048
        sc_da1 = at("sc_da1", [P, 768], o); o += 3072
        o += 1024
        at31 = at("at31", [P, 3, P], o)
        o = o_r
        qx = at("qx", [P, T, CX_W], o); o += 4096
        xq_s = at("xq_s", [P, T, P], o); o += 1024
        xk_s = at("xk_s", [P, T, P], o); o += 1024
        xqk = at("xqk", [P, 512], o); o += 2048
        xp = at("xp", [P, T, S], o); o += 2048
        xpt = at("xpt", [P, 4, P], o); o += 2048
        o = o_r + 16384
        xq_s1 = at("xq_s1", [P, T, P], o); o += 1024
        xk_s1 = at("xk_s1", [P, T, P], o); o += 1024
        xqk1 = at("xqk1", [P, 512], o); o += 2048
        xp1 = at("xp1", [P, T, S], o); o += 2048
        xpt1 = at("xpt1", [P, 4, P], o); o += 2048
        p2 = at("p2", [P, T, IN2], o_r)
        o = o_r + IN2 * T * 4
        kcc = at("kcc", [P, GB], o); o += 256
        vcc = at("vcc", [NC_, N_G * P], o); o += 2048
        gate = at("gate", [P, T, 48], o); o += 384
        b_n = at("b_n", [P, N_H, S], o)
        c0 = o
        blk_hi, blk_lo = [], []
        for n in range(2):
            if n == 1:
                post = at("post", [P, 2, CLEN], o); o += 256
                pos_s = at("pos_s", [CLEN, 2, P], o); o += 1024
            blk_hi.append(at(f"blk_hi{n}", [P, CLEN, GB], o, F32R)); o += 7680
            blk_lo.append(at(f"blk_lo{n}", [P, CLEN, GB], o, F32R)); o += 7680
        blk = at("blk", [P, CLEN, GB], o)
        gh = at("gh", [GB, 3, 2, CHID], o)
        ght = at("ght", [P, 2, 2, GB], o + 6144); o += 7680
        w2 = at("w2", [P, 2, 2, P], o); o += 2048
        assert o <= o_small
        o = c0 + 16384
        sn = at("sn", [P, 800], o); o += 3200
        pt = at("pt", [P, 1024], o); o += 4096
        ksw = at("ksw", [P, 512], o); o += 2048
        qn = at("qn", [P, S], o); o += 1024
        ns_q = at("ns_q", [P, T, P], o); o += 1024
        ns_ks = at("ns_ks", [P, T, P], o); o += 1024
        ns_kw = at("ns_kw", [P, T, P], o); o += 1024
        sn1 = at("sn1", [P, 800], o); o += 3200
        pt1 = at("pt1", [P, 1024], o); o += 4096
        qn1 = at("qn1", [P, S], o); o += 1024
        ns_q1 = at("ns_q1", [P, T, P], o); o += 1024
        assert o <= o_small
        oh_f = at("oh_f", [33, 512], o_r + 32768)
        oh_r = at("oh_r", [33, 512], o_r + 34816)
        bt = at("bt", [24, 512], o_r + 36864)
        g_rows = at("g_rows", [6 * 16, P], o_r + 38912)
        o = o_small
        ident = at("ident", [P, P], o); o += 512
        cums = at("cums", [P, P], o); o += 512
        bc = at("bc", [P, T, NC_, N_H], o); o += 1920
        tab = at("tab", [33, 24], o); o += 96
        sub_g = at("sub_g", [P, P], o); o += 512
        on_g = at("on_g", [P, P], o); o += 512
        lam4 = at("lam4", [P, 4, DA_D], o); o += 1024
        st = at("st", [P, 256], o); o += 1024
        g_cols = at("g_cols", [P, 6 * 16], o); o += 384
        assert base + o <= nc.sbuf_usable_end

        ss = st[:, 0:2]
        ss8 = st[:, 96:104].rearrange("p (t c) -> p t c", t=T)
        ss_y = st[:, 104:106]
        lam_d = st[:, 4:6]
        neg_lam = st[:, 6:7]
        ss16 = st[:, 32:64]
        nmx_l, sm_l, rc_l = ([st[:, o1 + 64 * l:o1 + 64 * l + 6] for l in range(2)] for o1 in (128, 136, 144))

        g = ctx.enter_context(nc.psum_tensor("g", [P, 4, NB], F32))
        m = ctx.enter_context(nc.psum_tensor("m", [P, 4, NB], F32))

        dram_bias = nc.dram_tensor("bias_rows", (24, P, S), F32, kind="Internal").ap()

        def sem(name):
            return ctx.enter_context(nc.semaphore(name))

        raw_full = [sem(f"raw_full{n}") for n in range(SLOTS)]
        hi_done, lo_done, unit_used = sem("hi_done"), sem("lo_done"), sem("unit_used")
        pair_free = [sem("pair_free0"), sem("pair_free1")]
        consts_in, masks_in, mem_in = sem("consts_in"), sem("masks_in"), sem("mem_in")
        tables_in, ident_in = sem("tables_in"), sem("ident_in")
        x_in = [sem(f"x_in{n}") for n in range(4)]
        ga_in, gb_in, bias_in = sem("ga_in"), sem("gb_in"), sem("bias_in")
        gains_in, gains_turned, gains_ready = sem("gains_in"), sem("gains_turned"), sem("gains_ready")
        chain_a, chain_d, chain_p = sem("act_step"), sem("dve_step"), sem("pool_step")
        tab_ready, bt_ready, bt_sb, bc_sb, bt_stored = (
            sem("tab_ready"), sem("bt_ready"), sem("bt_sb"), sem("bc_sb"), sem("bt_stored"))
        ss_done, var_done, sqrt_done, rstd_done = sem("ss_done"), sem("var_done"), sem("sqrt_done"), sem("rstd_done")
        turned, hi_evac, lo_evac = sem("turned"), sem("hi_evac"), sem("lo_evac")
        x_done, y_scaled, fin_done = sem("x_done"), sem("y_scaled"), sem("fin_done")
        out_done = sem("out_done")

        def spec(w, units, chunks):
            return {"w": w.rearrange("(k p) n -> p k n", p=P), "units": units, "chunks": chunks}

        gemms = {
            "in1f": spec(a["w_in"], 8, 2), "in1g": spec(a["w_in"], 8, 2), "in1q": spec(a["w_in"], 8, 4), "in1b": spec(a["w_in"], 8, 6),
            "ckv": spec(a["w_ckv"], 8, 2), "out1h": spec(a["w_out"], 4, 4), "out1": spec(a["w_out"], 4, 4),
            "cq": spec(a["w_cq"], 8, 1), "co": spec(a["w_co"], 2, 4),
            "ff1": spec(a["w_ffn_in"], 8, 22), "fo1": spec(a["w_ffn_out"], 22, 4),
            "in2c": spec(a["nsa_w_in_2"], 8, 2), "in2k": spec(a["nsa_w_in_2"], 8, 4), "cmp": {"units": 20, "chunks": 0},
            "in2q": spec(a["nsa_w_in_2"], 8, 1), "in2r": spec(a["nsa_w_in_2"], 8, 3),
            "out2": spec(a["nsa_w_out_2"], 8, 4),
            "ff2": spec(a["ffn_w_in_2"], 8, 22), "fo2": spec(a["ffn_w_out_2"], 22, 4),
        }
        at_unit, at_pair = 0, [0, 0]
        for name, s in gemms.items():
            s["u0"], s["pair0"] = at_unit, list(at_pair)
            if name == "cmp":
                at_unit += 20
                at_pair = [at_pair[0] + 1, at_pair[1] + 1]
            elif name in ("out1h", "in2r"):
                at_unit += s["units"] * s["chunks"]
                at_pair = [at_pair[0] + s["chunks"], at_pair[1]]
            else:
                at_unit += s["units"] * s["chunks"]
                at_pair = [at_pair[0] + (s["chunks"] + 1) // 2, at_pair[1] + s["chunks"] // 2]
            assert at_unit % SLOTS == 0

        def bodies(eng, s, body, step=2):
            n = s["chunks"]
            body(0, min(2, n), True)
            if n > 4:
                with eng.Fori(1, n // 2) as i:
                    body(i, 2, False)
            elif n == 4:
                body(1, 2, False)

        def sp_unit(sp, cyc, j, src, n=UE, shape=2):
            sp.wait_ge(lo_done, (cyc + j // SLOTS) * SLOTS + j % SLOTS + 1)
            sp.dma_start(raw[:, j % SLOTS, 0:n].rearrange("p (k n) -> p k n", k=shape), src)\
              .then_inc(raw_full[j % SLOTS], 16)

        def act_unit(act, cyc, j, n=UE):
            act.wait_ge(raw_full[j % SLOTS], (cyc + j // SLOTS) * 16 + 16)
            act.wait_ge(unit_used, (cyc + j // SLOTS) * SLOTS + j % SLOTS + 1)
            nc.scalar.activation(wh[:, j % SLOTS, 0:n], raw[:, j % SLOTS, 0:n], ACT.Copy).then_inc(hi_done, 1)

        def dve_unit(dve, cyc, j, n=UE):
            dve.wait_ge(hi_done, (cyc + j // SLOTS) * SLOTS + j % SLOTS + 1)
            nc.vector.tensor_tensor(wl[:, j % SLOTS, 0:n], raw[:, j % SLOTS, 0:n],
                                    wh[:, j % SLOTS, 0:n].bitcast(F32), ALU.subtract).then_inc(lo_done, 1)

        def pe_unit(pe, cyc, j, pair, hi, lo, k0, first, last):
            pe.wait_ge(lo_done, SLOTS + (cyc + j // SLOTS) * SLOTS + j % SLOTS + 1)
            for k in range(2):
                whk = wh[:, j % SLOTS, k * NB:(k + 1) * NB]
                wlk = wl[:, j % SLOTS, k * NB:(k + 1) * NB]
                for t in range(T):
                    dst = g[:, 2 * pair + t, :]
                    h = hi[:, k0 + k, t * P:(t + 1) * P]
                    l = lo[:, k0 + k, t * P:(t + 1) * P]
                    nc.tensor.matmul(dst, h, whk, start=(first and k == 0), stop=False)
                    nc.tensor.matmul(dst, h, wlk, start=False, stop=False)
                    ins = nc.tensor.matmul(dst, l, whk, start=False, stop=(last and k == 1))
            ins.then_inc(unit_used, 1)

        def used(s, chunk):
            return SLOTS + s["u0"] + s["units"] * (chunk + 1)

        def cyc_of(s, i):
            return s["u0"] // SLOTS + i * (2 * s["units"] // SLOTS)

        def sp_gemm(sp, name, col=lambda c: c * NB):
            s = gemms[name]

            def body(i, chunks, first):
                for j in range(chunks * s["units"]):
                    c, u = 2 * i + j // s["units"], j % s["units"]
                    sp_unit(sp, cyc_of(s, i), j, s["w"][:, 2 * u:2 * u + 2, bass.ds(col(c), NB)])
            bodies(sp, s, body)

        def act_gemm(act, name, evac, turn=None, held=None, hold=False, also={}, done=0, then=None):
            s = gemms[name]
            late = min(3, s["units"] - 1)

            def body(i, chunks, first):
                for j in range(chunks * s["units"]):
                    if not (first and j < done):
                        act_unit(act, cyc_of(s, i), j)
                    if first and turn:
                        act_lead_in(act, turn, j)
                    if first and held and j == late:
                        held()
                    if first and j in also:
                        also[j]()
                    if j == late and not first:
                        evac(i, -1)
                    if j == s["units"] + late:
                        evac(i, 0)
                if first and turn:
                    act_lead_in_rest(act, turn, chunks * s["units"])
            bodies(act, s, body)
            n = s["chunks"]
            if then:
                ahead(act_unit, act, then)
            if not hold:
                evac(*((n // 2, -1) if n > 1 else (0, 0)))

        AHEAD = 3

        def ahead(unit, eng, name, n=AHEAD):
            for j in range(n):
                unit(eng, gemms[name]["u0"] // SLOTS, j)

        def act_copy_out(act, name, dst, norm=None):
            s = gemms[name]

            def evac(i, c):
                chunk = 2 * i + c
                act.wait_ge(unit_used, used(s, chunk))
                if norm is None:
                    nc.scalar.activation(dst(chunk), g[:, 2 * (c % 2):2 * (c % 2) + 2, :], ACT.Copy)\
                      .then_inc(pair_free[c % 2], 1)
                    return
                act.wait_ge(rstd_done, NORM[norm] + 1)
                for t in range(T):
                    ins = nc.scalar.activation(dst(chunk)[:, t, :], g[:, 2 * (c % 2) + t, :], ACT.Copy,
                                               scale=rstd(norm)[:, t:t + 1])
                ins.then_inc(pair_free[c % 2], 1)
            return evac

        def act_squares_out(act, name, post, junk):
            s = gemms[name]

            def evac(i, c):
                chunk = 2 * i + c
                act.wait_ge(unit_used, used(s, chunk))
                for t in range(T):
                    nc.scalar.activation(junk[:, c % 2, t, :], g[:, 2 * (c % 2) + t, :], ACT.Square,
                                         accum_out=ss8[:, t, bass.ds(chunk, 1)]).then_inc(ss_done, 1)
            return evac

        def act_squares_x(act, name, junk):
            s = gemms[name]

            def evac(i, c):
                chunk = 2 * i + c
                act.wait_ge(pair_free[c % 2], s["pair0"][c % 2] + i + (2 if c >= 0 else 1))
                for t in range(T):
                    nc.scalar.activation(junk[:, c % 2, t, :], x[:, t, bass.ds(chunk * NB, NB)], ACT.Square,
                                         accum_out=ss8[:, t, bass.ds(chunk, 1)]).then_inc(ss_done, 1)
            return evac

        def dve_gemm(dve, name, evac=None, turn=None, also={}, done=0, then=None):
            s = gemms[name]
            late = min(3, s["units"] - 1)

            def body(i, chunks, first):
                if first and turn:
                    dve_add_block(dve, turn, 0)
                for j in range(chunks * s["units"]):
                    if not (first and j < done):
                        dve_unit(dve, cyc_of(s, i), j)
                    if first and turn:
                        dve_lead_in(dve, turn, j)
                    if first and j in also:
                        also[j]()
                    if evac and j == late and not first:
                        evac(i, -1)
                    if evac and j == s["units"] + late:
                        evac(i, 0)
                if first and turn:
                    dve_lead_in_rest(dve, turn, chunks * s["units"])
            bodies(dve, s, body)
            if then:
                ahead(dve_unit, dve, then)
            if evac:
                evac(s["chunks"] // 2, -1, True)

        def dve_scale_out(dve, name, post, y, gains):
            s = gemms[name]

            def evac(i, c, last=False):
                chunk = 2 * i + c
                dve.wait_ge(ss_done, SS[post] + T * chunk + T)
                if last:
                    link_d(dve, nc.vector.tensor_reduce(ss_y, ss8, X, ALU.add))
                    nc.vector.tensor_scalar(ss_y, ss_y, 1.0 / D, EPS, ALU.mult, ALU.add).then_inc(var_done, 1)
                dve.wait_ge(gb_in, 16 * gains)
                nc.vector.tensor_tensor(y[:, bass.ds(2 * chunk, 2), :, :],
                                        g[:, 2 * (c % 2):2 * (c % 2) + 2, :].rearrange("p t (b n) -> p b t n", b=2),
                                        g_b[:, bass.ds(chunk * NB, NB)].rearrange("p (b o n) -> p b o n", b=2, o=1)
                                        .broadcast_to([P, 2, T, HB]), ALU.mult).then_inc(pair_free[c % 2], 1)
                if last:
                    dve_rstd(dve, post)
                    dve.wait_ge(pair_free[0], s["pair0"][0] + s["chunks"] // 2 + 1)
                    dve.wait_ge(pair_free[1], s["pair0"][1] + s["chunks"] // 2 + 1)
            return evac

        def half_of_mixer(chunk):
            return p1[:, :, bass.ds(chunk * NB + Q_HG, NB)]

        def act_squares_y(act, name, y, junk):
            s = gemms[name]

            def evac(i, c):
                chunk = 2 * i + c
                act.wait_ge(pair_free[c % 2], s["pair0"][c % 2] + i + (2 if c >= 0 else 1))
                for t in range(T):
                    nc.scalar.activation(junk[:, c % 2, t, :].rearrange("p (b n) -> p b n", b=2),
                                         y[:, bass.ds(2 * chunk, 2), t, :], ACT.Square,
                                         accum_out=ss8[:, t, bass.ds(chunk, 1)]).then_inc(ss_done, 1)
            return evac

        def dve_halves_out(dve, name, post, y, gains):
            s = gemms[name]

            def evac(i, c, last=False):
                chunk = 2 * i + c
                yc = y[:, bass.ds(2 * chunk, 2), :, :]
                dve.wait_ge(unit_used, used(s, chunk))
                nc.vector.tensor_tensor(yc, g[:, 2 * (c % 2):2 * (c % 2) + 2, :].rearrange("p t (b n) -> p b t n", b=2),
                                        half_of_mixer(chunk).rearrange("p t (b n) -> p b t n", b=2), ALU.add)\
                  .then_inc(pair_free[c % 2], 1)
                dve.wait_ge(ss_done, SS[post] + T * chunk + T)
                if last:
                    link_d(dve, nc.vector.tensor_reduce(ss_y, ss8, X, ALU.add))
                    nc.vector.tensor_scalar(ss_y, ss_y, 1.0 / D, EPS, ALU.mult, ALU.add).then_inc(var_done, 1)
                dve.wait_ge(gb_in, 16 * gains)
                nc.vector.tensor_tensor(yc, yc, g_b[:, bass.ds(chunk * NB, NB)].rearrange("p (b o n) -> p b o n", b=2, o=1)
                                        .broadcast_to([P, 2, T, HB]), ALU.mult).then_inc(y_scaled, 1)
                if last:
                    dve_rstd(dve, post)
                    dve.wait_ge(y_scaled, 4)
            return evac

        def dve_add_out(dve, name):
            s = gemms[name]

            def evac(i, c, last=False):
                chunk = 2 * i + c
                dve.wait_ge(unit_used, used(s, chunk))
                xc = x[:, :, bass.ds(chunk * NB, NB)]
                nc.vector.tensor_tensor(xc, g[:, 2 * (c % 2):2 * (c % 2) + 2, :], xc, ALU.add).then_inc(pair_free[c % 2], 1)
            return evac

        def pe_gemm(pe, name, hi=None, lo=None, turn=None, also={}):
            s = gemms[name]
            hi, lo = (act_hi, act_lo) if hi is None else (hi, lo)

            def body(i, chunks, first):
                for j in range(chunks * s["units"]):
                    c, u = j // s["units"], j % s["units"]
                    if u == 0:
                        pe.wait_ge(pair_free[c], s["pair0"][c] + i + 1)
                    if first and turn:
                        pe_lead_in(pe, turn, j)
                    if first and j in also:
                        also[j]()
                    pe_unit(pe, cyc_of(s, i), j, c, hi, lo, 2 * u, u == 0, u == s["units"] - 1)
            bodies(pe, s, body)

        CONSTS = 16 * 7
        NORM, SS = {}, {}
        at_ss = 0
        for n, parts in (("n1", 2), ("nmem", 2), ("post1", 8), ("ncx", 2), ("postcx", 8), ("nff", 2), ("postff", 8),
                         ("n2", 2), ("nff2", 2), ("nfin", 8)):
            NORM[n], SS[n] = len(NORM), at_ss
            at_ss += parts
        BANKS = {}
        bank_at = 0
        for n, banks in (("n1", 8), ("nmem", 8), ("mixh", 4), ("mix1", 4), ("ncx", 8), ("cx", 2), ("nff", 8), ("ff1", 2 * PAIRS),
                         ("n2", 8), ("mix2", 8), ("nff2", 8), ("ff2", 2 * PAIRS)):
            BANKS[n] = bank_at
            bank_at += banks
        BANKS["mixh"] -= 4
        GAIN = {"n1": 0, "nmem": 1, "ncx": 2, "nff": 3, "n2": 4, "nff2": 5}
        ADDED = {"ncx": ("post1", 0, y_r), "nff": ("postcx", 16, y_r), "n2": ("postff", 32, y_a)}

        def rstd(name):
            return st[:, 72 + 2 * NORM[name]:74 + 2 * NORM[name]]

        def act_squares(act, name, src, junk):
            for t in range(T):
                nc.scalar.activation(junk[t], src[:, t, :], ACT.Square, accum_out=ss[:, t:t + 1]).then_inc(ss_done, 1)

        def act_sqrt(act, name, sums=ss):
            act.wait_ge(var_done, NORM[name] + 1)
            nc.scalar.activation(rstd(name), sums, ACT.Sqrt).then_inc(sqrt_done, 1)

        def dve_var(dve, name):
            dve.wait_ge(ss_done, SS[name] + 2)
            nc.vector.tensor_scalar(ss, ss, 1.0 / D, EPS, ALU.mult, ALU.add).then_inc(var_done, 1)

        def dve_rstd(dve, name):
            dve.wait_ge(sqrt_done, NORM[name] + 1)
            nc.vector.reciprocal(rstd(name), rstd(name)).then_inc(rstd_done, 1)
            dve.wait_ge(rstd_done, NORM[name] + 1)

        def dve_add_block(dve, name, b):
            if name in ADDED:
                post, _, y = ADDED[name]
                for t in range(T):
                    xb = x[:, t, b * HB:(b + 1) * HB]
                    nc.vector.scalar_tensor_tensor(out=xb, in0=y[:, b, t, :], scalar=rstd(post)[:, t:t + 1], in1=xb,
                                                   op0=ALU.mult, op1=ALU.add).then_inc(x_done, 1)

        def pe_lead_in(pe, name, j):
            n = TURNS[name][0]
            if j == 0:
                pe_turn_bank(pe, name, 0)
            if j + 1 < n:
                pe_turn_bank(pe, name, j + 1)
            if j < n:
                pe.wait_ge(lo_evac, BANKS[name] + j + 1)

        def act_lead_in(act, name, j):
            n = TURNS[name][0]
            if j < n:
                act_turn_bank(act, name, j)
            if name in GAIN:
                if j == n - 1:
                    if name in ADDED:
                        act.wait_ge(x_done, ADDED[name][1] + 16)
                    act_squares(act, name, x, [junk_x[:, 0, :], junk_x[:, 1, :]])
                if j == n + 2:
                    act_sqrt(act, name)

        def act_lead_in_rest(act, name, units):
            if name in GAIN and units < TURNS[name][0] + 3:
                act_sqrt(act, name)

        def dve_lead_in(dve, name, j):
            n = TURNS[name][0]
            if j + 1 < n:
                dve_add_block(dve, name, j + 1)
            if j < n:
                dve_turn_bank(dve, name, j)
            if name in GAIN and j == n + 1:
                dve_var(dve, name)
            if name in GAIN and j == n + 2:
                dve_rstd(dve, name)

        def dve_lead_in_rest(dve, name, units):
            if name in GAIN and units < TURNS[name][0] + 3:
                dve_var(dve, name)
                dve_rstd(dve, name)

        def pe_turn_bank(pe, name, b):
            n, src, ready = TURNS[name]
            bank = BANKS[name] + b
            ready(pe, b)
            if bank >= 4:
                pe.wait_ge(lo_evac, bank - 3)
            for k in range(2):
                for t in range(T):
                    ins = nc.tensor.transpose(m[:, bank % 4, (2 * k + t) * P:(2 * k + t + 1) * P], src(2 * b + k, t),
                                              ident[:, :])
            ins.then_inc(turned, 1)

        def act_turn_bank(act, name, b):
            bank = BANKS[name] + b
            act.wait_ge(turned, bank + 1)
            src = m[:, bank % 4, :].rearrange("p (k n) -> p k n", k=2)
            if name not in GAIN:
                nc.scalar.activation(act_hi[:, 2 * b:2 * b + 2, :], src, ACT.Copy).then_inc(hi_evac, 1)
                return
            act.wait_ge(gains_ready, 1)
            for k in range(2):
                gk = g_cols[:, 16 * GAIN[name] + 2 * b + k:16 * GAIN[name] + 2 * b + k + 1]
                ins = nc.scalar.activation(act_hi[:, 2 * b + k, :], src[:, k, :], ACT.Copy, scale=gk)
            ins.then_inc(hi_evac, 1)

        def dve_turn_bank(dve, name, b):
            bank = BANKS[name] + b
            dve.wait_ge(hi_evac, bank + 1)
            src = m[:, bank % 4, :].rearrange("p (k n) -> p k n", k=2)
            hi = act_hi[:, 2 * b:2 * b + 2, :].bitcast(F32)
            if name not in GAIN:
                nc.vector.tensor_tensor(act_lo[:, 2 * b:2 * b + 2, :], src, hi, ALU.subtract).then_inc(lo_evac, 1)
                return
            for k in range(2):
                gk = g_cols[:, 16 * GAIN[name] + 2 * b + k:16 * GAIN[name] + 2 * b + k + 1]
                ins = nc.vector.scalar_tensor_tensor(out=act_lo[:, 2 * b + k, :], in0=src[:, k, :], scalar=gk,
                                                     in1=hi[:, k, :], op0=ALU.mult, op1=ALU.subtract)
            ins.then_inc(lo_evac, 1)

        def x_rows(k, t):
            return x[:, t, k * P:(k + 1) * P]

        def after_add(name):
            return lambda pe, b: pe.wait_ge(x_done, ADDED[name][1] + 2 * b + 2)

        def after_out2(pe, b):
            c, s = b // 2, gemms["out2"]
            pe.wait_ge(pair_free[c % 2], s["pair0"][c % 2] + c // 2 + 2)

        TURNS = {
            "n1": (8, x_rows, lambda pe, b: pe.wait_ge(x_in[b // 2], 16)),
            "nmem": (8, lambda k, t: memx[:, t, k * P:(k + 1) * P], lambda pe, b: pe.wait_ge(mem_in, 16)),
            "mixh": (8, lambda k, t: mixed_rows(k, t), lambda pe, b: pe.wait_ge(mix_done, 2)),
            "mix1": (4, lambda k, t: mixed_rows(k, t), lambda pe, b: pe.wait_ge(mix_done, 4)),
            "ncx": (8, x_rows, after_add("ncx")),
            "cx": (2, lambda k, t: qx[:, t, k * P:(k + 1) * P], lambda pe, b: [pe.wait_ge(cx_kept[l], CX_H // 2 + 1) for l in LANES]),
            "nff": (8, x_rows, after_add("nff")),
            "n2": (8, x_rows, after_add("n2")),
            "mix2": (8, lambda k, t: p2[:, t, k * P:(k + 1) * P],
                     lambda pe, b: [pe.wait_ge(n_kept[l], N_H // 2 + 1) for l in LANES]),
            "nff2": (8, x_rows, after_out2),
        }

        count = {"a": 0, "d": 0}

        def turned_in(pe, name, n=8):
            pe.wait_ge(lo_evac, BANKS[name] + n)

        def link_d(dve, ins):
            count["d"] += 1
            ins.then_inc(chain_d, 1)
            dve.wait_ge(chain_d, count["d"])

        def link_a(act, ins):
            count["a"] += 1
            ins.then_inc(chain_a, 1)
            act.wait_ge(chain_a, count["a"])


        def sp_gemm_cols(sp, name):
            s = gemms[name]

            def body(i, chunks, first):
                for j in range(16):
                    u = j % 8
                    sp_unit(sp, cyc_of(s, i), j, s["w"][:, 2 * u:2 * u + 2, bass.ds(i * NB + (j // 8) * FH, NB)])
            bodies(sp, s, body)

        def pe_ff_turn(pe, name, i):
            b0 = BANKS[name]
            pe.wait_ge(pair_free[1], gemms[name]["pair0"][1] + i + 2)
            for b in range(2):
                pe.wait_ge(lo_evac, b0 + 2 * i + b - 1)
                for k in range(2):
                    for t in range(T):
                        ins = nc.tensor.transpose(m[:, b, (2 * k + t) * P:(2 * k + t + 1) * P],
                                                  ff_h[:, t, (2 * b + k) * P:(2 * b + k + 1) * P], ident[:, :])
                ins.then_inc(turned, 1)

        def act_ff_turn(act, name, i):
            b0 = BANKS[name]
            for b in range(2):
                act.wait_ge(turned, b0 + 2 * i + b + 1)
                nc.scalar.activation(ht_hi[:, bass.ds(4 * i + 2 * b, 2), :], m[:, b, :]
                                     .rearrange("p (k n) -> p k n", k=2), ACT.Copy).then_inc(hi_evac, 1)

        def dve_ff_turn(dve, name, i):
            b0 = BANKS[name]
            for b in range(2):
                dve.wait_ge(hi_evac, b0 + 2 * i + b + 1)
                nc.vector.tensor_tensor(ht_lo[:, bass.ds(4 * i + 2 * b, 2), :], m[:, b, :]
                                        .rearrange("p (k n) -> p k n", k=2),
                                        ht_hi[:, bass.ds(4 * i + 2 * b, 2), :].bitcast(F32), ALU.subtract)\
                  .then_inc(lo_evac, 1)

        def pe_ffn_in(pe, name, turn):
            s = gemms[name]

            def body(i, chunks, first):
                for j in range(16):
                    c, u = j // 8, j % 8
                    if u == 0:
                        pe.wait_ge(pair_free[c], s["pair0"][c] + i + 1)
                    if first:
                        pe_lead_in(pe, turn, j)
                    if j == 8 and not first:
                        pe_ff_turn(pe, name, i - 1)
                    pe_unit(pe, cyc_of(s, i), j, c, act_hi, act_lo, 2 * u, u == 0, u == 7)
            bodies(pe, s, body)
            pe_ff_turn(pe, name, PAIRS - 1)

        def act_ffn_in(act, name, turn, then):
            s = gemms[name]

            def body(i, chunks, first):
                for j in range(16):
                    if not first or j >= AHEAD:
                        act_unit(act, cyc_of(s, i), j)
                    if first:
                        act_lead_in(act, turn, j)
                    if j == 11:
                        if not first:
                            act_ff_turn(act, name, i - 1)
                            act.wait_ge(pair_free[1], s["pair0"][1] + i + 1)
                        act.wait_ge(unit_used, s["u0"] + SLOTS + 16 * i + 8)
                        act.wait_ge(rstd_done, NORM[turn] + 1)
                        for t in range(T):
                            ins = nc.scalar.activation(ff_s[:, t, :], g[:, t, :], ACT.Silu, scale=rstd(turn)[:, t:t + 1])
                        ins.then_inc(pair_free[0], 1)
            bodies(act, s, body)
            ahead(act_unit, act, then)
            act_ff_turn(act, name, PAIRS - 1)

        def dve_ffn_in(dve, name, turn, then):
            s = gemms[name]

            def mul(i):
                dve.wait_ge(pair_free[0], s["pair0"][0] + i + 2)
                dve.wait_ge(unit_used, s["u0"] + SLOTS + 16 * i + 16)
                for t in range(T):
                    ins = nc.vector.scalar_tensor_tensor(out=ff_h[:, t, :], in0=g[:, 2 + t, :], scalar=rstd(turn)[:, t:t + 1],
                                                         in1=ff_s[:, t, :], op0=ALU.mult, op1=ALU.mult)
                ins.then_inc(pair_free[1], 1)

            def body(i, chunks, first):
                if first:
                    dve_add_block(dve, turn, 0)
                for j in range(16):
                    if not first or j >= AHEAD:
                        dve_unit(dve, cyc_of(s, i), j)
                    if first:
                        dve_lead_in(dve, turn, j)
                    if j == 3 and not first:
                        mul(i - 1)
                    if j == 11 and not first:
                        dve_ff_turn(dve, name, i - 1)
            bodies(dve, s, body)
            ahead(dve_unit, dve, then)
            mul(PAIRS - 1)
            dve_ff_turn(dve, name, PAIRS - 1)

        hg_gates, hg_bulk = sem("hg_gates"), sem("hg_bulk")
        hg_staged, hg_turned, hg_copied, hg_diffed = sem("hg_staged"), sem("hg_turned"), sem("hg_copied"), sem("hg_diffed")
        hg_decayed, hg_weighted, hg_scored, hg_masked = sem("hg_decayed"), sem("hg_weighted"), sem("hg_scored"), sem("hg_masked")
        hg_summed, hg_far, hg_out, hg_kept = sem("hg_summed"), sem("hg_far"), sem("hg_out"), sem("hg_kept")
        f_all, g_all = p1[:, :, F_HG:F_HG + 1024], p1[:, :, G_HG:G_HG + 1024]

        def act_gates(act):
            def on_f(t, func, out=kk, src=None, done=False, **kw):
                def step():
                    ins = nc.scalar.activation(out[:, t, :], kk[:, t, :] if src is None else src[:, t, :], func, **kw)
                    ins.then_inc(hg_gates, 1) if done else link_a(act, ins)
                return step

            def first_abs():
                act.wait_ge(pair_free[1], gemms["in1f"]["pair0"][1] + 2)
                on_f(0, ACT.Abs, src=f_all)()

            def mem_squares(t, junk):
                return lambda: nc.scalar.activation(junk[:, :], memx[:, t, :], ACT.Square, accum_out=ss[:, t:t + 1])\
                    .then_inc(ss_done, 1)

            def mem_squares_first():
                act.wait_ge(mem_in, 16)
                mem_squares(0, junk_m0)()

            def after_bulk(t):
                def step():
                    act.wait_ge(hg_bulk, t + 1)
                    on_f(t, ACT.Exp, src=f_all, done=True)()
                return step

            def silu(t):
                def step():
                    act.wait_ge(pair_free[1], gemms["in1g"]["pair0"][1] + 2)
                    nc.scalar.activation(g_all[:, t, :], g_all[:, t, :], ACT.Silu).then_inc(hg_gates, 1)
                return step

            with_g = {4: first_abs, 5: on_f(1, ACT.Abs, src=f_all), 6: on_f(0, ACT.Exp, scale=-1.0),
                      7: on_f(1, ACT.Exp, scale=-1.0), 8: on_f(0, ACT.Ln, bias=1.0, done=True),
                      9: on_f(1, ACT.Ln, bias=1.0, done=True), 12: mem_squares_first, 13: mem_squares(1, junk_m1)}
            with_q = {1: lambda: act_sqrt(act, "nmem"), 4: after_bulk(0), 5: after_bulk(1), 6: silu(0), 7: silu(1),
                      10: lambda: act_lambda(act)}
            return with_g, with_q

        def dve_gates(dve):
            def log_f(t):
                def step():
                    dve.wait_ge(hg_gates, t + 1)
                    nc.vector.scalar_tensor_tensor(out=f_all[:, t, :], in0=f_all[:, t, :], scalar=0.0, in1=kk[:, t, :],
                                                   op0=ALU.min, op1=ALU.subtract).then_inc(hg_bulk, 1)
                return step

            def one_less_f(t):
                def step():
                    dve.wait_ge(hg_gates, 3 + t)
                    nc.vector.tensor_scalar(kk[:, t, :], kk[:, t, :], -1.0, 1.0, ALU.mult, ALU.add).then_inc(hg_bulk, 1)
                return step

            def gain(t):
                def step():
                    dve.wait_ge(hg_gates, 5 + t)
                    dve.wait_ge(consts_in, CONSTS)
                    link_d(dve, nc.vector.tensor_tensor(
                        p1[:, t, G_HG:G_HG + 1024].rearrange("p (h d) -> p h d", d=HG_D),
                        p1[:, t, G_HG:G_HG + 1024].rearrange("p (h d) -> p h d", d=HG_D),
                        on_g[:, :].rearrange("p (o d) -> p o d", o=1).broadcast_to([P, HG_H, HG_D]), ALU.mult))
                return step

            with_g = {10: log_f(0), 11: log_f(1)}
            with_q = {0: lambda: dve_var(dve, "nmem"), 2: lambda: dve_rstd(dve, "nmem"), 5: one_less_f(0),
                      6: one_less_f(1), 7: gain(0), 8: gain(1), 9: lambda: dve_lambda(dve)}
            return with_g, with_q

        def pool_hg(pool):
            pool.wait_ge(hg_bulk, 4)
            with pool.Fori(0, HG_H) as h:
                pool.wait_ge(hg_turned, h + 1)
                for dst, src, col in ((lf_s, p1, F_HG), (q_s, p1, Q_HG), (k_s, kk, 0)):
                    nc.gpsimd.tensor_copy(dst[:, :, :], src[:, :, bass.ds(h * HG_D + col, HG_D)]).then_inc(hg_staged, 1)

        def hg_heads(eng, head, turn):
            with eng.Fori(0, 3) as i:
                for c in range(2):
                    head(gemms["in1b"], 2 * i + c, i, c)
            for b in range(8):
                turn(eng, "nmem", b)
            for c in range(2):
                head(gemms["ckv"], 6 + c, 0, c)

        def pe_hg(pe):
            pe.wait_ge(consts_in, CONSTS)
            pe.sem_inc(hg_turned, 1)
            pe.sem_inc(hg_out, 1)

            def head(s, h, i, c):
                def units(first, n):
                    if first == 0:
                        pe.wait_ge(pair_free[c], s["pair0"][c] + i + 1)
                    for u in range(first, first + n):
                        pe_unit(pe, cyc_of(s, i), 8 * c + u, c, act_hi, act_lo, 2 * u, u == 0, u == 7)

                units(0, 1)
                pe.wait_ge(hg_staged, 3 * h + 3)
                pe.wait_ge(hg_kept, h + 1)
                for t in range(T):
                    nc.tensor.matmul(m[:, 0, t * P:(t + 1) * P], lf_s[:, t, :], cums[:, :], start=(t == 0), stop=(t == 1),
                                     skip_group_check=True)
                for t in range(T):
                    nc.tensor.transpose(m[:, 0, S + t * P:S + (t + 1) * P], q_s[:, t, :], ident[:, :])
                for t in range(T):
                    ins = nc.tensor.transpose(m[:, 1, t * P:(t + 1) * P], k_s[:, t, :], ident[:, :])
                ins.then_inc(hg_turned, 1)
                units(1, 5)
                pe.wait_ge(hg_weighted, h + 2)
                nc.tensor.matmul(m[:, 1, S:S + P], dec[:, 7, 0:P], dec[:, 7, P:S], start=True, stop=True)
                for t in range(T):
                    pe.wait_ge(hg_masked, 2 * h + t + 1)
                    for l in range(8):
                        lhs = dec[:, l, t * P:(t + 1) * P] if l < 7 else kt[:, t * P:(t + 1) * P]
                        rhs = dec[:, l, t * P:(t + 1) * P] if l < 7 else bq[:, S + t * P:S + (t + 1) * P]
                        ins = nc.tensor.matmul(m[:, 2 + l // 4, (l % 4) * P:(l % 4 + 1) * P], lhs, rhs,
                                               start=(l % 4 == 0), stop=(l % 4 == 3), skip_group_check=True)
                    ins.then_inc(hg_scored, 1)
                    units(6 + t, 1)
                pe.wait_ge(hg_summed, 2 * h + 3)
                pe.wait_ge(hg_far, h + 1)
                v = [p1[:, t, bass.ds(h * HG_D + I_HG, HG_D)] for t in range(T)]
                nc.tensor.matmul(m[:, 0, 0:P], at3[:, 0, :], v[0], start=True, stop=True)
                nc.tensor.matmul(m[:, 0, P:S], at3[:, 1, :], v[1], start=True, stop=False)
                nc.tensor.matmul(m[:, 0, P:S], at3[:, 2, :], v[0], start=False, stop=True).then_inc(hg_out, 1)

            def turn(pe, name, b):
                if b == 0:
                    pe.wait_ge(hg_kept, 7)
                    pe.wait_ge(hg_masked, 13)
                pe_turn_bank(pe, name, b)
                if b == 7:
                    turned_in(pe, name)

            hg_heads(pe, head, turn)

        def act_hg(act):
            act.sem_inc(hg_kept, 1)

            def head(s, h, i, c):
                def units(first, n):
                    for u in range(first, first + n):
                        act_unit(act, cyc_of(s, i), 8 * c + u)

                act.wait_ge(hg_turned, h + 2)
                act.wait_ge(hg_weighted, h + 1)
                nc.scalar.activation(bq[:, :], m[:, 0, :], ACT.Copy).then_inc(hg_copied, 1)
                nc.scalar.activation(kt[:, :], m[:, 1, 0:S], ACT.Copy).then_inc(hg_copied, 1)
                units(4, 2)
                act.wait_ge(hg_diffed, h + 1)
                nc.scalar.activation(dec[:, :, :], dec[:, :, :], ACT.Exp).then_inc(hg_decayed, 1)
                units(6, 4)
                act.wait_ge(hg_scored, 2 * h + 1)
                act.wait_ge(hg_out, h + 1)
                nc.scalar.activation(at3[:, 2, :], m[:, 1, S:S + P], ACT.Copy).then_inc(hg_far, 1)
                units(10, 1)
                mem = s is gemms["ckv"]
                dst = p1[:, :, bass.ds((2 * i + c) * NB + (KV if mem else 0), NB)]
                act_copy_out(act, "ckv" if mem else "in1b", lambda chunk: dst, "nmem" if mem else "n1")(i, c)
                act.wait_ge(hg_out, h + 2)
                nc.scalar.activation(p1[:, :, bass.ds(h * HG_D + Q_HG, HG_D)],
                                     m[:, 0, 0:S].rearrange("p (t d) -> p t d", t=T), ACT.Copy).then_inc(hg_kept, 1)
                units(11, 1)

            hg_heads(act, head, act_turn_bank)

        def dve_hg(dve):
            dve.sem_inc(hg_weighted, 1)
            dve.sem_inc(hg_masked, 1)
            dve.sem_inc(hg_summed, 1)
            dve.wait_ge(masks_in, 16)
            b = bq[:, 0:S]
            c0 = count["d"]

            def head(s, h, i, c):
                def units(first, n):
                    for u in range(first, first + n):
                        dve_unit(dve, cyc_of(s, i), 8 * c + u)

                dve.wait_ge(hg_copied, 2 * h + 2)
                nc.vector.tensor_tensor(lam_d[:, 0:1], b[:, 63:64], b[:, 127:128], ALU.add).then_inc(chain_d, 1)
                for l in range(7):
                    w = 1 << l
                    bv = b.rearrange("p (n w) -> p n w", w=2 * w)
                    dv = dec[:, l, :].rearrange("p (n w) -> p n w", w=2 * w)
                    ref = bv[:, :, w - 1:w].broadcast_to([P, S // (2 * w), w])
                    nc.vector.tensor_tensor(dv[:, :, 0:w], ref, bv[:, :, 0:w], ALU.subtract)
                    if l < 6:
                        nc.vector.tensor_tensor(dv[:, :, w:2 * w], bv[:, :, w:2 * w], ref, ALU.subtract)
                    else:
                        nc.vector.tensor_copy(dv[:, :, w:2 * w], bv[:, :, w:2 * w])
                dve.wait_ge(chain_d, c0 + h + 1)
                nc.vector.tensor_scalar(dec[:, 7, 0:64], b[:, 0:64], -1.0, lam_d[:, 0:1], ALU.mult, ALU.add)
                nc.vector.tensor_scalar(dec[:, 7, 64:128], b[:, 64:128], -1.0, b[:, 127:128], ALU.mult, ALU.add)
                nc.vector.tensor_copy(dec[:, 7, 128:192], b[:, 128:192])
                nc.vector.tensor_scalar(dec[:, 7, 192:256], b[:, 192:256], b[:, 191:192], None, ALU.add)\
                  .then_inc(hg_diffed, 1)
                units(4, 1)
                dve.wait_ge(hg_decayed, h + 1)
                for l in range(8):
                    w = 1 << l
                    dv = dec[:, l, :].rearrange("p (n w) -> p n w", w=2 * w)
                    kv_ = kt[:, :].rearrange("p (n w) -> p n w", w=2 * w)
                    qv = bq[:, S:2 * S].rearrange("p (n w) -> p n w", w=2 * w)
                    nc.vector.tensor_tensor(dv[:, :, 0:w], dv[:, :, 0:w], kv_[:, :, 0:w], ALU.mult)
                    ins = nc.vector.tensor_tensor(dv[:, :, w:2 * w], dv[:, :, w:2 * w], qv[:, :, w:2 * w], ALU.mult)
                ins.then_inc(hg_weighted, 1)
                units(5, 3)
                dve.wait_ge(hg_out, h + 1)
                for t in range(T):
                    dve.wait_ge(hg_summed, 2 * h + t + 1)
                    dve.wait_ge(hg_scored, 2 * h + t + 1)
                    nc.vector.tensor_tensor(mp[:, :], m[:, 2:4, :].rearrange("p a n -> p (a n)"), masks[:, :], ALU.mult)\
                      .then_inc(hg_masked, 1)
                    if t == 0:
                        units(8, 1)
                    dve.wait_ge(hg_masked, 2 * h + t + 2)
                    nc.vector.tensor_reduce(at3[:, t, :], mp[:, :].rearrange("p (l s) -> p s l", l=8), X, ALU.add)\
                      .then_inc(hg_summed, 1)
                units(9, 3)

            hg_heads(dve, head, dve_turn_bank)
            count["d"] += HG_H

        LANES = range(2)
        banks = [[m[:, 0, :], m[:, 1, :], m[:, 2, :]], [m[:, 3, :], g[:, 2, :], g[:, 3, :]]]

        def lane_sems(name):
            return [sem(f"{name}{l}") for l in LANES]

        da_staged, da_turned, da_copied, da_scored = (lane_sems(n) for n in ("da_staged", "da_turned", "da_copied", "da_scored"))
        da_max, da_exp, da_mixed, da_back = (lane_sems(n) for n in ("da_max", "da_exp", "da_mixed", "da_back"))
        da_at, da_out, da_kept = (lane_sems(n) for n in ("da_at", "da_out", "da_kept"))
        da_q, da_k, da_qk, da_sc, da_w = [q_s, q_s1], [k_s, k_s1], [bq, bq1], [sc_da, sc_da1], [at3, at31]
        lam_step = sem("lam_step")
        mix_sq, mix_var, mix_sqrt, mix_done = sem("mix_sq"), sem("mix_var"), sem("mix_sqrt"), sem("mix_done")

        def dve_lambda(dve):
            dve.wait_ge(consts_in, CONSTS)
            for n in range(2):
                link_d(dve, nc.vector.tensor_tensor(lam4[:, 2 * n, :], lam4[:, 2 * n, :], lam4[:, 2 * n + 1, :], ALU.mult))
                link_d(dve, nc.vector.tensor_reduce(st[:, 70 + n:71 + n], lam4[:, 2 * n, :], X, ALU.add))
            nc.vector.tensor_scalar(sub_g[:, :], sub_g[:, :], 1.0 - LAM_INIT, None, ALU.mult).then_inc(lam_step, 1)
            dve.wait_ge(lam_step, 2)
            link_d(dve, nc.vector.tensor_tensor(neg_lam, st[:, 71:72], st[:, 70:71], ALU.subtract))
            link_d(dve, nc.vector.tensor_scalar(neg_lam, neg_lam, -LAM_INIT, None, ALU.add))

        def act_lambda(act):
            act.wait_ge(lam_step, 1)
            nc.scalar.activation(st[:, 70:72], st[:, 70:72], ACT.Exp).then_inc(lam_step, 1)

        def pool_da(pool):
            pool.wait_ge(hg_kept, HG_H + 1)
            pool.wait_ge(pair_free[1], gemms["in1b"]["pair0"][1] + 4)
            with pool.Fori(0, DA_H // 2) as i:
                for l in LANES:
                    pool.wait_ge(da_turned[l], i + 1)
                    for dst, col in ((da_q[l], Q_DA), (da_k[l], K_DA)):
                        nc.gpsimd.tensor_copy(dst[:, :, :], p1[:, :, bass.ds((2 * i + l) * P + col, P)])\
                          .then_inc(da_staged[l], 1)

        oh = gemms["out1h"]

        def sp_half(sp):
            with sp.Fori(0, DA_H // 2) as i:
                for u in range(4):
                    sp_unit(sp, oh["u0"] // SLOTS + i, u, oh["w"][:, 8 + 2 * u:10 + 2 * u, bass.ds(i * NB, NB)])

        def pe_da(pe):
            pe.wait_ge(hg_kept, HG_H + 1)
            for l in LANES:
                pe.sem_inc(da_turned[l], 1)
            with pe.Fori(0, DA_H // 2) as i:
                pe.wait_ge(pair_free[0], oh["pair0"][0] + i + 1)
                for l in LANES:
                    pe.wait_ge(da_staged[l], 2 * i + 2)
                    pe.wait_ge(da_kept[l], i + 1)
                    for n, src in enumerate((da_q[l], da_k[l])):
                        for t in range(T):
                            ins = nc.tensor.transpose(banks[l][0][:, (2 * n + t) * P:(2 * n + t + 1) * P], src[:, t, :],
                                                      ident[:, :])
                    ins.then_inc(da_turned[l], 1)
                pe_unit(pe, oh["u0"] // SLOTS + i, 0, 0, act_hi, act_lo, 8, True, False)
                for l in LANES:
                    pe.wait_ge(da_copied[l], i + 1)
                    for q0, keys in ((0, P), (P, S)):
                        for j in range(2):
                            r = slice(j * DA_D, (j + 1) * DA_D)
                            ins = nc.tensor.matmul(banks[l][1 + j][:, q0:q0 + keys], da_qk[l][r, q0:q0 + P],
                                                   da_qk[l][r, S:S + keys], start=(q0 == 0), stop=(q0 != 0),
                                                   skip_group_check=True)
                    ins.then_inc(da_scored[l], 1)
                for u in range(1, 4):
                    pe_unit(pe, oh["u0"] // SLOTS + i, u, 0, act_hi, act_lo, 8 + 2 * u, False, u == 3)
                for l in LANES:
                    pe.wait_ge(da_mixed[l], 2 * i + 2)
                    for n, o1 in enumerate((0, S, S + P)):
                        ins = nc.tensor.transpose(banks[l][0][:, n * P:(n + 1) * P], da_sc[l][:, o1:o1 + P], ident[:, :])
                    ins.then_inc(da_back[l], 1)
                for l in LANES:
                    pe.wait_ge(da_at[l], i + 1)
                    v = [p1[:, t, bass.ds((2 * i + l) * P + V_DA, P)] for t in range(T)]
                    nc.tensor.matmul(banks[l][1][:, 0:P], da_w[l][:, 0, :], v[0], start=True, stop=True)
                    nc.tensor.matmul(banks[l][1][:, P:S], da_w[l][:, 1, :], v[0], start=True, stop=False)
                    nc.tensor.matmul(banks[l][1][:, P:S], da_w[l][:, 2, :], v[1], start=False, stop=True)\
                      .then_inc(da_out[l], 1)

        def act_da(act):
            for l in LANES:
                act.sem_inc(da_kept[l], 1)
            with act.Fori(0, DA_H // 2) as i:
                for l in LANES:
                    act.wait_ge(da_turned[l], i + 2)
                    nc.scalar.activation(da_qk[l][:, :], banks[l][0], ACT.Copy).then_inc(da_copied[l], 1)
                for l in LANES:
                    act.wait_ge(da_max[l], 2 * i + 2)
                    for n, (o1, w) in enumerate(((0, P), (P, P), (S, S), (2 * S, S))):
                        nc.scalar.activation(da_sc[l][:, o1:o1 + w], da_sc[l][:, o1:o1 + w], ACT.Exp,
                                             bias=nmx_l[l][:, n:n + 1], accum_out=sm_l[l][:, n:n + 1])\
                          .then_inc(da_exp[l], 1)
                for u in range(4, 7):
                    act_unit(act, oh["u0"] // SLOTS + i, u)
                for l in LANES:
                    act.wait_ge(da_back[l], i + 1)
                    nc.scalar.activation(da_w[l][:, :, :], banks[l][0][:, 0:3 * P].rearrange("p (a n) -> p a n", a=3), ACT.Copy)\
                      .then_inc(da_at[l], 1)
                act.wait_ge(unit_used, used(oh, i))
                nc.scalar.activation(half_of_mixer(i), g[:, 0:2, :], ACT.Copy).then_inc(pair_free[0], 1)
                act_unit(act, oh["u0"] // SLOTS + i, 7)
                for l in LANES:
                    act.wait_ge(da_out[l], i + 1)
                    nc.scalar.activation(p1[:, :, bass.ds((2 * i + l) * P, P)],
                                         banks[l][1][:, 0:S].rearrange("p (t d) -> p t d", t=T), ACT.Copy)\
                      .then_inc(da_kept[l], 1)

        def dve_da(dve):
            dve.wait_ge(bias_in, 16)
            steps = count["d"]
            n_steps = 5 * 2

            def link(i, k, ins):
                ins.then_inc(chain_d, 1)
                dve.wait_ge(chain_d, steps + i * n_steps + k + 1)

            with dve.Fori(0, DA_H // 2) as i:
                for l in LANES:
                    dve.wait_ge(da_scored[l], i + 1)
                    bias = b_da[:, bass.ds(2 * i + l, 1), :]
                    s0 = da_sc[l][:, 0:S].rearrange("p (i n) -> p i n", i=2)
                    s1 = da_sc[l][:, S:3 * S].rearrange("p (i n) -> p i n", i=2)
                    pair = (m[:, 1:3, :], g[:, 2:4, :])[l]
                    nc.vector.scalar_tensor_tensor(out=s0, in0=pair[:, :, 0:P], scalar=DA_D ** -0.5,
                                                   in1=bias[:, :, P:S].broadcast_to([P, 2, P]),
                                                   op0=ALU.mult, op1=ALU.add)
                    link(i, l, nc.vector.scalar_tensor_tensor(out=s1, in0=pair[:, :, P:P + S], scalar=DA_D ** -0.5,
                                                              in1=bias.broadcast_to([P, 2, S]),
                                                              op0=ALU.mult, op1=ALU.add))
                    nc.vector.tensor_reduce(nmx_l[l][:, 0:2], s0, X, ALU.max, negate=True).then_inc(da_max[l], 1)
                    nc.vector.tensor_reduce(nmx_l[l][:, 2:4], s1, X, ALU.max, negate=True).then_inc(da_max[l], 1)
                for l in LANES:
                    rc_, sc_ = rc_l[l], da_sc[l]
                    dve.wait_ge(da_exp[l], 4 * i + 4)
                    link(i, 2 + 4 * l, nc.vector.reciprocal(rc_[:, 0:4], sm_l[l][:, 0:4]))
                    link(i, 3 + 4 * l, nc.vector.tensor_scalar(rc_[:, 1:4:2], rc_[:, 1:4:2], neg_lam, None, ALU.mult))
                    nc.vector.tensor_scalar(sc_[:, P:S], sc_[:, P:S], rc_[:, 1:2], None, ALU.mult).then_inc(chain_d, 1)
                    link(i, 5 + 4 * l, nc.vector.tensor_scalar(sc_[:, 2 * S:3 * S], sc_[:, 2 * S:3 * S], rc_[:, 3:4], None,
                                                               ALU.mult))
                    nc.vector.scalar_tensor_tensor(out=sc_[:, 0:P], in0=sc_[:, 0:P], scalar=rc_[:, 0:1], in1=sc_[:, P:S],
                                                   op0=ALU.mult, op1=ALU.add).then_inc(da_mixed[l], 1)
                    nc.vector.scalar_tensor_tensor(out=sc_[:, S:2 * S], in0=sc_[:, S:2 * S], scalar=rc_[:, 2:3],
                                                   in1=sc_[:, 2 * S:3 * S], op0=ALU.mult, op1=ALU.add)\
                      .then_inc(da_mixed[l], 1)
                for u in range(4, 8):
                    dve_unit(dve, oh["u0"] // SLOTS + i, u)
            count["d"] += DA_H // 2 * n_steps

        HALVES = ((Q_DA, K_DA), (Q_HG, I_HG))

        def act_mix_norm(act, n):
            if n:
                act.wait_ge(hg_kept, HG_H + 1)
            else:
                for l in LANES:
                    act.wait_ge(da_kept[l], DA_H // 2 + 1)
            src, junk = HALVES[n]
            nc.scalar.activation(p1[:, :, junk:junk + 1024], p1[:, :, src:src + 1024], ACT.Square).then_inc(mix_sq, 1)
            act.wait_ge(mix_var, 2 - n)
            nc.scalar.activation(ss16[:, 16 * n:16 * n + 16], ss16[:, 16 * n:16 * n + 16], ACT.Sqrt).then_inc(mix_sqrt, 1)

        def dve_mix_norm(dve, n):
            s16 = ss16[:, 16 * n:16 * n + 16]
            s3 = s16.rearrange("p (t h) -> p t h", t=T)
            src, junk = HALVES[n]
            dve.wait_ge(mix_sq, 2 - n)
            link_d(dve, nc.vector.tensor_reduce(
                s3, p1[:, :, junk:junk + 1024].rearrange("p t (h d) -> p t h d", d=P), X, ALU.add))
            nc.vector.tensor_scalar(s16, s16, 1.0 / P, EPS, ALU.mult, ALU.add).then_inc(mix_var, 1)
            dve.wait_ge(mix_sqrt, 2 - n)
            link_d(dve, nc.vector.reciprocal(s16, s16))
            for t in range(T):
                rows = p1[:, t, src:src + 1024].rearrange("p (h d) -> p h d", d=P)
                scale = s3[:, t, :].rearrange("p (h o) -> p h o", o=1).broadcast_to([P, 8, P])
                gain = (p1[:, t, G_HG:G_HG + 1024].rearrange("p (h d) -> p h d", d=P) if n else
                        sub_g[:, :].rearrange("p (o d) -> p o d", o=1).broadcast_to([P, 8, P]))
                link_d(dve, nc.vector.tensor_tensor(rows, rows, scale, ALU.mult))
                nc.vector.tensor_tensor(rows, rows, gain, ALU.mult).then_inc(mix_done, 1)

        def mixed_rows(k, t):
            col = k * P if k < 8 else Q_HG + (k - 8) * P
            return p1[:, t, col:col + P]

        cx_staged, cx_turned, cx_copied, cx_scored = (lane_sems(n) for n in ("cx_staged", "cx_turned", "cx_copied", "cx_scored"))
        cx_max, cx_exp, cx_soft, cx_back = (lane_sems(n) for n in ("cx_max", "cx_exp", "cx_soft", "cx_back"))
        cx_pt, cx_out, cx_kept = (lane_sems(n) for n in ("cx_pt", "cx_out", "cx_kept"))
        cx_banks, cx_q, cx_k, cx_qk, cx_p, cx_w = [m, g], [xq_s, xq_s1], [xk_s, xk_s1], [xqk, xqk1], [xp, xp1], [xpt, xpt1]
        CX_SCALE = P ** -0.5

        def pool_cx(pool):
            pool.wait_ge(pair_free[0], gemms["cq"]["pair0"][0] + 2)
            pool.wait_ge(pair_free[1], gemms["ckv"]["pair0"][1] + 2)
            with pool.Fori(0, CX_H // 2) as i:
                for l in LANES:
                    pool.wait_ge(cx_turned[l], i + 1)
                    nc.gpsimd.tensor_copy(cx_q[l][:, :, :], qx[:, :, bass.ds((2 * i + l) * P, P)]).then_inc(cx_staged[l], 1)
                    nc.gpsimd.tensor_copy(cx_k[l][:, :, :], p1[:, :, bass.ds((2 * i + l) * P + KV, P)])\
                      .then_inc(cx_staged[l], 1)

        def pe_cx(pe):
            pe.wait_ge(pair_free[0], gemms["cq"]["pair0"][0] + 2)
            for l in LANES:
                pe.sem_inc(cx_turned[l], 1)
            with pe.Fori(0, CX_H // 2) as i:
                for l in LANES:
                    bk = cx_banks[l]
                    pe.wait_ge(cx_staged[l], 2 * i + 2)
                    for n, src in enumerate((cx_q[l], cx_k[l])):
                        for t in range(T):
                            ins = nc.tensor.transpose(bk[:, 0, (2 * n + t) * P:(2 * n + t + 1) * P], src[:, t, :], ident[:, :])
                    ins.then_inc(cx_turned[l], 1)
                for l in LANES:
                    bk = cx_banks[l]
                    pe.wait_ge(cx_copied[l], i + 1)
                    for t in range(T):
                        ins = nc.tensor.matmul(bk[:, 1, t * S:(t + 1) * S], cx_qk[l][:, t * P:(t + 1) * P],
                                               cx_qk[l][:, S:2 * S], start=(t == 0), stop=(t == 1), skip_group_check=True)
                    ins.then_inc(cx_scored[l], 1)
                for l in LANES:
                    bk = cx_banks[l]
                    pe.wait_ge(cx_soft[l], 2 * i + 2)
                    for k in range(2):
                        for t in range(T):
                            ins = nc.tensor.transpose(bk[:, 2, (2 * k + t) * P:(2 * k + t + 1) * P],
                                                      cx_p[l][:, t, k * P:(k + 1) * P], ident[:, :])
                    ins.then_inc(cx_back[l], 1)
                for l in LANES:
                    bk = cx_banks[l]
                    pe.wait_ge(cx_pt[l], i + 1)
                    pe.wait_ge(cx_kept[l], i + 1)
                    for t in range(T):
                        for k in range(2):
                            ins = nc.tensor.matmul(bk[:, 3, t * P:(t + 1) * P], cx_w[l][:, 2 * k + t, :],
                                                   p1[:, k, bass.ds((2 * i + l) * P + KV + CX_W, P)],
                                                   start=(k == 0), stop=(k == 1))
                    ins.then_inc(cx_out[l], 1)

        def act_cx(act):
            for l in LANES:
                act.sem_inc(cx_kept[l], 1)
            with act.Fori(0, CX_H // 2) as i:
                for l in LANES:
                    act.wait_ge(cx_turned[l], i + 2)
                    nc.scalar.activation(cx_qk[l][:, :], cx_banks[l][:, 0, :], ACT.Copy).then_inc(cx_copied[l], 1)
                for l in LANES:
                    act.wait_ge(cx_max[l], i + 1)
                    for t in range(T):
                        nc.scalar.activation(cx_p[l][:, t, :], cx_banks[l][:, 1, t * S:(t + 1) * S], ACT.Exp,
                                             bias=nmx_l[l][:, 2 + t:3 + t], scale=CX_SCALE, accum_out=sm_l[l][:, t:t + 1])\
                          .then_inc(cx_exp[l], 1)
                for l in LANES:
                    act.wait_ge(cx_back[l], i + 1)
                    nc.scalar.activation(cx_w[l][:, :, :], cx_banks[l][:, 2, :].rearrange("p (a n) -> p a n", a=4), ACT.Copy)\
                      .then_inc(cx_pt[l], 1)
                for l in LANES:
                    act.wait_ge(cx_out[l], i + 1)
                    nc.scalar.activation(qx[:, :, bass.ds((2 * i + l) * P, P)],
                                         cx_banks[l][:, 3, 0:S].rearrange("p (t d) -> p t d", t=T), ACT.Copy)\
                      .then_inc(cx_kept[l], 1)

        def dve_cx(dve):
            steps = count["d"]
            with dve.Fori(0, CX_H // 2) as i:
                for l in LANES:
                    dve.wait_ge(cx_scored[l], i + 1)
                    nc.vector.tensor_reduce(nmx_l[l][:, 0:2], cx_banks[l][:, 1, :].rearrange("p (t n) -> p t n", t=T), X, ALU.max,
                                            negate=True).then_inc(chain_d, 1)
                    dve.wait_ge(chain_d, steps + 4 * i + l + 1)
                    nc.vector.tensor_scalar(nmx_l[l][:, 2:4], nmx_l[l][:, 0:2], CX_SCALE, None, ALU.mult).then_inc(cx_max[l], 1)
                for l in LANES:
                    dve.wait_ge(cx_exp[l], 2 * i + 2)
                    nc.vector.reciprocal(rc_l[l][:, 0:2], sm_l[l][:, 0:2]).then_inc(chain_d, 1)
                    dve.wait_ge(chain_d, steps + 4 * i + l + 3)
                    for t in range(T):
                        nc.vector.tensor_scalar(cx_p[l][:, t, :], cx_p[l][:, t, :], rc_l[l][:, t:t + 1], None, ALU.mult)\
                          .then_inc(cx_soft[l], 1)
            count["d"] += 2 * CX_H

        cp = gemms["cmp"]
        kc_turned, kc_copied, blk_sum, blk_split = sem("kc_turned"), sem("kc_copied"), sem("blk_sum"), sem("blk_split")
        cmp_in, gelu_step, gelu_act, g_turned, g_copied, cmp_out = (
            sem("cmp_in"), sem("gelu_step"), sem("gelu_act"), sem("g_turned"), sem("g_copied"), sem("cmp_out"))

        def sp_cmp(sp):
            cyc = cp["u0"] // SLOTS
            wg = gemms["in2k"]["w"]
            for j in range(4):
                sp_unit(sp, cyc, j, wg[:, 4 * j:4 * j + 4, GL:GL + 48], 4 * 48, 4)
            for b, w in enumerate((a["cmp_w1_k_2"], a["cmp_w1_v_2"])):
                wv = w.rearrange("(k p) n -> p k n", p=P)
                for j in range(8):
                    sp_unit(sp, cyc, 4 + 8 * b + j, wv[:, 4 * j:4 * j + 4, :], UE, 4)

        BLK_BANKS = ((1, 2), (3, 0))

        def pe_blocks(pe):
            def turn_pos():
                pe.wait_ge(cmp_in, 64)
                for b in range(2):
                    ins = nc.tensor.transpose(m[:, 0, b * CLEN:(b + 1) * CLEN], pos_s[:, b, :], ident[0:CLEN, 0:CLEN])
                ins.then_inc(kc_turned, 1)

            def turn(b):
                def step():
                    pe.wait_ge(pair_free[b], gemms["in2c"]["pair0"][b] + 2)
                    if b == 1:
                        pe.wait_ge(kc_copied, 1)
                    for n in range(N_G):
                        for t in range(T):
                            ins = nc.tensor.transpose(
                                m[:, BLK_BANKS[b][n // 2], (n % 2) * S + t * P:(n % 2) * S + (t + 1) * P],
                                p2[:, t, KC + b * 512 + n * P:KC + b * 512 + (n + 1) * P], ident[:, :])
                    ins.then_inc(kc_turned, 1)
                return step
            return {2: turn_pos, 4: turn(0), 7: turn(1)}

        def act_blocks(act):
            def copy_pos():
                act.wait_ge(kc_turned, 1)
                nc.scalar.activation(post[:, :, :], m[:, 0, 0:2 * CLEN].rearrange("p (b i) -> p b i", b=2), ACT.Copy)\
                  .then_inc(kc_copied, 1)

            def split(b):
                def step():
                    act.wait_ge(blk_sum, b + 1)
                    nc.scalar.activation(blk_hi[b][:, :, :], blk[:, :, :], ACT.Copy).then_inc(blk_split, 1)
                return step
            return {6: copy_pos, 9: split(0), 13: split(1)}

        def dve_blocks(dve):
            def build_blk(b):
                def step():
                    dve.wait_ge(kc_copied, 1)
                    dve.wait_ge(kc_turned, b + 2)
                    if b == 1:
                        dve.wait_ge(blk_split, 2)
                    for n in range(N_G):
                        src = m[:, BLK_BANKS[b][n // 2], (n % 2) * S:(n % 2 + 1) * S]
                        win = bass.AP(tensor=src.tensor, offset=src.offset, ap=[list(src.ap[0]), [1, CLEN], [CSTR, NC_]])
                        ins = nc.vector.tensor_tensor(blk[:, :, n * NC_:(n + 1) * NC_], win,
                                                      post[:, b, :].rearrange("p (i o) -> p i o", o=1)
                                                      .broadcast_to([P, CLEN, NC_]), ALU.add)
                    ins.then_inc(blk_sum, 1)
                return step

            def rest(b):
                def step():
                    dve.wait_ge(blk_split, 2 * b + 1)
                    nc.vector.tensor_tensor(blk_lo[b][:, :, :], blk[:, :, :], blk_hi[b][:, :, :].bitcast(F32), ALU.subtract)\
                      .then_inc(blk_split, 1)
                return step
            return {8: build_blk(0), 10: rest(0), 12: build_blk(1), 14: rest(1)}

        def pe_cmp(pe):
            pe.wait_ge(pair_free[0], cp["pair0"][0] + 1)
            for j in range(4):
                pe.wait_ge(lo_done, SLOTS + cp["u0"] + j + 1)
                for k in range(4):
                    for t in range(T):
                        h = act_hi[:, 4 * j + k, t * P:(t + 1) * P]
                        l = act_lo[:, 4 * j + k, t * P:(t + 1) * P]
                        whk, wlk = wh[:, j, k * 48:(k + 1) * 48], wl[:, j, k * 48:(k + 1) * 48]
                        dst = g[:, t, 0:48]
                        nc.tensor.matmul(dst, h, whk, start=(j == 0 and k == 0), stop=False)
                        nc.tensor.matmul(dst, h, wlk, start=False, stop=False)
                        ins = nc.tensor.matmul(dst, l, whk, start=False, stop=(j == 3 and k == 3))
                ins.then_inc(unit_used, 1)
            pe.wait_ge(pair_free[1], cp["pair0"][1] + 1)
            for b in range(2):
                pe.wait_ge(blk_split, 2 * b + 2)
                for j in range(8):
                    u = 4 + 8 * b + j
                    pe.wait_ge(lo_done, SLOTS + cp["u0"] + u + 1)
                    for k in range(4):
                        h, l = blk_hi[b][:, 4 * j + k, :], blk_lo[b][:, 4 * j + k, :]
                        whk = wh[:, u % SLOTS, k * CHID:(k + 1) * CHID]
                        wlk = wl[:, u % SLOTS, k * CHID:(k + 1) * CHID]
                        dst = g[0:GB, 2 + b, 0:CHID]
                        nc.tensor.matmul(dst, h, whk, start=(j == 0 and k == 0), stop=False)
                        nc.tensor.matmul(dst, h, wlk, start=False, stop=False)
                        ins = nc.tensor.matmul(dst, l, whk, start=False, stop=(j == 7 and k == 3))
                    ins.then_inc(unit_used, 1)

        def act_cmp(act, held):
            for j in range(20):
                act_unit(act, cp["u0"] // SLOTS, j, 192 if j < 4 else UE)
                if j == 3:
                    held()
                if j == 7:
                    act.wait_ge(unit_used, SLOTS + cp["u0"] + 4)
                    for t in range(T):
                        ins = nc.scalar.activation(gate[:, t, :], g[:, t, 0:48], ACT.Sigmoid, scale=rstd("n2")[:, t:t + 1])
                    ins.then_inc(pair_free[0], 1)

        def dve_cmp(dve):
            for j in range(20):
                dve_unit(dve, cp["u0"] // SLOTS, j, 192 if j < 4 else UE)

        gx, gt, gr = gh[:, 2, :, :], gh[:, 1, :, :], gh[:, 0, :, :]
        hidden = g[0:GB, 2:4, 0:CHID]

        def pe_hidden(pe):
            def turn():
                pe.wait_ge(gelu_step, 3)
                for b in range(2):
                    for k in range(2):
                        ins = nc.tensor.transpose(m[:, 3, (2 * b + k) * GB:(2 * b + k + 1) * GB],
                                                  gh[:, 0, b, k * P:(k + 1) * P], ident[0:GB, 0:GB])
                ins.then_inc(g_turned, 1)

            def product():
                pe.wait_ge(g_copied, 1)
                for k in range(2):
                    nc.tensor.matmul(m[:, 2, 0:GB], w2[:, 0, k, :], ght[:, 0, k, :], start=(k == 0), stop=(k == 1))
                for n in range(N_G):
                    for k in range(2):
                        ins = nc.tensor.matmul(m[0:NC_, 1, n * P:(n + 1) * P], ght[:, 1, k, n * NC_:(n + 1) * NC_],
                                               w2[:, 1, k, :], start=(k == 0), stop=(k == 1))
                ins.then_inc(cmp_out, 1)
            return {3: turn, 5: product}

        def act_hidden(act):
            def square():
                act.wait_ge(unit_used, SLOTS + cp["u0"] + 20)
                nc.scalar.activation(gt, hidden, ACT.Square).then_inc(gelu_act, 1)

            def tanh():
                act.wait_ge(gelu_step, 2)
                nc.scalar.activation(gt, gt, ACT.Tanh, scale=0.7978845608028654).then_inc(gelu_act, 1)

            def copy():
                act.wait_ge(g_turned, 1)
                nc.scalar.activation(ght[:, :, :, :], m[:, 3, 0:4 * GB].rearrange("p (b k n) -> p b k n", b=2, k=2), ACT.Copy)\
                  .then_inc(g_copied, 1)
            return {3: square, 4: tanh, 6: copy}

        def act_compressed(act):
            act.wait_ge(cmp_out, 1)
            nc.scalar.activation(kcc[:, :], m[:, 2, 0:GB], ACT.Copy).then_inc(kc_copied, 1)
            nc.scalar.activation(vcc[:, :], m[0:NC_, 1, :], ACT.Copy).then_inc(kc_copied, 1)

        def dve_hidden(dve):
            def cubic():
                dve.wait_ge(gelu_act, 1)
                nc.vector.tensor_copy(gx, hidden).then_inc(pair_free[1], 1)
                link_d(dve, nc.vector.tensor_scalar(gt, gt, 0.044715, 1.0, ALU.mult, ALU.add))
                dve.wait_ge(pair_free[1], cp["pair0"][1] + 2)
                nc.vector.tensor_tensor(gt, gt, gx, ALU.mult).then_inc(gelu_step, 2)

            def gelu():
                dve.wait_ge(gelu_act, 2)
                link_d(dve, nc.vector.scalar_tensor_tensor(out=gr, in0=gt, scalar=1.0, in1=gx, op0=ALU.add, op1=ALU.mult))
                nc.vector.tensor_scalar(gr, gr, 0.5, None, ALU.mult).then_inc(gelu_step, 1)
            return {3: cubic, 4: gelu}

        ng_staged, ng_turned, ng_copied = sem("ng_staged"), sem("ng_turned"), sem("ng_copied")
        n_staged, n_turned, n_copied, n_scored = (lane_sems(n) for n in ("n_staged", "n_turned", "n_copied", "n_scored"))
        n_max, n_exp, n_soft, n_back, n_pt, n_out, n_kept, n_gated = (
            lane_sems(n) for n in ("n_max", "n_exp", "n_soft", "n_back", "n_pt", "n_out", "n_kept", "n_gated"))
        n_q, n_qt, n_sc, n_w = [ns_q, ns_q1], [qn, qn1], [sn, sn1], [pt, pt1]
        SEG = ((2 * P + 4 * P, 15, 0), (0, P, 1), (P, P, 2), (3 * S + 16, 15, 3), (S, S, 4), (2 * S, S, 5))
        C0, C1 = 3 * S, 3 * S + 16

        n_banks = [[m[:, 0, :], m[:, 1, :], m[:, 2, :]], [m[:, 3, :], g[:, 2, :], g[:, 3, :]]]
        nr = gemms["in2r"]

        def n_groups(eng, group):
            with eng.Fori(0, N_G - 1) as gi:
                group(gi, True)
            group(N_G - 1, False)

        def n_unit(fn, eng, gi, hj, streams, first, n=1, **kw):
            if streams:
                for u in range(4 * hj + first, 4 * hj + first + n):
                    fn(eng, nr["u0"] // SLOTS + 2 * gi, u, **kw)

        def n_split(fn, eng, gi, hj, streams, first, n=1):
            if streams:
                for u in range(4 * hj + first + AHEAD, 4 * hj + first + AHEAD + n):
                    fn(eng, nr["u0"] // SLOTS + 2 * gi, u)

        def sp_queries(sp):
            with sp.Fori(0, N_G - 1) as gi:
                for u in range(8):
                    sp_unit(sp, nr["u0"] // SLOTS + 2 * gi, u, nr["w"][:, 2 * u:2 * u + 2, bass.ds(gi * NB + NB, NB)])

        def pool_n(pool):
            pool.wait_ge(pair_free[1], nr["pair0"][1] + 1)
            pool.wait_ge(cmp_out, 1)
            with pool.Fori(0, N_G) as gi:
                pool.wait_ge(ng_turned, gi + 1)
                nc.gpsimd.tensor_copy(ns_ks[:, :, :], p2[:, :, bass.ds(gi * P + KS, P)]).then_inc(ng_staged, 1)
                pool.wait_ge(pair_free[0], nr["pair0"][0] + gi + 1)
                nc.gpsimd.tensor_copy(ns_kw[:, :, :], p2[:, :, bass.ds(gi * P + KW, P)]).then_inc(ng_staged, 1)
                with pool.Fori(0, HPG // 2) as hj:
                    i = gi * 2 + hj
                    for l in LANES:
                        pool.wait_ge(n_turned[l], i + 1)
                        nc.gpsimd.tensor_copy(n_q[l][:, :, :], p2[:, :, bass.ds((2 * i + l) * P, P)]).then_inc(n_staged[l], 1)

        def pe_n(pe):
            pe.wait_ge(kc_copied, 3)
            pe.wait_ge(pair_free[1], nr["pair0"][1] + 1)
            pe.sem_inc(ng_turned, 1)
            for l in LANES:
                pe.sem_inc(n_turned[l], 1)

            def unit(eng, cyc, u):
                pe_unit(eng, cyc, u, 0, act_hi, act_lo, 2 * u, u == 0, u == 7)

            def group(gi, streams):
                if streams:
                    pe.wait_ge(pair_free[0], nr["pair0"][0] + gi + 1)
                n_unit(unit, pe, gi, 0, streams, 0)
                pe.wait_ge(ng_staged, 2 * gi + 2)
                pe.wait_ge(n_kept[0], 2 * gi + 1)
                for n, src in enumerate((ns_ks, ns_kw)):
                    for t in range(T):
                        ins = nc.tensor.transpose(n_banks[0][2][:, (2 * n + t) * P:(2 * n + t + 1) * P], src[:, t, :],
                                                  ident[:, :])
                ins.then_inc(ng_turned, 1)
                for hj in range(HPG // 2):
                    i = gi * 2 + hj
                    for l in LANES:
                        pe.wait_ge(n_staged[l], i + 1)
                        pe.wait_ge(n_kept[l], i + 1)
                        for t in range(T):
                            ins = nc.tensor.transpose(n_banks[l][0][:, t * P:(t + 1) * P], n_q[l][:, t, :], ident[:, :])
                        ins.then_inc(n_turned[l], 1)
                    n_unit(unit, pe, gi, hj, streams, 1 - hj)
                    for l in LANES:
                        bk = n_banks[l]
                        pe.wait_ge(n_copied[l], i + 1)
                        pe.wait_ge(ng_copied, gi + 1)
                        q = [n_qt[l][:, t * P:(t + 1) * P] for t in range(T)]
                        kcg = kcc[:, bass.ds(gi * NC_, NC_)]
                        for dst, qt, keys in ((bk[1][:, 0:P], q[0], ksw[:, 0:P]), (bk[1][:, P:S], q[0], ksw[:, S:S + P]),
                                              (bk[1][:, S:S + NC_], q[0], kcg), (bk[1][:, S + 16:S + 16 + NC_], q[1], kcg)):
                            nc.tensor.matmul(dst, qt, keys, start=True, stop=True, skip_group_check=True)
                        nc.tensor.matmul(bk[2], q[1], ksw[:, :], start=True, stop=True).then_inc(n_scored[l], 1)
                    n_unit(unit, pe, gi, hj, streams, 2 - hj, 2 + hj)
                    for l in LANES:
                        bk, sc_ = n_banks[l], n_sc[l]
                        pe.wait_ge(n_soft[l], 6 * i + 6)
                        for n, o1 in enumerate((0, P, S, S + P, 2 * S, 2 * S + P)):
                            nc.tensor.transpose(bk[n // 4][:, (n % 4) * P:(n % 4 + 1) * P], sc_[:, o1:o1 + P], ident[:, :])
                        nc.tensor.transpose(bk[1][0:NC_, 2 * P:3 * P], sc_[:, C0:C0 + NC_], ident[:, :])
                        nc.tensor.transpose(bk[1][0:NC_, 3 * P:4 * P], sc_[:, C1:C1 + NC_], ident[:, :]).then_inc(n_back[l], 1)
                    for l in LANES:
                        bk, w = n_banks[l], n_w[l]
                        pe.wait_ge(n_pt[l], 3 * i + 3)
                        vs = [p2[:, t, bass.ds(gi * P + VS, P)] for t in range(T)]
                        vw = [p2[:, t, bass.ds(gi * P + VW, P)] for t in range(T)]
                        vc = vcc[:, bass.ds(gi * P, P)]
                        p_ = [w[:, n * P:(n + 1) * P] for n in range(6)] + [w[0:NC_, n * P:(n + 1) * P] for n in (6, 7)]
                        for dst, terms in ((bk[2][:, 0:P], ((0, vs[0]), (1, vw[0]), (6, vc))),
                                           (bk[2][:, P:S], ((2, vs[0]), (3, vs[1]), (4, vw[0]), (5, vw[1]), (7, vc)))):
                            for n, (pn, v) in enumerate(terms):
                                ins = nc.tensor.matmul(dst, p_[pn], v, start=(n == 0), stop=(n == len(terms) - 1))
                        ins.then_inc(n_out[l], 1)

            n_groups(pe, group)

        def act_n(act):
            for l in LANES:
                act.sem_inc(n_kept[l], 1)

            def group(gi, streams):
                for hj in range(HPG // 2):
                    i = gi * 2 + hj
                    if hj == 0:
                        act.wait_ge(ng_turned, gi + 2)
                        nc.scalar.activation(ksw[:, :], n_banks[0][2], ACT.Copy).then_inc(ng_copied, 1)
                    for l in LANES:
                        act.wait_ge(n_turned[l], i + 2)
                        nc.scalar.activation(n_qt[l][:, :], n_banks[l][0][:, 0:S], ACT.Copy, scale=P ** -0.5)\
                          .then_inc(n_copied[l], 1)
                    n_split(act_unit, act, gi, hj, streams, 0)
                    for l in LANES:
                        sc_ = n_sc[l]
                        act.wait_ge(n_max[l], i + 1)
                        for o1, w, n in SEG:
                            nc.scalar.activation(sc_[:, o1:o1 + w], sc_[:, o1:o1 + w], ACT.Exp, bias=nmx_l[l][:, n:n + 1],
                                                 accum_out=sm_l[l][:, n:n + 1]).then_inc(n_exp[l], 1)
                    n_split(act_unit, act, gi, hj, streams, 1, 3)
                    for l in LANES:
                        bk, w = n_banks[l], n_w[l]
                        act.wait_ge(n_back[l], i + 1)
                        nc.scalar.activation(w[:, 0:512], bk[0], ACT.Copy).then_inc(n_pt[l], 1)
                        nc.scalar.activation(w[:, 512:768], bk[1][:, 0:S], ACT.Copy).then_inc(n_pt[l], 1)
                        nc.scalar.activation(w[0:NC_, 768:1024], bk[1][0:NC_, S:2 * S], ACT.Copy).then_inc(n_pt[l], 1)
                    if hj == 1 and streams:
                        act.wait_ge(unit_used, used(nr, gi))
                        for t in range(T):
                            ins = nc.scalar.activation(p2[:, t, bass.ds(gi * NB + NB, NB)], g[:, t, :], ACT.Copy,
                                                       scale=rstd("n2")[:, t:t + 1])
                        ins.then_inc(pair_free[0], 1)
                    for l in LANES:
                        act.wait_ge(n_out[l], i + 1)
                        nc.scalar.activation(p2[:, :, bass.ds((2 * i + l) * P, P)],
                                             n_banks[l][2][:, 0:S].rearrange("p (t d) -> p t d", t=T), ACT.Copy)\
                          .then_inc(n_kept[l], 1)

            n_groups(act, group)

        def dve_n(dve):
            dve.wait_ge(bias_in, 32)
            steps = count["d"]
            n_steps = 4 * 2

            def link(i, k, ins):
                ins.then_inc(chain_d, 1)
                dve.wait_ge(chain_d, steps + i * n_steps + k + 1)

            def group(gi, streams):
                for hj in range(HPG // 2):
                    i = gi * 2 + hj
                    n_split(dve_unit, dve, gi, hj, streams, 0)
                    for l in LANES:
                        bk, sc_ = n_banks[l], n_sc[l]
                        dve.wait_ge(n_scored[l], i + 1)
                        bias = b_n[:, bass.ds(2 * i + l, 1), :]
                        s0 = sc_[:, 0:S].rearrange("p (i n) -> p i n", i=2)
                        s1 = sc_[:, S:3 * S].rearrange("p (i n) -> p i n", i=2)
                        sc = sc_[:, C0:C0 + 32].rearrange("p (t n) -> p t n", t=2)[:, :, 0:NC_]
                        nc.vector.tensor_tensor(s0, bk[1][:, 0:S].rearrange("p (i n) -> p i n", i=2),
                                                bias[:, :, P:S].broadcast_to([P, 2, P]), ALU.add)
                        nc.vector.tensor_tensor(sc, bk[1][:, S:S + 32].rearrange("p (t n) -> p t n", t=2)[:, :, 0:NC_],
                                                bc[:, :, :, bass.ds(2 * i + l, 1)].rearrange("p t c o -> p t (c o)"), ALU.add)
                        link(i, 2 * l, nc.vector.tensor_tensor(s1, bk[2].rearrange("p (i n) -> p i n", i=2),
                                                               bias.broadcast_to([P, 2, S]), ALU.add))
                        mx = nmx_l[l][:, 0:6].rearrange("p (t b) -> p t b", b=3)
                        nc.vector.tensor_reduce(mx[:, :, 0], sc, X, ALU.max, negate=True)
                        nc.vector.tensor_reduce(mx[:, 0, 1:3], s0, X, ALU.max, negate=True)
                        link(i, 2 * l + 1, nc.vector.tensor_reduce(mx[:, 1, 1:3], s1, X, ALU.max, negate=True))
                        nc.vector.tensor_scalar(nmx_l[l][:, 0:6], nmx_l[l][:, 0:6], 1e29, None, ALU.min).then_inc(n_max[l], 1)
                    for l in LANES:
                        sc_, rc_ = n_sc[l], rc_l[l]
                        dve.wait_ge(n_exp[l], 6 * i + 6)
                        link(i, 4 + 2 * l, nc.vector.tensor_scalar(rc_[:, 0:6], sm_l[l][:, 0:6], 1e-30, None, ALU.max))
                        link(i, 5 + 2 * l, nc.vector.reciprocal(rc_[:, 0:6], rc_[:, 0:6]))
                        gv = gate[:, :, :].rearrange("p t (b h) -> p t b h", b=3)[:, :, :, bass.ds(2 * i + l, 1)]
                        nc.vector.tensor_tensor(rc_[:, 0:6].rearrange("p (t b) -> p t b", b=3),
                                                rc_[:, 0:6].rearrange("p (t b) -> p t b", b=3),
                                                gv.rearrange("p t b o -> p t (b o)"), ALU.mult).then_inc(n_gated[l], 1)
                        dve.wait_ge(n_gated[l], i + 1)
                        for o1, w, n in SEG:
                            nc.vector.tensor_scalar(sc_[:, o1:o1 + w], sc_[:, o1:o1 + w], rc_[:, n:n + 1], None, ALU.mult)\
                              .then_inc(n_soft[l], 1)
                    n_split(dve_unit, dve, gi, hj, streams, 1, 3)

            n_groups(dve, group)
            count["d"] += N_H // 2 * n_steps

        def bcast(ap1, n):
            return bass.AP(tensor=ap1.tensor, offset=ap1.offset, ap=[[0, P], [1, n]])

        block = ctx.enter_context(nc.Block())

        @block.sync
        def _(sp):
            sp.dma_start(oh_r[:, :], a["c_rising"]).then_inc(tables_in, 16)
            sp.dma_start(tab[0:32, 0:8], a["rel_bias"]).then_inc(tables_in, 16)
            sp.dma_start(tab[0:32, 8:24], a["rel_bias_2"]).then_inc(tables_in, 16)
            sp.dma_start(oh_f[:, :], a["c_falling"]).then_inc(tables_in, 16)
            sp.dma_start(ident[:, :], a["c_ident"]).then_inc(ident_in, 16)
            sp.dma_start(x[:, :, 0:NB], a["x"].rearrange("(t p) d -> p t d", p=P)[:, :, 0:NB]).then_inc(x_in[0], 16)
            for n, k in enumerate(("mix_pre_g", "mem_norm_g", "cross_pre_g", "ffn_pre_g", "mix_norm_g_2", "ffn_norm_g_2")):
                sp.dma_start(g_rows[16 * n:16 * n + 16, :], a[k].rearrange("(k p) -> k p", p=P)).then_inc(gains_in, 16)
            for n in range(1, 4):
                sp.dma_start(x[:, :, n * NB:(n + 1) * NB], a["x"].rearrange("(t p) d -> p t d", p=P)[:, :, n * NB:(n + 1) * NB])\
                  .then_inc(x_in[n], 16)
            sp_gemm(sp, "in1f", lambda c: c * NB + F_HG)
            sp_gemm(sp, "in1g", lambda c: c * NB + G_HG)
            sp_gemm(sp, "in1q", lambda c: c * NB + Q_HG)
            sp_gemm(sp, "in1b")
            sp_gemm(sp, "ckv")
            sp_half(sp)
            sp_gemm(sp, "out1")
            sp_gemm(sp, "cq")
            sp_gemm(sp, "co")
            sp_gemm_cols(sp, "ff1")
            sp_gemm(sp, "fo1")
            sp_gemm(sp, "in2c", lambda c: c * NB + KC)
            sp_gemm(sp, "in2k", lambda c: c * NB + KS)
            sp_cmp(sp)
            sp_gemm(sp, "in2q")
            sp_queries(sp)
            sp_gemm(sp, "out2")
            sp_gemm_cols(sp, "ff2")
            sp_gemm(sp, "fo2")
            for t in range(T):
                sp.wait_ge(fin_done, t + 1)
                sp.dma_start(out.rearrange("(t p) d -> p t d", p=P)[:, t, :], x[:, t, :]).then_inc(out_done, 16)
            sp.wait_ge(out_done, 32)

        @block.gpsimd
        def _(pool):
            pool.dma_start(cums[:, :], a["c_cums"]).then_inc(consts_in, 16)
            pool.dma_start(sub_g[:, :], bcast(a["da_subln_g"], P)).then_inc(consts_in, 16)
            pool.dma_start(on_g[:, :], bcast(a["hg_onorm_g"], P)).then_inc(consts_in, 16)
            for n, k in enumerate(("lambda_q1", "lambda_k1", "lambda_q2", "lambda_k2")):
                pool.dma_start(lam4[:, n, :], bcast(a[k], DA_D)).then_inc(consts_in, 16)
            pool.wait_ge(x_in[3], 16)
            pool.dma_start(masks[:, :], a["c_masks"]).then_inc(masks_in, 16)
            pool.dma_start(memx[:, :, :], a["mem"].rearrange("(t p) d -> p t d", p=P)).then_inc(mem_in, 16)
            pool.wait_ge(bt_sb, 1)
            rows = bt[:, :]
            skewed = bass.AP(tensor=rows.tensor, offset=rows.offset + P - 1, ap=[list(rows.ap[0]), [-1, P], [1, S]])
            pool.dma_start(dram_bias, skewed).then_inc(bt_stored, 16)
            pool_hg(pool)
            pool.wait_ge(bt_stored, 16)
            pool.wait_ge(lo_evac, BANKS["nmem"] + 8)
            pool.dma_start(b_da[:, :, :], dram_bias[0:DA_H].rearrange("h p k -> p h k")).then_inc(bias_in, 16)
            pool.dma_start(g_b[:, :], bcast(a["mix_post_g"], D)).then_inc(gb_in, 16)
            pool_da(pool)
            pool.wait_ge(y_scaled, 4)
            pool.dma_start(g_b[:, :], bcast(a["cross_post_g"], D)).then_inc(gb_in, 16)
            pool_cx(pool)
            pool.wait_ge(pair_free[1], gemms["co"]["pair0"][1] + 3)
            pool.dma_start(g_b[:, :], bcast(a["ffn_post_g"], D)).then_inc(gb_in, 16)
            pool.wait_ge(lo_evac, BANKS["n2"] + 8)
            for n, k in enumerate(("cmp_pos_k_2", "cmp_pos_v_2")):
                pool.dma_start(pos_s[:, n, :], a[k]).then_inc(cmp_in, 16)
            for n, k in enumerate(("cmp_w2_k_2", "cmp_w2_v_2")):
                pool.dma_start(w2[:, n, :, :], a[k].rearrange("(k p) d -> p k d", p=P)).then_inc(cmp_in, 16)
            pool.wait_ge(unit_used, SLOTS + cp["u0"] + 12)
            pool.dma_start(b_n[:, :, :], dram_bias[DA_H:DA_H + N_H].rearrange("h p k -> p h k")).then_inc(bias_in, 16)
            pool_n(pool)
            pool.wait_ge(lo_evac, BANKS["ff2"] + 2 * PAIRS)
            pool.dma_start(g_a[:, :], bcast(a["final_norm_g_2"], D)).then_inc(ga_in, 16)

        @block.tensor
        def _(pe):
            pe.sem_inc(unit_used, SLOTS)
            pe.wait_ge(tables_in, 16 * 4)
            pe.wait_ge(tab_ready, 1)
            nc.tensor.matmul(g[0:24, 0, :], tab[:, :], oh_f[:, :], start=True, stop=True).then_inc(bt_ready, 1)
            for t in range(T):
                for c in range(NC_):
                    o0 = P * t - CSTR * c - (CLEN - 1) + 256
                    ins = nc.tensor.matmul(g[:, 1, (t * NC_ + c) * N_H:(t * NC_ + c + 1) * N_H], oh_r[:, o0:o0 + P], tab[:, 8:24],
                                           start=(t == 0 and c == 0), stop=(t == 1 and c == NC_ - 1), skip_group_check=True)
            ins.then_inc(bt_ready, 1)
            pe.wait_ge(ident_in, 16)
            pe.wait_ge(gains_in, 16 * 6)
            nc.tensor.transpose(g[:, 2, 0:6 * 16], g_rows[:, :], ident[0:6 * 16, 0:6 * 16]).then_inc(gains_turned, 1)
            pe.wait_ge(gains_ready, 1)
            pe.wait_ge(bt_sb, 1)
            pe.wait_ge(bc_sb, 1)
            pe_gemm(pe, "in1f", turn="n1")
            pe_gemm(pe, "in1g")
            pe_gemm(pe, "in1q")
            pe_hg(pe)
            for b in range(4, 8):
                pe_turn_bank(pe, "mixh", b)
            turned_in(pe, "mixh", 8)
            pe_da(pe)
            pe_gemm(pe, "out1", turn="mix1")
            pe_gemm(pe, "cq", turn="ncx")
            pe_cx(pe)
            pe_gemm(pe, "co", turn="cx")
            pe_ffn_in(pe, "ff1", "nff")
            turned_in(pe, "ff1", 2 * PAIRS)
            pe_gemm(pe, "fo1", ht_hi, ht_lo)
            pe_gemm(pe, "in2c", turn="n2")
            pe_gemm(pe, "in2k", also=pe_blocks(pe))
            pe_cmp(pe)
            pe_gemm(pe, "in2q", also=pe_hidden(pe))
            pe_n(pe)
            pe_gemm(pe, "out2", turn="mix2")
            pe_ffn_in(pe, "ff2", "nff2")
            turned_in(pe, "ff2", 2 * PAIRS)
            pe_gemm(pe, "fo2", ht_hi, ht_lo)

        def cols(dst):
            return lambda c: dst[:, :, bass.ds(c * NB, NB)]

        @block.scalar
        def _(act):
            act.sem_inc(pair_free[0], 1)
            act.sem_inc(pair_free[1], 1)
            act.wait_ge(bt_ready, 2)
            nc.scalar.activation(bt[:, :], g[0:24, 0, :], ACT.Copy).then_inc(bt_sb, 1)
            for n in range(4):
                act.wait_ge(x_in[n], 16)
            with_g, with_q = act_gates(act)
            f_out = act_copy_out(act, "in1f", lambda c: p1[:, :, bass.ds(c * NB + F_HG, NB)], "n1")
            g_out = act_copy_out(act, "in1g", lambda c: p1[:, :, bass.ds(c * NB + G_HG, NB)], "n1")
            act_gemm(act, "in1f", f_out, "n1", hold=True)
            act_gemm(act, "in1g", g_out, held=lambda: f_out(1, -1), hold=True, also=with_g)
            act_gemm(act, "in1q", act_copy_out(act, "in1q", lambda c: p1[:, :, bass.ds(c * NB + Q_HG, NB)], "n1"),
                     held=lambda: g_out(1, -1), also=with_q, then="in1b")
            act.wait_ge(bt_stored, 16)
            act_unit(act, gemms["in1b"]["u0"] // SLOTS, AHEAD)
            act_hg(act)
            act_mix_norm(act, 1)
            for b in range(4, 8):
                act_turn_bank(act, "mixh", b)
            act_da(act)
            act_mix_norm(act, 0)
            act_gemm(act, "out1", act_squares_y(act, "out1", y_r, junk_r), "mix1", done=SLOTS, then="cq")
            act_sqrt(act, "post1", ss_y)
            act_gemm(act, "cq", act_copy_out(act, "cq", cols(qx), "ncx"), "ncx", done=AHEAD, then="co")
            act_unit(act, gemms["co"]["u0"] // SLOTS, AHEAD)
            act_cx(act)
            act_gemm(act, "co", act_squares_out(act, "co", "postcx", junk_r), "cx", done=SLOTS, then="ff1")
            act_sqrt(act, "postcx", ss_y)
            act_ffn_in(act, "ff1", "nff", "fo1")
            act_gemm(act, "fo1", act_squares_out(act, "fo1", "postff", junk_a), done=AHEAD, then="in2c")
            act_sqrt(act, "postff", ss_y)
            c_out = act_copy_out(act, "in2c", lambda c: p2[:, :, bass.ds(c * NB + KC, NB)], "n2")
            k_out = act_copy_out(act, "in2k", lambda c: p2[:, :, bass.ds(c * NB + KS, NB)], "n2")
            act_gemm(act, "in2c", c_out, "n2", hold=True, done=AHEAD)
            act_gemm(act, "in2k", k_out, held=lambda: c_out(1, -1), hold=True, also=act_blocks(act))
            act_cmp(act, lambda: k_out(2, -1))
            act_gemm(act, "in2q", act_copy_out(act, "in2q", cols(p2), "n2"), also=act_hidden(act), then="in2r")
            act_compressed(act)
            act_n(act)
            act_gemm(act, "out2", lambda i, c: None, "mix2", done=AHEAD, then="ff2")
            act_ffn_in(act, "ff2", "nff2", "fo2")
            act_gemm(act, "fo2", act_squares_x(act, "fo2", junk_a), done=AHEAD)
            act_sqrt(act, "nfin", ss_y)

        @block.vector
        def _(dve):
            dve.sem_inc(lo_done, SLOTS)
            nc.vector.memset(tab[32:33, :], MASKED).then_inc(tab_ready, 1)
            dve.wait_ge(bt_ready, 2)
            nc.vector.tensor_copy(bc[:, :, :, :].rearrange("p t c h -> p (t c h)"), g[:, 1, 0:T * NC_ * N_H]).then_inc(bc_sb, 1)
            dve.wait_ge(gains_turned, 1)
            nc.vector.tensor_copy(g_cols[:, :], g[:, 2, 0:6 * 16]).then_inc(gains_ready, 1)
            dve.wait_ge(gains_ready, 1)
            with_g, with_q = dve_gates(dve)
            dve_gemm(dve, "in1f", turn="n1")
            dve_gemm(dve, "in1g", also=with_g)
            dve_gemm(dve, "in1q", also=with_q)
            ahead(dve_unit, dve, "in1b", SLOTS)
            dve_hg(dve)
            dve_mix_norm(dve, 1)
            for b in range(4, 8):
                dve_turn_bank(dve, "mixh", b)
            dve_da(dve)
            dve_mix_norm(dve, 0)
            dve_gemm(dve, "out1", dve_halves_out(dve, "out1", "post1", y_r, 1), "mix1", done=SLOTS,
                     then="cq")
            dve_gemm(dve, "cq", turn="ncx", done=AHEAD)
            ahead(dve_unit, dve, "co", SLOTS)
            dve_cx(dve)
            dve_gemm(dve, "co", dve_scale_out(dve, "co", "postcx", y_r, 2), "cx", done=SLOTS, then="ff1")
            dve_ffn_in(dve, "ff1", "nff", "fo1")
            dve_gemm(dve, "fo1", dve_scale_out(dve, "fo1", "postff", y_a, 3), done=AHEAD, then="in2c")
            dve_gemm(dve, "in2c", turn="n2", done=AHEAD)
            dve_gemm(dve, "in2k", also=dve_blocks(dve))
            dve_cmp(dve)
            dve_gemm(dve, "in2q", also=dve_hidden(dve))
            ahead(dve_unit, dve, "in2r")
            dve_n(dve)
            dve_gemm(dve, "out2", dve_add_out(dve, "out2"), "mix2", done=AHEAD, then="ff2")
            dve_ffn_in(dve, "ff2", "nff2", "fo2")
            dve_gemm(dve, "fo2", dve_add_out(dve, "fo2"), done=AHEAD)
            dve.wait_ge(ss_done, SS["nfin"] + 8)
            link_d(dve, nc.vector.tensor_reduce(ss_y, ss8, X, ALU.add))
            nc.vector.tensor_scalar(ss_y, ss_y, 1.0 / D, EPS, ALU.mult, ALU.add).then_inc(var_done, 1)
            dve_rstd(dve, "nfin")
            dve.wait_ge(ga_in, 16)
            for t in range(T):
                nc.vector.scalar_tensor_tensor(out=x[:, t, :], in0=x[:, t, :], scalar=rstd("nfin")[:, t:t + 1],
                                               in1=g_a[:, :], op0=ALU.mult, op1=ALU.mult).then_inc(fin_done, 1)


_INS = ["x", "mem", "w_in", "w_out", "w_cq", "w_ckv", "w_co", "w_ffn_in", "w_ffn_out", "mix_pre_g", "mix_post_g",
        "cross_pre_g", "cross_post_g", "mem_norm_g", "ffn_pre_g", "ffn_post_g", "da_subln_g", "hg_onorm_g",
        "lambda_q1", "lambda_k1", "lambda_q2", "lambda_k2", "rel_bias", "rel_bias_2", "mix_norm_g_2", "ffn_norm_g_2",
        "final_norm_g_2", "nsa_w_in_2", "nsa_w_out_2", "cmp_pos_k_2", "cmp_w1_k_2", "cmp_w2_k_2", "cmp_pos_v_2",
        "cmp_w1_v_2", "cmp_w2_v_2", "ffn_w_in_2", "ffn_w_out_2"]
_WHOLE = ("rel_bias", "rel_bias_2", "final_norm_g_2")


def kernel(**inputs):
    import numpy as _np
    import concourse.bacc as _bacc
    from concourse import mybir as _mybir
    from concourse.bass_utils import run_bass_kernel_spmd as _run

    nc = _bacc.Bacc("TRN2", target_bir_lowering=False, num_devices=1)
    arrays, aps = {}, {}
    for name in _INS:
        v = _np.ascontiguousarray(inputs[name])
        arrays[f"in_{name}"] = v if name in _WHOLE else v.reshape(v.shape[1:])
    falling, rising = rel_rows()
    for name, v in (("c_ident", _np.eye(128, dtype=_np.float32)), ("c_cums", cumsum_lhs()), ("c_masks", level_masks()),
                    ("c_falling", falling), ("c_rising", rising)):
        arrays[f"in_{name}"] = v
    for key, v in arrays.items():
        aps[key[3:]] = nc.dram_tensor(key, v.shape, _mybir.dt.float32, kind="ExternalInput").ap()
    out = nc.dram_tensor("out_x", (256, 2048), _mybir.dt.float32, kind="ExternalOutput").ap()
    build(nc, aps, out)
    r = _run(nc, [arrays], core_ids=[0])
    return r.results[0]["out_x"].reshape(1, 256, 2048)
```
